# Optimizing a Trainium2 kernel written in Bass

```python
import math
import jax
import jax.numpy as jnp
from jax import lax
import numpy as np
import jax, jax.numpy as jnp

D_MODEL = 1024
BATCH = 1
SEQ = 512
DEPTH = 2

CHUNK = 64
EPS = 1e-6
D_FF = 2816

SSD_HEADS = 8
SSD_HEAD_DIM = 64
SSD_INNER = SSD_HEADS * SSD_HEAD_DIM
SSD_GROUPS = 2
SSD_STATE = 128
SSD_CONV = 4
SSD_XBC = SSD_INNER + 2 * SSD_GROUPS * SSD_STATE
SSD_HPG = SSD_HEADS // SSD_GROUPS

S5_WIDTH = 512
S5_GROUP = 16
S5_GROUPS = S5_WIDTH // S5_GROUP
S5_STATE = 64

ATT_HEADS = 8
ATT_HEAD_DIM = 64
ATT_WIDTH = ATT_HEADS * ATT_HEAD_DIM
LEFT_CHUNKS = 8
BAND_CHUNKS = LEFT_CHUNKS + 1
BAND = BAND_CHUNKS * CHUNK
MAX_REL = 128

POOL_WINDOWS = (2, 4, 8, 16)
POOL_GROUPS = len(POOL_WINDOWS)
POOL_WIDTH = 512
POOL_GROUP = POOL_WIDTH // POOL_GROUPS
POOL_MAX = max(POOL_WINDOWS)

EVEN_IN = SSD_INNER + SSD_XBC + SSD_HEADS + S5_WIDTH
EVEN_OUT = SSD_INNER + S5_WIDTH
ODD_IN = 3 * ATT_WIDTH + POOL_WIDTH
ODD_OUT = ATT_WIDTH + POOL_WIDTH
N_EVEN = (DEPTH + 1) // 2
N_ODD = DEPTH // 2


def _rmsnorm(x, gain):
    xf = x.astype(jnp.float32)
    y = xf * lax.rsqrt(jnp.mean(xf * xf, axis=-1, keepdims=True) + EPS)
    return (y * gain.astype(jnp.float32)).astype(x.dtype)

def _swiglu(h, w_gate, w_up, w_down):
    return (jax.nn.silu(h @ w_gate) * (h @ w_up)) @ w_down

def _causal_depthwise_conv(x, w, b):
    c = x.shape[-1]
    y = lax.conv_general_dilated(
        x.astype(jnp.float32), w.astype(jnp.float32)[:, None, :],
        window_strides=(1,), padding=[(SSD_CONV - 1, 0)],
        dimension_numbers=('NWC', 'WIO', 'NWC'), feature_group_count=c)
    return y + b.astype(jnp.float32)

def _ssd_mixer(zxbcdt, conv_w, conv_b, dt_bias, a_log, d_skip, norm_gain):
    f32 = jnp.float32
    bsz, s, _ = zxbcdt.shape
    nc = s // CHUNK
    z, xbc, dt = jnp.split(zxbcdt, [SSD_INNER, SSD_INNER + SSD_XBC], axis=-1)
    xbc = jax.nn.silu(_causal_depthwise_conv(xbc, conv_w, conv_b))
    xs, bm, cm = jnp.split(xbc, [SSD_INNER, SSD_INNER + SSD_GROUPS * SSD_STATE], axis=-1)
    xs = xs.reshape(bsz, nc, CHUNK, SSD_GROUPS, SSD_HPG, SSD_HEAD_DIM)
    bm = bm.reshape(bsz, nc, CHUNK, SSD_GROUPS, SSD_STATE)
    cm = cm.reshape(bsz, nc, CHUNK, SSD_GROUPS, SSD_STATE)
    dt = jax.nn.softplus(dt.astype(f32) + dt_bias.astype(f32))
    dt = dt.reshape(bsz, nc, CHUNK, SSD_GROUPS, SSD_HPG)
    a = -jnp.exp(a_log.astype(f32)).reshape(SSD_GROUPS, SSD_HPG)
    a_cs = jnp.cumsum(dt * a, axis=2)
    xdt = xs * dt[..., None]
    causal = jnp.tril(jnp.ones((CHUNK, CHUNK), dtype=bool))[:, :, None, None]
    seg = a_cs[:, :, :, None] - a_cs[:, :, None, :]
    decay = jnp.exp(jnp.where(causal, seg, -jnp.inf))
    cb = jnp.einsum('bclgn,bcsgn->bclsg', cm, bm)
    y_diag = jnp.einsum('bclsg,bclsgj,bcsgjp->bclgjp', cb, decay, xdt)
    to_end = jnp.exp(a_cs[:, :, -1:] - a_cs)
    states = jnp.einsum('bclgn,bclgj,bclgjp->bcgjpn', bm, to_end, xdt)
    chunk_decay = jnp.exp(a_cs[:, :, -1])

    def step(h, inp):
        st, dec = inp
        return dec[..., None, None] * h + st, h

    h0 = jnp.zeros((bsz, SSD_GROUPS, SSD_HPG, SSD_HEAD_DIM, SSD_STATE), f32)
    _, h_prev = lax.scan(step, h0, (jnp.moveaxis(states, 1, 0), jnp.moveaxis(chunk_decay, 1, 0)))
    h_prev = jnp.moveaxis(h_prev, 0, 1)
    y_off = jnp.einsum('bclgn,bcgjpn,bclgj->bclgjp', cm, h_prev, jnp.exp(a_cs))
    y = y_diag + y_off + d_skip.astype(f32).reshape(SSD_GROUPS, SSD_HPG, 1) * xs
    y = y.reshape(bsz, s, SSD_INNER) * jax.nn.silu(z.astype(f32))
    yg = y.reshape(bsz, s, SSD_GROUPS, SSD_INNER // SSD_GROUPS)
    yg = yg * lax.rsqrt(jnp.mean(yg * yg, axis=-1, keepdims=True) + EPS)
    return (yg.reshape(bsz, s, SSD_INNER) * norm_gain.astype(f32)).astype(zxbcdt.dtype)

def _complex_affine_combine(e1, e2):
    a1r, a1i, x1r, x1i = e1
    a2r, a2i, x2r, x2i = e2
    return (a2r * a1r - a2i * a1i,
            a2r * a1i + a2i * a1r,
            a2r * x1r - a2i * x1i + x2r,
            a2r * x1i + a2i * x1r + x2i)

def _s5_mixer(u, a_re, a_im, log_dt, b_re, b_im, c_re, c_im, d_skip, w_glu, b_glu):
    f32 = jnp.float32
    bsz, s, _ = u.shape
    uf = u.astype(f32).reshape(bsz, s, S5_GROUPS, S5_GROUP)
    ar = a_re.astype(f32)
    ai = a_im.astype(f32)
    dt = jnp.exp(log_dt.astype(f32))[:, None]
    mag = jnp.exp(dt * ar)
    abar_re = mag * jnp.cos(dt * ai)
    abar_im = mag * jnp.sin(dt * ai)
    den = ar * ar + ai * ai
    f_re = ((abar_re - 1.0) * ar + abar_im * ai) / den
    f_im = (abar_im * ar - (abar_re - 1.0) * ai) / den
    br = b_re.astype(f32)
    bi = b_im.astype(f32)
    bb_re = f_re[..., None] * br - f_im[..., None] * bi
    bb_im = f_re[..., None] * bi + f_im[..., None] * br
    drive_re = jnp.einsum('bsgi,gpi->sbgp', uf, bb_re)
    drive_im = jnp.einsum('bsgi,gpi->sbgp', uf, bb_im)
    shape_a = (s, 1, S5_GROUPS, S5_STATE)
    dec_re = jnp.broadcast_to(abar_re, shape_a)
    dec_im = jnp.broadcast_to(abar_im, shape_a)
    _, _, h_re, h_im = lax.associative_scan(
        _complex_affine_combine, (dec_re, dec_im, drive_re, drive_im), axis=0)
    y = (jnp.einsum('gip,sbgp->bsgi', c_re.astype(f32), h_re)
         - jnp.einsum('gip,sbgp->bsgi', c_im.astype(f32), h_im)
         + d_skip.astype(f32) * uf)
    y = y.reshape(bsz, s, S5_WIDTH)
    gate = jax.nn.gelu(y) @ w_glu.astype(f32) + b_glu.astype(f32)
    return (y * jax.nn.sigmoid(gate)).astype(u.dtype)

def _chunk_band_attention(q, k, v, q_gain, k_gain, rel_bias):
    f32 = jnp.float32
    bsz, s, _ = q.shape
    nc = s // CHUNK
    q = _rmsnorm(q.reshape(bsz, nc, CHUNK, ATT_HEADS, ATT_HEAD_DIM), q_gain)
    k = _rmsnorm(k.reshape(bsz, s, ATT_HEADS, ATT_HEAD_DIM), k_gain)
    v = v.reshape(bsz, s, ATT_HEADS, ATT_HEAD_DIM)
    front = ((0, 0), (LEFT_CHUNKS * CHUNK, 0), (0, 0), (0, 0))
    kp = jnp.pad(k, front).reshape(bsz, nc + LEFT_CHUNKS, CHUNK, ATT_HEADS, ATT_HEAD_DIM)
    vp = jnp.pad(v, front).reshape(bsz, nc + LEFT_CHUNKS, CHUNK, ATT_HEADS, ATT_HEAD_DIM)
    band_idx = jnp.arange(nc)[:, None] + jnp.arange(BAND_CHUNKS)[None, :]
    kb = kp[:, band_idx].reshape(bsz, nc, BAND, ATT_HEADS, ATT_HEAD_DIM)
    vb = vp[:, band_idx].reshape(bsz, nc, BAND, ATT_HEADS, ATT_HEAD_DIM)
    scores = jnp.einsum('bclhd,bckhd->bhclk', q.astype(f32), kb.astype(f32)) * (ATT_HEAD_DIM ** -0.5)
    q_off = LEFT_CHUNKS * CHUNK + jnp.arange(CHUNK)
    dist = q_off[:, None] - jnp.arange(BAND)[None, :]
    bias = rel_bias.astype(f32)[:, jnp.clip(dist, -MAX_REL, MAX_REL) + MAX_REL]
    valid = jnp.repeat(band_idx >= LEFT_CHUNKS, CHUNK, axis=1)
    scores = jnp.where(valid[None, None, :, None, :], scores + bias[None, :, None], -jnp.inf)
    probs = jax.nn.softmax(scores, axis=-1)
    out = jnp.einsum('bhclk,bckhd->bclhd', probs, vb.astype(f32))
    return out.reshape(bsz, s, ATT_WIDTH).astype(q.dtype)

def _multiscale_pool(u, w_pool, scale):
    f32 = jnp.float32
    bsz, s, _ = u.shape
    uf = u.astype(f32).reshape(bsz, s, POOL_GROUPS, POOL_GROUP)
    csum = jnp.pad(jnp.cumsum(uf, axis=1), ((0, 0), (POOL_MAX, 0), (0, 0), (0, 0)))
    pos = jnp.arange(s)
    means = []
    for g, w in enumerate(POOL_WINDOWS):
        win = csum[:, POOL_MAX:, g] - csum[:, POOL_MAX - w:POOL_MAX - w + s, g]
        count = jnp.minimum(pos + 1, w).astype(f32)[None, :, None]
        means.append(win / count)
    pooled = jnp.stack(means, axis=2) - uf
    y = jnp.einsum('bsgi,gio->bsgo', pooled, w_pool.astype(f32)).reshape(bsz, s, POOL_WIDTH)
    return (y * scale.astype(f32)).astype(u.dtype)

def first_inputs(seed: int = 0) -> dict:
    key = jax.random.key(seed)
    keys = iter(jax.random.split(key, 48))
    f32 = jnp.float32

    def normal(shape, scale):
        return scale * jax.random.normal(next(keys), shape, f32)

    def gain(shape):
        return 1.0 + 0.05 * jax.random.normal(next(keys), shape, f32)

    def log_uniform(shape, lo, hi):
        return jax.random.uniform(next(keys), shape, f32, math.log(lo), math.log(hi))

    ssd_dt = jnp.exp(log_uniform((N_EVEN, SSD_HEADS), 1e-3, 1e-1))
    ssd_dt_bias = ssd_dt + jnp.log(-jnp.expm1(-ssd_dt))
    ssd_a_log = jnp.log(jax.random.uniform(next(keys), (N_EVEN, SSD_HEADS), f32, 1.0, 16.0))
    s5_shape = (N_EVEN, S5_GROUPS, S5_STATE)
    s5_a_re = -0.5 + normal(s5_shape, 0.01)
    s5_a_im = math.pi * jnp.arange(S5_STATE, dtype=f32) + normal(s5_shape, 0.01)
    s5_log_dt = log_uniform((N_EVEN, S5_GROUPS), 1e-3, 1e-1)
    return {
        'x': normal((BATCH, SEQ, D_MODEL), 1.0),
        'ffn1_norm': gain((DEPTH, D_MODEL)),
        'ffn1_w_gate': normal((DEPTH, D_MODEL, D_FF), D_MODEL ** -0.5),
        'ffn1_w_up': normal((DEPTH, D_MODEL, D_FF), D_MODEL ** -0.5),
        'ffn1_w_down': normal((DEPTH, D_FF, D_MODEL), D_FF ** -0.5),
        'mix_norm': gain((DEPTH, D_MODEL)),
        'even_w_in': normal((N_EVEN, D_MODEL, EVEN_IN), D_MODEL ** -0.5),
        'even_w_out': normal((N_EVEN, EVEN_OUT, D_MODEL), EVEN_OUT ** -0.5),
        'ssd_conv_w': normal((N_EVEN, SSD_CONV, SSD_XBC), SSD_CONV ** -0.5),
        'ssd_conv_b': normal((N_EVEN, SSD_XBC), 0.02),
        'ssd_dt_bias': ssd_dt_bias,
        'ssd_a_log': ssd_a_log,
        'ssd_d': gain((N_EVEN, SSD_HEADS)),
        'ssd_norm': gain((N_EVEN, SSD_INNER)),
        's5_a_re': s5_a_re,
        's5_a_im': s5_a_im,
        's5_log_dt': s5_log_dt,
        's5_b_re': normal((N_EVEN, S5_GROUPS, S5_STATE, S5_GROUP), (2 * S5_GROUP) ** -0.5),
        's5_b_im': normal((N_EVEN, S5_GROUPS, S5_STATE, S5_GROUP), (2 * S5_GROUP) ** -0.5),
        's5_c_re': normal((N_EVEN, S5_GROUPS, S5_GROUP, S5_STATE), S5_STATE ** -0.5),
        's5_c_im': normal((N_EVEN, S5_GROUPS, S5_GROUP, S5_STATE), S5_STATE ** -0.5),
        's5_d': normal((N_EVEN, S5_GROUPS, S5_GROUP), 1.0),
        's5_w_glu': normal((N_EVEN, S5_WIDTH, S5_WIDTH), S5_WIDTH ** -0.5),
        's5_b_glu': normal((N_EVEN, S5_WIDTH), 0.02),
        'odd_w_in': normal((N_ODD, D_MODEL, ODD_IN), D_MODEL ** -0.5),
        'odd_w_out': normal((N_ODD, ODD_OUT, D_MODEL), ODD_OUT ** -0.5),
        'attn_q_norm': gain((N_ODD, ATT_HEAD_DIM)),
        'attn_k_norm': gain((N_ODD, ATT_HEAD_DIM)),
        'attn_rel_bias': normal((N_ODD, ATT_HEADS, 2 * MAX_REL + 1), 0.1),
        'pool_w': normal((N_ODD, POOL_GROUPS, POOL_GROUP, POOL_GROUP), POOL_GROUP ** -0.5),
        'pool_scale': gain((N_ODD, POOL_WIDTH)),
        'ffn2_norm': gain((DEPTH, D_MODEL)),
        'ffn2_w_gate': normal((DEPTH, D_MODEL, D_FF), D_MODEL ** -0.5),
        'ffn2_w_up': normal((DEPTH, D_MODEL, D_FF), D_MODEL ** -0.5),
        'ffn2_w_down': normal((DEPTH, D_FF, D_MODEL), D_FF ** -0.5),
    }

def first_block(x, ffn1_norm, ffn1_w_gate, ffn1_w_up, ffn1_w_down, mix_norm,
              even_w_in, even_w_out, ssd_conv_w, ssd_conv_b, ssd_dt_bias, ssd_a_log, ssd_d, ssd_norm,
              s5_a_re, s5_a_im, s5_log_dt, s5_b_re, s5_b_im, s5_c_re, s5_c_im, s5_d, s5_w_glu, s5_b_glu,
              odd_w_in, odd_w_out, attn_q_norm, attn_k_norm, attn_rel_bias, pool_w, pool_scale,
              ffn2_norm, ffn2_w_gate, ffn2_w_up, ffn2_w_down):
    for layer in range(DEPTH):
        i = layer // 2
        h = _rmsnorm(x, ffn1_norm[layer])
        x = x + 0.5 * _swiglu(h, ffn1_w_gate[layer], ffn1_w_up[layer], ffn1_w_down[layer])
        h = _rmsnorm(x, mix_norm[layer])
        if layer % 2 == 0:
            proj = h @ even_w_in[i]
            zxbcdt, u = jnp.split(proj, [SSD_INNER + SSD_XBC + SSD_HEADS], axis=-1)
            y_a = _ssd_mixer(zxbcdt, ssd_conv_w[i], ssd_conv_b[i], ssd_dt_bias[i],
                             ssd_a_log[i], ssd_d[i], ssd_norm[i])
            y_b = _s5_mixer(u, s5_a_re[i], s5_a_im[i], s5_log_dt[i], s5_b_re[i], s5_b_im[i],
                            s5_c_re[i], s5_c_im[i], s5_d[i], s5_w_glu[i], s5_b_glu[i])
            mixed = jnp.concatenate([y_a, y_b], axis=-1).astype(x.dtype) @ even_w_out[i]
        else:
            proj = h @ odd_w_in[i]
            q, k, v, u = jnp.split(proj, [ATT_WIDTH, 2 * ATT_WIDTH, 3 * ATT_WIDTH], axis=-1)
            y_c = _chunk_band_attention(q, k, v, attn_q_norm[i], attn_k_norm[i], attn_rel_bias[i])
            y_d = _multiscale_pool(u, pool_w[i], pool_scale[i])
            mixed = jnp.concatenate([y_c, y_d], axis=-1).astype(x.dtype) @ odd_w_out[i]
        x = x + mixed.astype(x.dtype)
        h = _rmsnorm(x, ffn2_norm[layer])
        x = x + 0.5 * _swiglu(h, ffn2_w_gate[layer], ffn2_w_up[layer], ffn2_w_down[layer])
    return x


DEPTH_2 = 1

HEAD_DIM = 64
N_HEADS = 8
DILATED_GROUPS = ((128, 1), (512, 4), (2048, 16))
N_GROUPS = len(DILATED_GROUPS)
ATTN_WIDTH = N_HEADS * HEAD_DIM
CONV_CHANNELS = 512
CONV_WIDTH = 31
D_FF_2 = -(-8 * D_MODEL // (3 * 256)) * 256
ROPE_THETA = 10000.0
BLOCK = 128
LN_EPS = 1e-5
QKV_COLS = N_GROUPS * 3 * ATTN_WIDTH
IN_COLS = QKV_COLS + 2 * CONV_CHANNELS + 2 * D_MODEL


def layer_norm(x, g, b):
    xf = x.astype(jnp.float32)
    mu = jnp.mean(xf, axis=-1, keepdims=True)
    var = jnp.mean(jnp.square(xf - mu), axis=-1, keepdims=True)
    y = (xf - mu) * lax.rsqrt(var + LN_EPS)
    return (y * g.astype(jnp.float32) + b.astype(jnp.float32)).astype(x.dtype)

def rotary_tables(seq_len):
    inv_freq = 1.0 / (ROPE_THETA ** (jnp.arange(0, HEAD_DIM, 2, dtype=jnp.float32) / HEAD_DIM))
    ang = jnp.arange(seq_len, dtype=jnp.float32)[:, None] * inv_freq[None, :]
    return jnp.cos(ang)[:, None, :], jnp.sin(ang)[:, None, :]

def apply_rotary(x, cos, sin):
    xf = x.astype(jnp.float32)
    x1, x2 = jnp.split(xf, 2, axis=-1)
    return jnp.concatenate([x1 * cos - x2 * sin, x2 * cos + x1 * sin], axis=-1).astype(x.dtype)

def dilated_window_attention(q, k, v, window, dilation):
    B, S, H, Dh = q.shape
    n_keys = window // dilation
    L = S // dilation
    n_blk = -(-L // BLOCK)
    Lp = n_blk * BLOCK

    def by_residue(a):
        return a.reshape(B, L, dilation, H, Dh).transpose(0, 2, 1, 3, 4)

    qb = jnp.pad(by_residue(q), ((0, 0), (0, 0), (0, Lp - L), (0, 0), (0, 0)))
    qb = qb.reshape(B, dilation, n_blk, BLOCK, H, Dh)
    pad_k = ((0, 0), (0, 0), (BLOCK, Lp - L), (0, 0), (0, 0))
    kp = jnp.pad(by_residue(k), pad_k)
    vp = jnp.pad(by_residue(v), pad_k)

    def band(a):
        prev = a[:, :, :Lp].reshape(B, dilation, n_blk, BLOCK, H, Dh)
        cur = a[:, :, BLOCK:].reshape(B, dilation, n_blk, BLOCK, H, Dh)
        return jnp.concatenate([prev, cur], axis=3)

    kb, vb = band(kp), band(vp)
    s = jnp.einsum('brnqhd,brnkhd->brnhqk', qb, kb,
                   preferred_element_type=jnp.float32) * (Dh ** -0.5)
    iq = jnp.arange(BLOCK)[:, None]
    ik = jnp.arange(2 * BLOCK)[None, :]
    dist = iq + BLOCK - ik
    k_pos = jnp.arange(n_blk)[:, None, None] * BLOCK - BLOCK + ik[None]
    mask = (dist >= 0) & (dist <= n_keys) & (k_pos >= 0)
    s = jnp.where(mask[None, None, :, None], s, -jnp.inf)
    m = jnp.max(s, axis=-1, keepdims=True)
    p = jnp.exp(s - m)
    den = jnp.sum(p, axis=-1, keepdims=True)
    o = jnp.einsum('brnhqk,brnkhd->brnqhd', p, vb.astype(jnp.float32))
    o = o / den.transpose(0, 1, 2, 4, 3, 5)
    lse = (m + jnp.log(den))[..., 0].transpose(0, 1, 2, 4, 3)
    o = o.reshape(B, dilation, Lp, H, Dh)[:, :, :L].transpose(0, 2, 1, 3, 4).reshape(B, S, H, Dh)
    lse = lse.reshape(B, dilation, Lp, H)[:, :, :L].transpose(0, 2, 1, 3).reshape(B, S, H)
    return o, lse

def hybrid_mixer(x, w_in, conv_w, conv_b, conv_ln_g, conv_ln_b, w_attn_out, w_conv_out, w_o):
    B, S, _ = x.shape
    h = x @ w_in
    qkv = h[..., :QKV_COLS].reshape(B, S, N_GROUPS, 3, N_HEADS, HEAD_DIM)
    conv_in = h[..., QKV_COLS:QKV_COLS + 2 * CONV_CHANNELS]
    gates = jax.nn.sigmoid(h[..., QKV_COLS + 2 * CONV_CHANNELS:].astype(jnp.float32)).astype(x.dtype)
    g_attn, g_conv = jnp.split(gates, 2, axis=-1)

    cos, sin = rotary_tables(S)
    outs, lses = [], []
    for g, (window, dilation) in enumerate(DILATED_GROUPS):
        q = apply_rotary(qkv[:, :, g, 0], cos, sin)
        k = apply_rotary(qkv[:, :, g, 1], cos, sin)
        o, lse = dilated_window_attention(q, k, qkv[:, :, g, 2], window, dilation)
        outs.append(o)
        lses.append(lse)
    wts = jax.nn.softmax(jnp.stack(lses, axis=0), axis=0)
    o = jnp.sum(wts[..., None] * jnp.stack(outs, axis=0), axis=0).astype(x.dtype)
    y_attn = o.reshape(B, S, ATTN_WIDTH) @ w_attn_out

    a, b = jnp.split(conv_in, 2, axis=-1)
    u = a * jax.nn.sigmoid(b)
    u = lax.conv_general_dilated(u, conv_w[:, None, :].astype(u.dtype), window_strides=(1,),
                                 padding=[(CONV_WIDTH - 1, 0)],
                                 dimension_numbers=('NWC', 'WIO', 'NWC'),
                                 feature_group_count=CONV_CHANNELS) + conv_b
    u = jax.nn.silu(layer_norm(u, conv_ln_g, conv_ln_b))
    y_conv = u @ w_conv_out

    merged = g_attn * y_attn + g_conv * y_conv
    return merged @ w_o

def swiglu_ffn(x, w_gate, w_up, w_down):
    return (jax.nn.silu(x @ w_gate) * (x @ w_up)) @ w_down

def second_inputs(seed: int = 0) -> dict:
    key = jax.random.key(seed)
    ks = jax.random.split(key, 17)
    f32 = jnp.float32
    beta = (8 * DEPTH_2) ** -0.25
    nrm = lambda k, shape, scale: jax.random.normal(k, shape, f32) * scale
    return {
        "x": jax.random.normal(ks[0], (BATCH, SEQ, D_MODEL), f32),
        "w_in": nrm(ks[1], (DEPTH_2, D_MODEL, IN_COLS), D_MODEL ** -0.5),
        "conv_w": nrm(ks[2], (DEPTH_2, CONV_WIDTH, CONV_CHANNELS), CONV_WIDTH ** -0.5),
        "conv_b": nrm(ks[3], (DEPTH_2, CONV_CHANNELS), 0.02),
        "conv_ln_g": 1.0 + nrm(ks[4], (DEPTH_2, CONV_CHANNELS), 0.05),
        "conv_ln_b": nrm(ks[5], (DEPTH_2, CONV_CHANNELS), 0.02),
        "w_attn_out": nrm(ks[6], (DEPTH_2, ATTN_WIDTH, D_MODEL), ATTN_WIDTH ** -0.5),
        "w_conv_out": nrm(ks[7], (DEPTH_2, CONV_CHANNELS, D_MODEL), CONV_CHANNELS ** -0.5),
        "w_o": nrm(ks[8], (DEPTH_2, D_MODEL, D_MODEL), beta * D_MODEL ** -0.5),
        "ln1_g": 1.0 + nrm(ks[9], (DEPTH_2, D_MODEL), 0.05),
        "ln1_b": nrm(ks[10], (DEPTH_2, D_MODEL), 0.02),
        "w_ffn_gate": nrm(ks[11], (DEPTH_2, D_MODEL, D_FF_2), D_MODEL ** -0.5),
        "w_ffn_up": nrm(ks[12], (DEPTH_2, D_MODEL, D_FF_2), D_MODEL ** -0.5),
        "w_ffn_down": nrm(ks[13], (DEPTH_2, D_FF_2, D_MODEL), beta * D_FF_2 ** -0.5),
        "ln2_g": 1.0 + nrm(ks[14], (DEPTH_2, D_MODEL), 0.05),
        "ln2_b": nrm(ks[15], (DEPTH_2, D_MODEL), 0.02),
    }

def second_block(x, w_in, conv_w, conv_b, conv_ln_g, conv_ln_b, w_attn_out, w_conv_out, w_o,
              ln1_g, ln1_b, w_ffn_gate, w_ffn_up, w_ffn_down, ln2_g, ln2_b):
    alpha = (2 * DEPTH_2) ** 0.25
    for l in range(DEPTH_2):
        mix = hybrid_mixer(x, w_in[l], conv_w[l], conv_b[l], conv_ln_g[l], conv_ln_b[l],
                           w_attn_out[l], w_conv_out[l], w_o[l])
        x = layer_norm(alpha * x + mix, ln1_g[l], ln1_b[l])
        ff = swiglu_ffn(x, w_ffn_gate[l], w_ffn_up[l], w_ffn_down[l])
        x = layer_norm(alpha * x + ff, ln2_g[l], ln2_b[l])
    return x


def setup_inputs(seed=0):
    out = dict(first_inputs(seed))
    for name, value in second_inputs(seed + 1).items():
        if name != "x":
            out[name + "_2"] = value
    return out


def reference(
    x, ffn1_norm, ffn1_w_gate, ffn1_w_up, ffn1_w_down, mix_norm, even_w_in, even_w_out,
    ssd_conv_w, ssd_conv_b, ssd_dt_bias, ssd_a_log, ssd_d, ssd_norm, s5_a_re, s5_a_im,
    s5_log_dt, s5_b_re, s5_b_im, s5_c_re, s5_c_im, s5_d, s5_w_glu, s5_b_glu, odd_w_in,
    odd_w_out, attn_q_norm, attn_k_norm, attn_rel_bias, pool_w, pool_scale, ffn2_norm,
    ffn2_w_gate, ffn2_w_up, ffn2_w_down, w_in_2, conv_w_2, conv_b_2, conv_ln_g_2, conv_ln_b_2,
    w_attn_out_2, w_conv_out_2, w_o_2, ln1_g_2, ln1_b_2, w_ffn_gate_2, w_ffn_up_2, w_ffn_down_2,
    ln2_g_2, ln2_b_2,
):
    x = first_block(
        x, ffn1_norm, ffn1_w_gate, ffn1_w_up, ffn1_w_down, mix_norm, even_w_in, even_w_out,
        ssd_conv_w, ssd_conv_b, ssd_dt_bias, ssd_a_log, ssd_d, ssd_norm, s5_a_re, s5_a_im,
        s5_log_dt, s5_b_re, s5_b_im, s5_c_re, s5_c_im, s5_d, s5_w_glu, s5_b_glu, odd_w_in,
        odd_w_out, attn_q_norm, attn_k_norm, attn_rel_bias, pool_w, pool_scale, ffn2_norm,
        ffn2_w_gate, ffn2_w_up, ffn2_w_down,
    )
    return second_block(
        x, w_in_2, conv_w_2, conv_b_2, conv_ln_g_2, conv_ln_b_2, w_attn_out_2, w_conv_out_2,
        w_o_2, ln1_g_2, ln1_b_2, w_ffn_gate_2, w_ffn_up_2, w_ffn_down_2, ln2_g_2, ln2_b_2,
    )


_drawn_inputs = setup_inputs


def setup_inputs(seed=0):
    import zlib

    import numpy as np

    out = dict(_drawn_inputs(seed))
    spreads = {}
    factors = {'ssd_conv_b': 2.951,
     'ssd_d': 6.791,
     's5_a_re': 64.0,
     's5_b_re': 2.771,
     's5_b_im': 2.811,
     's5_c_re': 2.834,
     's5_c_im': 2.799,
     's5_b_glu': 8.0,
     'attn_q_norm': 8.0,
     'attn_k_norm': 8.0,
     'attn_rel_bias': 8.0,
     'conv_b_2': 8.0,
     'conv_ln_g_2': 8.0,
     'conv_ln_b_2': 31.849,
     'ln1_b_2': 2.768,
     'ln2_b_2': 2.884}
    for name, (base, spread) in spreads.items():
        noise = np.random.default_rng([zlib.crc32(name.encode()), seed]).standard_normal(out[name].shape)
        drawn = base * np.exp(spread * noise) if base else spread * noise
        out[name] = jnp.asarray(drawn.astype(out[name].dtype))
    for name, factor in factors.items():
        out[name] = (out[name] * factor).astype(out[name].dtype)
    return out
```

```python
from contextlib import ExitStack

import numpy as np

import concourse.bass as bass
from concourse import mybir

F32 = mybir.dt.float32
F32R = mybir.dt.float32r
BF16 = mybir.dt.bfloat16
ALU = mybir.AluOpType
ACT = mybir.ActivationFunctionType
AX = mybir.AxisListType

P = 128
S = 512
D = 1024
DC = D // P
FF = 2816
FC = FF // P
HALF = FC // 2
EPS = 1e-6
LN_EPS = 1e-5
RAW = 4
SPLIT = 2
TT = S // P
HD = 64
NEG = -1e30
MAGIC = 1.5 * 2.0 ** 23
S5G = 32


class Unit:

    def __init__(self, kc, src, x, k0, bank, start=True, stop=True):
        self.kc, self.src, self.x, self.k0 = kc, src, x, k0
        self.bank, self.start, self.stop = bank, start, stop


class Stage:

    def __init__(self, bodies, units, chunks, banks):
        self.bodies, self.units, self.chunks, self.banks = bodies, units, chunks, banks
        self.base = None


class StageSems(ExitStack):

    def __init__(self):
        super().__init__()
        self.handles = []

    def enter_context(self, made):
        self.handles.append(super().enter_context(made))
        return self.handles[-1]


def stage(f):
    def run(co, *args, **kwargs):
        co.begin()
        f(co, *args, **kwargs)
        co.end()
    return run


class Core:

    def __init__(self, nc, ctx, dram):
        self.nc, self.ctx, self.dram = nc, ctx, dram
        self.n = 0
        self.stage_sems, self.retired, self.clearing = None, [], []
        self.X = self.sb("X", [P, DC, S])
        self.Hh = self.sb("Hh", [P, DC, S], F32R)
        self.Hl = self.sb("Hl", [P, DC, S], F32R)
        self.raw = [self.sb(f"raw{j}", [P, HALF * P]) for j in range(RAW)]
        self.wh = [self.sb(f"wh{j}", [P, HALF * P], F32R) for j in range(SPLIT)]
        self.wl = [self.sb(f"wl{j}", [P, HALF * P], F32R) for j in range(SPLIT)]
        self.ones = self.sb("ones", [P, P])
        self.cols = self.sb("cols", [P, dram["cols"].shape[1]])
        self.mats = self.sb("mats", [P, 5, P])
        self.ident, self.triu, self.flip, self.rot, self.heads = (self.mats[:, k, :] for k in range(5))
        self.PS = ctx.enter_context(nc.psum_tensor("PS", [P, 8, 512], F32))
        self.raw_in = [self.sem(f"raw_in{j}") for j in range(RAW)]
        self.hi_ready = self.sem("hi_ready")
        self.lo_ready = self.sem("lo_ready")
        self.unit_done = self.sem("unit_done")
        self.stages = []

    def sb(self, name, shape, dt=F32, ctx=None):
        return (ctx or self.ctx).enter_context(self.nc.sbuf_tensor(name, shape, dt))

    def sem(self, name):
        return (self.stage_sems or self.ctx).enter_context(self.nc.semaphore(self.tag(name)))

    def begin(self):
        for done in self.clearing:
            done.close()
        self.clearing = self.retired
        self.retired = []
        for done in self.clearing:
            for s in done.handles:
                self.nc.gpsimd.sem_clear(s)
        self.stage_sems = StageSems()

    def end(self):
        self.retired.append(self.stage_sems)
        self.stage_sems = None

    def tag(self, name):
        self.n += 1
        return f"{name}_{self.n}"

    def plan(self, stage):
        stage.base = self.stages[-1].base + RAW * self.stages[-1].bodies if self.stages else 0
        self.stages.append(stage)
        return stage

    def load_turn(self, sp, st, i):
        for j, u in enumerate(st.units):
            at = st.base + RAW * i + j
            if not (isinstance(at, int) and at < RAW):
                sp.wait_ge(self.lo_ready, at + 1 - RAW)
            sp.dma_start(self.raw[j][:, 0:u.kc * P], u.src(i)).then_inc(self.raw_in[j], 16)

    def load(self, sp, st):
        if st.bodies > 1:
            with sp.Fori(1, st.bodies) as i:
                self.load_turn(sp, st, i)
        k = self.stages.index(st)
        if k + 1 < len(self.stages):
            self.load_turn(sp, self.stages[k + 1], 0)

    def split_hi(self, act, st, i, j):
        kw = st.units[j].kc * P
        act.wait_ge(self.raw_in[j], 16 * (st.base // RAW + 1) + 16 * i)
        act.wait_ge(self.unit_done, st.base + j + 1 + RAW * i)
        self.nc.scalar.activation(self.wh[j % SPLIT][:, 0:kw], self.raw[j][:, 0:kw], ACT.Copy).then_inc(self.hi_ready, 1)

    def split_lo(self, dve, st, i, j):
        kw = st.units[j].kc * P
        dve.wait_ge(self.hi_ready, st.base + j + 1 + RAW * i)
        self.nc.vector.tensor_sub(self.wl[j % SPLIT][:, 0:kw], self.raw[j][:, 0:kw],
                                  self.wh[j % SPLIT][:, 0:kw].bitcast(F32)).then_inc(self.lo_ready, 1)

    def multiply(self, pe, st, bank_free):
        per = RAW // st.chunks

        def turn(i):
            for j, u in enumerate(st.units):
                if j % per == 0:
                    pe.wait_ge(bank_free, st.chunks * i + j // per + 1)
                pe.wait_ge(self.lo_ready, st.base + j + 1 + RAW * i)
                xh, xl = u.x
                out = self.PS[:, u.bank, :]
                for k in range(u.kc):
                    wh = self.wh[j % SPLIT][:, k * P:(k + 1) * P]
                    wl = self.wl[j % SPLIT][:, k * P:(k + 1) * P]
                    first, last = u.start and k == 0, u.stop and k == u.kc - 1
                    self.nc.tensor.matmul(out, wl, xh[:, u.k0 + k, :], start=first, stop=False)
                    self.nc.tensor.matmul(out, wh, xh[:, u.k0 + k, :], start=False, stop=False)
                    done = self.nc.tensor.matmul(out, wh, xl[:, u.k0 + k, :], start=False, stop=last)
                done.then_inc(self.unit_done, 1)
        if st.bodies > 1:
            with pe.Fori(0, st.bodies) as i:
                turn(i)
        else:
            turn(0)

    def wait_units(self, eng, st, i, c, part=None):
        per = RAW // st.chunks
        j = c * per + (per - 1 if part is None else part)
        eng.wait_ge(self.unit_done, SPLIT + st.base + j + 1 + RAW * i)

    def run(self, eng, st, split, read):
        per = RAW // st.chunks

        def turn(i, first):
            for c in range(st.chunks):
                for j in range(c * per, (c + 1) * per):
                    split(eng, st, i, j)
                if c > 0:
                    read(i, c - 1)
                elif not first:
                    read(i - 1, st.chunks - 1)
        turn(0, True)
        if st.bodies > 1:
            with eng.Fori(1, st.bodies) as i:
                turn(i, False)
        read(st.bodies - 1, st.chunks - 1)


def one(t, n, k=None):
    return t[:, bass.ds(n, 1), :]



@stage
def norm_stage(co, n, gain, out, eps, center=False, bias=None, src=None, block_ones=None, width=None):
    nc = co.nc
    src = co.X if src is None else src
    name = co.tag("norm")
    width = width or n * P
    with ExitStack() as ctx:
        SQ = co.sb(f"{name}_sq", [P, n, S], ctx=ctx)
        RS = co.sb(f"{name}_rs", [P, S], ctx=ctx)
        T = co.sb(f"{name}_t", [P, 2, S], ctx=ctx)
        squared = co.sem(f"{name}_squared")
        summed = co.sem(f"{name}_summed")
        rooted = co.sem(f"{name}_rooted")
        scaled = co.sem(f"{name}_scaled")
        mean_summed = co.sem(f"{name}_mean_summed")
        mean_ready = co.sem(f"{name}_mean_ready")
        centered = co.sem(f"{name}_centered")
        normed = co.sem(f"{name}_normed")
        rounded = co.sem(f"{name}_rounded")
        split = isinstance(out, tuple)
        block = ctx.enter_context(nc.Block())

        @block.tensor
        def _(pe):
            if center:
                for c in range(n):
                    m = nc.tensor.matmul(co.PS[:, 1, :], co.ones[:], src[:, c, :], start=c == 0, stop=c == n - 1)
                m.then_inc(mean_summed, 1)
            for c in range(n):
                pe.wait_ge(squared, c + 1)
                m = nc.tensor.matmul(co.PS[:, 0, :], co.ones[:], SQ[:, c, :], start=c == 0, stop=c == n - 1)
            m.then_inc(summed, 1)

        @block.scalar
        def _(act):
            for c in range(n):
                if center:
                    act.wait_ge(centered, c + 1)
                nc.scalar.activation(SQ[:, c, :], src[:, c, :], ACT.Square).then_inc(squared, 1)
            act.wait_ge(scaled, 1)
            nc.scalar.activation(RS[:], RS[:], ACT.Sqrt).then_inc(rooted, 1)
            if split:
                for c in range(n):
                    act.wait_ge(normed, c + 1)
                    nc.scalar.activation(out[0][:, out[2] + c, :], T[:, c % 2, :], ACT.Copy).then_inc(rounded, 1)

        @block.vector
        def _(dve):
            if center:
                dve.wait_ge(mean_summed, 1)
                nc.vector.tensor_scalar(T[:, 0, :], co.PS[:, 1, :], 1.0 / width, None, ALU.mult).then_inc(mean_ready, 1)
                dve.wait_ge(mean_ready, 1)
                for c in range(n):
                    nc.vector.tensor_sub(src[:, c, :], src[:, c, :], T[:, 0, :]).then_inc(centered, 1)
            dve.wait_ge(summed, 1)
            nc.vector.tensor_scalar(RS[:], co.PS[:, 0, :], 1.0 / width, eps, ALU.mult, ALU.add).then_inc(scaled, 1)
            dve.wait_ge(rooted, 1)
            nc.vector.reciprocal(RS[:], RS[:]).then_inc(scaled, 1)
            dve.wait_ge(scaled, 2)
            if center:
                dve.wait_ge(centered, n)
            for c in range(n):
                if split and c >= 2:
                    dve.wait_ge(rounded, c - 1)
                to = T[:, c % 2, :] if split or bias is not None else out[:, c, :]
                nc.vector.scalar_tensor_tensor(to, src[:, c, :], co.cols[:, gain + c:gain + c + 1], RS[:],
                                               ALU.mult, ALU.mult).then_inc(normed, 1)
                if bias is not None:
                    dve.wait_ge(normed, c + 1)
                    nc.vector.tensor_scalar(out[:, c, :], T[:, c % 2, :], co.cols[:, bias + c:bias + c + 1], None,
                                            ALU.add).then_inc(centered, 1)
                if split:
                    dve.wait_ge(rounded, c + 1)
                    nc.vector.tensor_sub(out[1][:, out[2] + c, :], T[:, c % 2, :],
                                         out[0][:, out[2] + c, :].bitcast(F32)).then_inc(centered, 1)


@stage
def split_stage(co, pairs):
    nc = co.nc
    name = co.tag("split")
    rounded, done = co.sem(f"{name}_rounded"), co.sem(f"{name}_done")
    with nc.Block() as block:
        @block.scalar
        def _(act):
            for src, hi, lo in pairs:
                nc.scalar.activation(hi, src, ACT.Copy).then_inc(rounded, 1)

        @block.vector
        def _(dve):
            for n, (src, hi, lo) in enumerate(pairs):
                dve.wait_ge(rounded, n + 1)
                nc.vector.tensor_sub(lo, src, hi.bitcast(F32)).then_inc(done, 1)



def feed(co, name, x=None):
    w = co.dram[name]
    x = x or (co.Hh, co.Hl)
    kc = w.shape[2] // P
    return co.plan(Stage(w.shape[0] // RAW, [
        Unit(kc, lambda i, j=j: w[bass.ds(RAW * i + j, 1)].rearrange("o p n -> p (o n)"), x, 0, j) for j in range(RAW)
    ], RAW, 4))


@stage
def copy_stage(co, st, reads):
    nc = co.nc
    name = co.tag("copy")
    bank_free = co.sem(f"{name}_bank_free")
    with nc.Block() as block:
        @block.sync
        def _(sp):
            co.load(sp, st)

        @block.tensor
        def _(pe):
            co.multiply(pe, st, bank_free)

        @block.scalar
        def _(act):
            act.sem_inc(bank_free, 4)

            def read(i, c):
                if reads and reads(i, c)[0] == "act":
                    co.wait_units(act, st, i, c)
                    reads(i, c)[1](one(co.PS, c)).then_inc(bank_free, 1)
            co.run(act, st, co.split_hi, read)

        @block.vector
        def _(dve):
            def read(i, c):
                if reads and reads(i, c)[0] == "dve":
                    co.wait_units(dve, st, i, c)
                    reads(i, c)[1](one(co.PS, c)).then_inc(bank_free, 1)
            co.run(dve, st, co.split_lo, read)


def plan_ffn(co, k):
    gu, dn = co.dram[f"gu{k}"], co.dram[f"dn{k}"]
    x = (co.Hh, co.Hl)
    up = co.plan(Stage(FC // 2, [
        Unit(DC, lambda i, j=j: gu[bass.ds(RAW * i + j, 1)].rearrange("o p n -> p (o n)"), x, 0, j) for j in range(RAW)
    ], 2, 2))
    down = co.plan(Stage(DC // 2, [
        Unit(HALF, lambda i, j=j: dn[bass.ds(RAW * i + j, 1)].rearrange("o p n -> p (o n)"), None, HALF * (j % 2),
             4 + j // 2, j % 2 == 0, j % 2 == 1) for j in range(RAW)
    ], 2, 2))
    return up, down


@stage
def ffn(co, up, down, half, alpha=1.0):
    assert half == 1.0 or alpha == 1.0
    nc = co.nc
    name = co.tag("ffn")
    with ExitStack() as ctx:
        Gh = co.sb(f"{name}_gh", [P, FC, S], F32R, ctx)
        Gl = co.sb(f"{name}_gl", [P, FC, S], F32R, ctx)
        SG = co.sb(f"{name}_sg", [P, 2, 1, S], ctx=ctx)
        T = co.sb(f"{name}_t", [P, 2, 1, S], ctx=ctx)
        for u in down.units:
            u.x = (Gh, Gl)
        gated = co.sem(f"{name}_gated")
        product = co.sem(f"{name}_product")
        rounded = co.sem(f"{name}_rounded")
        g_ready = co.sem(f"{name}_g_ready")
        down_free = co.sem(f"{name}_down_free")
        with nc.Block() as block:
            @block.sync
            def _(sp):
                co.load(sp, up)

            @block.tensor
            def _(pe):
                co.multiply(pe, up, product)

            @block.scalar
            def _(act):
                def read(i, c):
                    co.wait_units(act, up, i, c, 0)
                    nc.scalar.activation(SG[:, c], one(co.PS, 2 * c), ACT.Silu).then_inc(gated, 1)
                    act.wait_ge(product, 2 + 2 * i + c + 1)
                    nc.scalar.activation(one(Gh, 2 * i + c), T[:, c], ACT.Copy).then_inc(rounded, 1)
                co.run(act, up, co.split_hi, read)

            @block.vector
            def _(dve):
                dve.sem_inc(product, 2)

                def read(i, c):
                    co.wait_units(dve, up, i, c, 1)
                    dve.wait_ge(gated, 2 * i + c + 1)
                    nc.vector.tensor_mul(T[:, c], one(co.PS, 2 * c + 1), SG[:, c]).then_inc(product, 1)
                    dve.wait_ge(rounded, 2 * i + c + 1)
                    nc.vector.tensor_sub(one(Gl, 2 * i + c), T[:, c], one(Gh, 2 * i + c).bitcast(F32)).then_inc(g_ready, 1)
                co.run(dve, up, co.split_lo, read)
        with nc.Block() as block:
            @block.sync
            def _(sp):
                co.load(sp, down)

            @block.tensor
            def _(pe):
                co.multiply(pe, down, down_free)

            @block.scalar
            def _(act):
                co.run(act, down, co.split_hi, lambda i, c: None)

            @block.vector
            def _(dve):
                dve.sem_inc(down_free, 2)

                def read(i, c):
                    co.wait_units(dve, down, i, c)
                    x = one(co.X, 2 * i + c)
                    a, b = (x, one(co.PS, 4 + c)) if half == 1.0 else (one(co.PS, 4 + c), x)
                    nc.vector.scalar_tensor_tensor(x, a, alpha * half, b, ALU.mult, ALU.add).then_inc(down_free, 1)
                co.run(dve, down, co.split_lo, read)


def add_stage(co, st, alpha=1.0):
    def reads(i, c):
        x = one(co.X, RAW * i + c)
        return "dve", lambda ps: co.nc.vector.scalar_tensor_tensor(x, x, alpha, ps, ALU.mult, ALU.add)
    copy_stage(co, st, reads)





SSD_H = 8
OFF = [0, 512, 896, 1152]
TRI = 1280


@stage
def causal_conv_silu(co, EZ, XC, cols, dtm):
    nc = co.nc
    name = "ssd_conv"
    DT, AT, W = dtm
    c0 = co.cols
    tapped, activated, dt_step, a_step = (co.sem(f"{name}_{s}") for s in ("tapped", "activated", "dt_step", "a_step"))
    with nc.Block() as block:
        @block.vector
        def _(dve):
            v = nc.vector
            ps = co.PS[0:SSD_H, 4, :]
            steps = [0]

            def step(ins):
                steps[0] += 1
                ins.then_inc(dt_step, 1)
                dve.wait_ge(dt_step, steps[0])
            xb, ab, q, z, z2, rl = (W[:, n, :] for n in range(6))
            step(v.tensor_scalar(xb, ps, c0[0:SSD_H, cols["dt_bias"]:cols["dt_bias"] + 1], None, ALU.add))
            step(v.scalar_tensor_tensor(ab, xb, -1.0, xb, ALU.mult, ALU.max))
            step(v.tensor_scalar(rl, xb, 0.0, None, ALU.max))
            for tap in range(4):
                for c in range(8):
                    w = c0[:, cols["conv_w"] + 8 * (3 - tap) + c:cols["conv_w"] + 8 * (3 - tap) + c + 1]
                    if tap == 0:
                        v.tensor_scalar(XC[:, c, :], EZ[:, 4 + c, :], w, c0[:, cols["conv_b"] + c:cols["conv_b"] + c + 1],
                                        ALU.mult, ALU.add).then_inc(tapped, 1)
                    else:
                        dve.wait_ge(tapped, 8 * (tap - 1) + c + 1)
                        v.scalar_tensor_tensor(XC[:, c, tap:], EZ[:, 4 + c, 0:S - tap], w, XC[:, c, tap:],
                                               ALU.mult, ALU.add).then_inc(tapped, 1)
            dve.wait_ge(a_step, 2)
            step(v.tensor_scalar(q, ab, 2.0, None, ALU.add))
            step(v.reciprocal(q, q))
            step(v.tensor_mul(z, ab, q))
            step(v.tensor_mul(z2, z, z))
            step(v.tensor_scalar(q, z2, 1.0 / 15, None, ALU.mult))
            for odd in (13, 11, 9, 7, 5, 3):
                step(v.scalar_tensor_tensor(q, q, 1.0 / odd, z2, ALU.add, ALU.mult))
            step(v.scalar_tensor_tensor(q, q, 1.0, z, ALU.add, ALU.mult))
            step(v.scalar_tensor_tensor(DT[:], q, 2.0, rl, ALU.mult, ALU.add))
            step(v.tensor_scalar(xb, DT[:], W[:, 6, 0:1], -1.0, ALU.mult, ALU.mult))
            step(v.tensor_tensor_scan(AT[:], co.ones8[:], xb, 0.0, ALU.mult, ALU.add))

        @block.scalar
        def _(act):
            nc.scalar.activation(W[:, 6, 0:1], c0[0:SSD_H, cols["a_log"]:cols["a_log"] + 1], ACT.Exp).then_inc(a_step, 1)
            act.wait_ge(dt_step, 2)
            nc.scalar.activation(W[:, 1, :], W[:, 1, :], ACT.Exp, scale=-1.0).then_inc(a_step, 1)
            for c in range(4):
                nc.scalar.activation(EZ[:, c, :], EZ[:, c, :], ACT.Silu).then_inc(activated, 1)
            for c in range(8):
                act.wait_ge(tapped, 24 + c + 1)
                nc.scalar.activation(XC[:, c, :], XC[:, c, :], ACT.Silu).then_inc(activated, 1)


@stage
def ssd_tokens(co, XC, dtm, AC, XDT, CB):
    nc = co.nc
    DT, AT, W = dtm
    name = "ssd_tok"
    cols_done, x_done, cb_done, cols_read, x_read, cb_read, masked = (
        co.sem(f"{name}_{s}") for s in ("cols_done", "x_done", "cb_done", "cols_read", "x_read", "cb_read", "masked"))
    with nc.Block() as block:
        @block.tensor
        def _(pe):
            for k, src in enumerate((AT, DT)):
                for t in range(TT):
                    m = nc.tensor.matmul(co.PS[:, 7, (k * TT + t) * 8:(k * TT + t + 1) * 8], src[:, t * P:(t + 1) * P],
                                         co.ident[0:8, 0:8], start=True, stop=True)
            m.then_inc(cols_done, 1)
            for t in range(TT):
                for c in range(4):
                    m = nc.tensor.transpose(co.PS[:, t, c * P:(c + 1) * P], XC[:, c, t * P:(t + 1) * P], co.ident)
                m.then_inc(x_done, 1)
            for g in range(2):
                for t in range(TT):
                    n = g * TT + t
                    if n >= 3:
                        pe.wait_ge(cb_read, n - 2)
                    nc.tensor.matmul(co.PS[:, 4 + n % 3, 0:S - t * P], XC[:, 4 + g, t * P:(t + 1) * P],
                                     XC[:, 6 + g, t * P:], start=True, stop=True).then_inc(cb_done, 1)

        @block.scalar
        def _(act):
            for g in range(2):
                for t in range(TT):
                    act.wait_ge(cb_done, g * TT + t + 1)
                    nc.scalar.activation(CB[:, g, OFF[t]:OFF[t] + S - t * P], co.PS[:, 4 + (g * TT + t) % 3, 0:S - t * P],
                                         ACT.Copy).then_inc(cb_read, 1)

        @block.vector
        def _(dve):
            dve.wait_ge(cols_done, 1)
            nc.vector.tensor_copy(AC[:], co.PS[:, 7, 0:64]).then_inc(cols_read, 1)
            dve.wait_ge(cols_read, 1)
            for t in range(TT):
                dve.wait_ge(x_done, t + 1)
                dt = AC[:, 32 + 8 * t:32 + 8 * t + 8].unsqueeze(2).broadcast_to([P, 8, HD])
                nc.vector.tensor_mul(XDT[:, t, :].rearrange("p (h d) -> p h d", d=HD),
                                     co.PS[:, t, :].rearrange("p (h d) -> p h d", d=HD), dt).then_inc(x_read, 1)
            for g in range(2):
                for t in range(TT):
                    dve.wait_ge(cb_read, g * TT + t + 1)
                    d = CB[:, g, OFF[t]:OFF[t] + P]
                    nc.vector.tensor_mul(d, d, co.triu).then_inc(masked, 1)


@stage
def ssd_heads(co, dtm, AC, XDT, CB, XC, EZ, Y, cols):
    nc = co.nc
    DT, AT, W = dtm
    name = "ssd_heads"
    with ExitStack() as ctx:
        SEG = co.sb(f"{name}_seg", [P, 2, TRI], ctx=ctx)
        M = co.sb(f"{name}_m", [P, 2, TRI], ctx=ctx)
        spread, seg_ready, decayed, weighted, y_done, skipped = (
            co.sem(f"{name}_{s}") for s in ("spread", "seg_ready", "decayed", "weighted", "y_done", "skipped"))
        block = ctx.enter_context(nc.Block())

        @block.tensor
        def _(pe):
            def spread_a(h):
                if h >= 2:
                    pe.wait_ge(seg_ready, h - 1)
                nc.tensor.matmul(co.PS[:, h % 2, :], co.sel8[:, h * P:(h + 1) * P], AT[:], start=True, stop=True).then_inc(spread, 1)
            spread_a(0)
            for h in range(SSD_H):
                if h + 1 < SSD_H:
                    spread_a(h + 1)
                pe.wait_ge(weighted, h + 1)
                po = HD * (h % 2)
                for t in range(TT):
                    m = nc.tensor.matmul(co.PS[po:po + HD, 2 + h // 2, t * P:], XDT[:, t, h * HD:(h + 1) * HD],
                                         M[:, h % 2, OFF[t]:OFF[t] + S - t * P], start=t == 0, stop=t == TT - 1)
                m.then_inc(y_done, 1)

        @block.scalar
        def _(act):
            for h in range(SSD_H):
                act.wait_ge(seg_ready, h + 1)
                nc.scalar.activation(SEG[:, h % 2, :], SEG[:, h % 2, :], ACT.Exp).then_inc(decayed, 1)

        @block.vector
        def _(dve):
            def weigh(h):
                dve.wait_ge(decayed, h + 1)
                if h >= 2:
                    dve.wait_ge(y_done, h - 1)
                nc.vector.tensor_mul(M[:, h % 2, :], SEG[:, h % 2, :], CB[:, h // 4, :]).then_inc(weighted, 1)
            for h in range(SSD_H):
                dve.wait_ge(spread, h + 1)
                if h >= 2:
                    dve.wait_ge(weighted, h - 1)
                for t in range(TT):
                    s = nc.vector.tensor_scalar(SEG[:, h % 2, OFF[t]:OFF[t] + S - t * P], co.PS[:, h % 2, t * P:],
                                                AC[:, 8 * t + h:8 * t + h + 1], 0.0, ALU.subtract, ALU.min)
                s.then_inc(seg_ready, 1)
                if h >= 1:
                    weigh(h - 1)
            weigh(SSD_H - 1)
            for c in range(4):
                dve.wait_ge(y_done, 2 * c + 2)
                nc.vector.scalar_tensor_tensor(Y[:, c, :], XC[:, c, :], co.cols[:, cols["ssd_d"] + c:cols["ssd_d"] + c + 1],
                                               co.PS[:, 2 + c, :], ALU.mult, ALU.add).then_inc(skipped, 1)
            for c in range(4):
                dve.wait_ge(skipped, c + 1)
                nc.vector.tensor_mul(Y[:, c, :], Y[:, c, :], EZ[:, c, :]).then_inc(skipped, 1)


NT = 48
TWO_PI = 6.283185307179586
WRAP = 6.2831845
CW1 = 6.28125
CW2 = TWO_PI - CW1


@stage
def s5_parameters(co, SP, PH, B, C, BT, CT, cols):
    nc = co.nc
    with ExitStack() as ctx:
        N = co.sb("s5_n", [P, S5G, NT], ctx=ctx)
        L = co.sb("s5_l", [P, S5G, NT], ctx=ctx)
        BB = co.sb("s5_bb", [P, 2, S5G, 16], ctx=ctx)
        CC = co.sb("s5_cc", [P, 2, S5G, 16], ctx=ctx)
        loaded, vstep, astep, turned, zeroed = (co.sem(f"s5p_{s}") for s in ("loaded", "vstep", "astep", "turned", "zeroed"))
        block = ctx.enter_context(nc.Block())
        ar, ai, dt, mag, ang, ph, sn, cs, n, t1, t2, den, fre, fim, phh, phl = (SP[:, k, :] for k in range(16))
        sg = co.cols[:, cols["sign"]:cols["sign"] + 1]

        @block.sync
        def _(sp):
            sp.dma_start(SP[:, 0:3, :], co.dram["s5p"].rearrange("p (a g) -> p a g", g=S5G)).then_inc(loaded, 16)
            sp.dma_start(B[:], co.dram["s5b"].rearrange("p (a g i) -> p a g i", g=S5G, i=16)).then_inc(loaded, 16)
            sp.dma_start(C[:], co.dram["s5c"].rearrange("p (a g i) -> p a g i", g=S5G, i=16)).then_inc(loaded, 16)

        @block.gpsimd
        def _(pool):
            nc.gpsimd.memset(CT[:], 0.0).then_inc(zeroed, 1)

        @block.scalar
        def _(act):
            act.wait_ge(loaded, 48)
            nc.scalar.activation(dt, dt, ACT.Exp).then_inc(astep, 1)
            act.wait_ge(vstep, 1)
            nc.scalar.activation(mag, t1, ACT.Exp).then_inc(astep, 1)
            act.wait_ge(vstep, 10)
            nc.scalar.activation(sn, sn, ACT.Sin, scale=WRAP).then_inc(astep, 1)
            nc.scalar.activation(cs, cs, ACT.Sin, scale=WRAP).then_inc(astep, 1)

        @block.tensor
        def _(pe):
            pe.wait_ge(vstep, 33)
            for k in range(2):
                for q in range(4):
                    m = nc.tensor.transpose(co.PS[:, k, q * P:(q + 1) * P],
                                            BB[:, k, 8 * q:8 * q + 8, :].rearrange("p g i -> p (g i)"), co.ident)
            m.then_inc(turned, 1)

        @block.vector
        def _(dve):
            v = nc.vector
            steps = [0]

            def step(ins):
                steps[0] += 1
                ins.then_inc(vstep, 1)
                dve.wait_ge(vstep, steps[0])

            def over(x, k):
                return x.unsqueeze(2).broadcast_to([P, S5G, k])
            dve.wait_ge(astep, 1)
            step(v.tensor_mul(t1, dt, ar))
            step(v.tensor_mul(ang, dt, ai))
            step(v.tensor_scalar(n, ang, 1.0 / TWO_PI, MAGIC, ALU.mult, ALU.add))
            step(v.tensor_scalar(n, n, MAGIC, None, ALU.subtract))
            step(v.scalar_tensor_tensor(ph, n, -CW1, ang, ALU.mult, ALU.add))
            step(v.scalar_tensor_tensor(ph, n, -CW2, ph, ALU.mult, ALU.add))
            step(v.tensor_scalar(ph, ph, 1.0 / TWO_PI, None, ALU.mult))
            step(v.tensor_scalar(sn, ph, 0.5, -0.5, ALU.min, ALU.max))
            step(v.scalar_tensor_tensor(cs, sn, -1.0, sn, ALU.mult, ALU.max))
            step(v.tensor_scalar(cs, cs, -1.0, 0.25, ALU.mult, ALU.add))
            dve.wait_ge(astep, 4)
            step(v.tensor_mul(sn, sn, mag))
            step(v.tensor_mul(cs, cs, mag))
            step(v.tensor_scalar(cs, cs, 1.0, None, ALU.subtract))
            step(v.tensor_mul(den, ar, ar))
            step(v.tensor_mul(t1, ai, ai))
            step(v.tensor_add(den, den, t1))
            step(v.reciprocal(den, den))
            step(v.tensor_mul(t1, cs, ar))
            step(v.tensor_mul(t2, sn, ai))
            step(v.tensor_add(t1, t1, t2))
            step(v.tensor_mul(fre, t1, den))
            step(v.tensor_mul(t1, sn, ar))
            step(v.tensor_mul(t2, cs, ai))
            step(v.tensor_sub(t1, t1, t2))
            step(v.tensor_mul(fim, t1, den))
            step(v.tensor_scalar(t1, fim, sg, -1.0, ALU.mult, ALU.mult))
            step(v.tensor_scalar(t2, fre, sg, None, ALU.mult))
            step(v.tensor_mul(BB[:, 0], B[:, 0], over(fre, 16)))
            step(v.tensor_mul(BB[:, 1], B[:, 1], over(t1, 16)))
            step(v.tensor_add(BB[:, 0], BB[:, 0], BB[:, 1]))
            step(v.tensor_mul(BB[:, 1], B[:, 1], over(t2, 16)))
            step(v.tensor_mul(CC[:, 0], B[:, 0], over(fim, 16)))
            step(v.tensor_add(BB[:, 1], BB[:, 1], CC[:, 0]))
            step(v.tensor_scalar(CC[:, 0], C[:, 0], sg, None, ALU.mult))
            step(v.tensor_scalar(CC[:, 1], C[:, 1], -1.0, None, ALU.mult))
            step(v.tensor_scalar(phh, ph, 3072.0, None, ALU.add))
            step(v.tensor_scalar(phh, phh, 3072.0, None, ALU.subtract))
            step(v.tensor_sub(phl, ph, phh))
            tv = co.cols[:, cols["tokens"]:cols["tokens"] + NT].unsqueeze(1).broadcast_to([P, S5G, NT])
            step(v.tensor_mul(PH[:], over(phh, NT), tv))
            step(v.tensor_scalar(N[:], PH[:], MAGIC, None, ALU.add))
            step(v.tensor_scalar(N[:], N[:], MAGIC, None, ALU.subtract))
            step(v.tensor_sub(PH[:], PH[:], N[:]))
            step(v.tensor_mul(L[:], over(phl, NT), tv))
            step(v.tensor_add(PH[:], PH[:], L[:]))
            dve.wait_ge(zeroed, 1)
            for k in range(2):
                for e in range(2):
                    v.tensor_copy(CT[:, k, :, e, 16 * e:16 * e + 16],
                                  CC[:, k].rearrange("p (a e) i -> p a e i", e=2)[:, :, e, :]).then_inc(zeroed, 1)
            dve.wait_ge(turned, 1)
            for k in range(2):
                for e in range(2):
                    m = co.cols[:, cols["pair"] + e:cols["pair"] + e + 1]
                    v.tensor_scalar(BT[:, k, :, e, :], co.PS[:, k, :].rearrange("p (q n) -> p q n", n=P), m, None,
                                    ALU.mult).then_inc(zeroed, 1)


@stage
def s5_groups(co, SP, PH, BT, CT, U, cols):
    nc = co.nc
    with ExitStack() as ctx:
        W = co.sb("s5_w", [P, 2, S], ctx=ctx)
        R = co.sb("s5_r", [P, 2, S], ctx=ctx)
        CS = co.sb("s5_cs", [P, 2, S], ctx=ctx)
        SN = co.sb("s5_sn", [P, 2, S], ctx=ctx)
        D1 = co.sb("s5_d1", [P, 2, S], ctx=ctx)
        D2 = co.sb("s5_d2", [P, 2, S], ctx=ctx)
        G = co.sb("s5_g", [P, 2, S], ctx=ctx)
        O1 = co.sb("s5_o1", [P, 2, S], ctx=ctx)
        O2 = co.sb("s5_o2", [P, 2, S], ctx=ctx)
        (phased, whole, wrapped, sine, folded, cosine, driven, turned1, turned2, drive, states, back, out_done) = (
            co.sem(f"s5_{s}") for s in ("phased", "whole", "wrapped", "sine", "folded", "cosine", "driven",
                                        "turned1", "turned2", "drive", "states", "back", "out_done"))
        block = ctx.enter_context(nc.Block())
        PI2 = co.cols[:, cols["half_pi"]:cols["half_pi"] + 1]

        @block.gpsimd
        def _(pool):
            def phase(g):
                b = g % 2
                if g >= 2:
                    pool.wait_ge(cosine, g - 1)
                a = PH[:, g, 32:48].unsqueeze(2).broadcast_to([P, 16, 32])
                t = PH[:, g, 0:32].unsqueeze(1).broadcast_to([P, 16, 32])
                nc.gpsimd.tensor_add(R[:, b].rearrange("p (a t) -> p a t", t=32), a, t).then_inc(phased, 1)
                pool.wait_ge(whole, g + 1)
                nc.gpsimd.tensor_sub(R[:, b], R[:, b], W[:, b]).then_inc(wrapped, 1)
            phase(0)
            for g in range(S5G):
                if g + 1 < S5G:
                    phase(g + 1)
                pool.wait_ge(turned2, g + 1)
                nc.gpsimd.tensor_add(D1[:, g % 2], D1[:, g % 2], D2[:, g % 2]).then_inc(drive, 1)

        @block.scalar
        def _(act):
            for g in range(S5G):
                b = g % 2
                act.wait_ge(wrapped, g + 1)
                if g >= 2:
                    act.wait_ge(back, g - 1)
                nc.scalar.activation(SN[:, b], R[:, b], ACT.Sin, scale=WRAP).then_inc(sine, 1)
                act.wait_ge(sine, g + 1)
                nc.scalar.activation(R[:, b], R[:, b], ACT.Abs).then_inc(folded, 1)
                act.wait_ge(folded, g + 1)
                nc.scalar.activation(CS[:, b], R[:, b], ACT.Sin, scale=-WRAP, bias=PI2).then_inc(cosine, 1)

        @block.tensor
        def _(pe):
            def drives(g):
                q, j = g // 8, g % 8
                r = 32 * (j // 2)
                if g >= 2:
                    pe.wait_ge(turned2, g - 1)
                for k in range(2):
                    m = nc.tensor.matmul(co.PS[:, 2 * (g % 2) + k, :], BT[r:r + 32, k, q, j % 2, :], U[r:r + 32, q, :],
                                         start=True, stop=True)
                m.then_inc(driven, 1)
            drives(0)
            for g in range(S5G):
                if g + 1 < S5G:
                    drives(g + 1)
                q, j = g // 8, g % 8
                r = 32 * (j // 2)
                pe.wait_ge(back, g + 1)
                for k, o in enumerate((O1, O2)):
                    m = nc.tensor.matmul(co.PS[r:r + 32, 4 + q, :], CT[:, k, g // 2, j % 2, :], o[:, g % 2, :],
                                         start=j % 2 == 0 and k == 0, stop=j % 2 == 1 and k == 1)
                m.then_inc(out_done, 1)

        @block.vector
        def _(dve):
            v = nc.vector

            def whole_turns(g):
                dve.wait_ge(phased, g + 1)
                if g >= 2:
                    dve.wait_ge(wrapped, g - 1)
                v.tensor_scalar(W[:, g % 2], R[:, g % 2], MAGIC, MAGIC, ALU.add, ALU.subtract).then_inc(whole, 1)

            def turn(g):
                b = g % 2
                dve.wait_ge(driven, g + 1)
                dve.wait_ge(cosine, g + 1)
                if g >= 2:
                    dve.wait_ge(states, g - 1)
                v.tensor_mul(D1[:, b], co.PS[:, 2 * b, :], CS[:, b]).then_inc(turned1, 1)
                v.tensor_mul(D2[:, b], co.PS[:, 2 * b + 1, :], SN[:, b]).then_inc(turned2, 1)
            whole_turns(0)
            whole_turns(1)
            turn(0)
            for g in range(S5G):
                b = g % 2
                if g + 2 < S5G:
                    whole_turns(g + 2)
                if g + 1 < S5G:
                    turn(g + 1)
                dve.wait_ge(drive, g + 1)
                mag = SP[:, 3, g:g + 1].broadcast_to([P, S])
                v.tensor_tensor_scan(G[:, b], mag, D1[:, b], 0.0, ALU.mult, ALU.add).then_inc(states, 1)
                dve.wait_ge(states, g + 1)
                if g >= 2:
                    dve.wait_ge(out_done, g - 1)
                v.tensor_mul(O1[:, b], G[:, b], CS[:, b])
                v.tensor_mul(O2[:, b], G[:, b], SN[:, b]).then_inc(back, 1)


@stage
def s5_out(co, U, YB, G4, cols):
    nc = co.nc
    with ExitStack() as ctx:
        T = co.sb("s5o_t", [P, 4, S], ctx=ctx)
        y_ready, gelued, rounded, done = (co.sem(f"s5o_{s}") for s in ("y_ready", "gelued", "rounded", "done"))
        block = ctx.enter_context(nc.Block())

        @block.vector
        def _(dve):
            for c in range(4):
                nc.vector.scalar_tensor_tensor(YB[:, c, :], U[:, c, :], co.cols[:, cols["s5_d"] + c:cols["s5_d"] + c + 1],
                                               co.PS[:, 4 + c, :], ALU.mult, ALU.add).then_inc(y_ready, 1)
            for c in range(4):
                dve.wait_ge(rounded, c + 1)
                nc.vector.tensor_sub(G4[1][:, c, :], T[:, c, :], G4[0][:, c, :].bitcast(F32)).then_inc(done, 1)

        @block.scalar
        def _(act):
            for c in range(4):
                act.wait_ge(y_ready, c + 1)
                nc.scalar.activation(T[:, c, :], YB[:, c, :], ACT.Gelu_apprx_tanh).then_inc(gelued, 1)
                act.wait_ge(gelued, c + 1)
                nc.scalar.activation(G4[0][:, c, :], T[:, c, :], ACT.Copy).then_inc(rounded, 1)


@stage
def gated_split(co, YB, SGT, c0):
    nc = co.nc
    name = co.tag("gsplit")
    product, rounded, done = (co.sem(f"{name}_{s}") for s in ("product", "rounded", "done"))
    with nc.Block() as block:
        @block.vector
        def _(dve):
            for c in range(4):
                nc.vector.tensor_mul(YB[:, c, :], YB[:, c, :], SGT[:, c, :]).then_inc(product, 1)
            for c in range(4):
                dve.wait_ge(rounded, c + 1)
                nc.vector.tensor_sub(co.Hl[:, c0 + c, :], YB[:, c, :], co.Hh[:, c0 + c, :].bitcast(F32)).then_inc(done, 1)

        @block.scalar
        def _(act):
            for c in range(4):
                act.wait_ge(product, c + 1)
                nc.scalar.activation(co.Hh[:, c0 + c, :], YB[:, c, :], ACT.Copy).then_inc(rounded, 1)


def to_buffer(co, buf, func=ACT.Copy):
    def reads(i, c):
        if c % 2 == 0 or func != ACT.Copy:
            return "act", lambda ps: co.nc.scalar.activation(one(buf, RAW * i + c), ps, func)
        return "dve", lambda ps: co.nc.vector.tensor_copy(one(buf, RAW * i + c), ps)
    return reads


def plan_even(co):
    u = feed(co, "ein_u")
    zx = feed(co, "ein_zx")
    w = co.dram["ein_dt"]
    dt = co.plan(Stage(1, [Unit(2, lambda i, j=j: w[j], (co.Hh, co.Hl), 2 * j, 4, j == 0, j == RAW - 1)
                           for j in range(RAW)], 1, 1))
    glu = feed(co, "glu")
    out = feed(co, "eout")
    return u, zx, dt, glu, out


def even_mixer(co, plan, cols):
    nc = co.nc
    st_u, st_zx, st_dt, st_glu, st_out = plan
    with ExitStack() as ctx:
        U = co.sb("U", [P, 4, S], ctx=ctx)
        copy_stage(co, st_u, to_buffer(co, U))
        with ExitStack() as inner:
            EZ = co.sb("EZ", [P, 12, S], ctx=inner)
            XC = co.sb("XC", [P, 8, S], ctx=inner)
            DT = co.sb("DT", [SSD_H, S], ctx=inner)
            AT = co.sb("AT", [SSD_H, S], ctx=inner)
            AC = co.sb("AC", [P, 64], ctx=inner)
            co.sel8 = co.sb("sel8", [SSD_H, SSD_H * P], ctx=inner)
            copy_stage(co, st_zx, to_buffer(co, EZ))
            with ExitStack() as tmp:
                W8 = co.sb("W8", [SSD_H, 7, S], ctx=tmp)
                co.ones8 = co.sb("ones8", [SSD_H, S], ctx=tmp)
                copy_stage(co, st_dt, None)
                fill, sel_in = co.sem("ones8_filled"), co.sem("sel8_in")
                with nc.Block() as block:
                    @block.sync
                    def _(sp):
                        sp.dma_start(co.sel8[:], co.dram["sel8"]).then_inc(sel_in, 16)
                        sp.wait_ge(sel_in, 16)

                    @block.gpsimd
                    def _(pool):
                        nc.gpsimd.memset(co.ones8[:], 1.0).then_inc(fill, 1)
                causal_conv_silu(co, EZ, XC, cols, (DT, AT, W8))
            with ExitStack() as tmp:
                XDT = co.sb("XDT", [P, TT, S], ctx=tmp)
                CB = co.sb("CB", [P, 2, TRI], ctx=tmp)
                Y = co.sb("Y", [P, 4, S], ctx=tmp)
                ssd_tokens(co, XC, (DT, AT, None), AC, XDT, CB)
                ssd_heads(co, (DT, AT, None), AC, XDT, CB, XC, EZ, Y, cols)
                for g in range(2):
                    norm_stage(co, 2, cols["ssd_norm"] + 2 * g, (co.Hh, co.Hl, 2 * g), EPS, src=Y[:, 2 * g:2 * g + 2, :])
        with ExitStack() as inner:
            YB = co.sb("YB", [P, 4, S], ctx=inner)
            with ExitStack() as tmp:
                SP = co.sb("s5_sp", [P, 16, S5G], ctx=tmp)
                PH = co.sb("s5_ph", [P, S5G, NT], ctx=tmp)
                BT = co.sb("s5_bt", [P, 2, 4, 2, P], ctx=tmp)
                CT = co.sb("s5_ct", [P, 2, S5G // 2, 2, 32], ctx=tmp)
                B = co.sb("s5_b", [P, 2, S5G, 16], ctx=tmp)
                C = co.sb("s5_c", [P, 2, S5G, 16], ctx=tmp)
                s5_parameters(co, SP, PH, B, C, BT, CT, cols)
                s5_groups(co, SP, PH, BT, CT, U, cols)
            GH = co.sb("s5_gh", [P, 4, S], F32R, inner)
            GL = co.sb("s5_gl", [P, 4, S], F32R, inner)
            s5_out(co, U, YB, (GH, GL), cols)
            for u in st_glu.units:
                u.x = (GH, GL)
            SGT = co.sb("s5_sgt", [P, 4, S], ctx=inner)
            copy_stage(co, st_glu, lambda i, c: ("act", lambda ps: nc.scalar.activation(
                SGT[:, c:c + 1, :], ps, ACT.Sigmoid, bias=co.cols[:, cols["b_glu"] + c:cols["b_glu"] + c + 1])))
            gated_split(co, YB, SGT, 4)
        add_stage(co, st_out)





@stage
def head_norms(co, QK, n, q_chunks, cols):
    nc = co.nc
    with ExitStack() as ctx:
        SQ = co.sb("hn_sq", [P, n, S], ctx=ctx)
        R = co.sb("hn_r", [P, TT, n, 2], ctx=ctx)
        RT = co.sb("hn_rt", [2 * n, S], ctx=ctx)
        SEL = co.sb("hn_sel", [2 * n, n * P], ctx=ctx)
        squared, summed, scaled, rooted, inverted, turned, selected, spread, done = (
            co.sem(f"hn_{s}") for s in ("squared", "summed", "scaled", "rooted", "inverted", "turned", "selected",
                                        "spread", "done"))
        block = ctx.enter_context(nc.Block())

        @block.scalar
        def _(act):
            for c in range(n):
                nc.scalar.activation(SQ[:, c, :], QK[:, c, :], ACT.Square).then_inc(squared, 1)
            act.wait_ge(scaled, 1)
            nc.scalar.activation(R[:], R[:], ACT.Sqrt).then_inc(rooted, 1)

        @block.tensor
        def _(pe):
            for c in range(n):
                pe.wait_ge(squared, c + 1)
                for t in range(TT):
                    m = nc.tensor.matmul(co.PS[:, 0, (t * n + c) * 2:(t * n + c) * 2 + 2], SQ[:, c, t * P:(t + 1) * P],
                                         co.heads[:, 0:P:64], start=True, stop=True)
            m.then_inc(summed, 1)
            pe.wait_ge(inverted, 2)
            for t in range(TT):
                m = nc.tensor.transpose(co.PS[0:2 * n, 5, t * P:(t + 1) * P], R[:, t, :, :].rearrange("p c e -> p (c e)"),
                                        co.ident)
            m.then_inc(turned, 1)
            pe.wait_ge(inverted, 3)
            pe.wait_ge(selected, 16)
            for c in range(n):
                if c >= 4:
                    pe.wait_ge(done, c - 3)
                nc.tensor.matmul(co.PS[:, 1 + c % 4, :], SEL[:, c * P:(c + 1) * P], RT[:], start=True, stop=True).then_inc(spread, 1)

        @block.sync
        def _(sp):
            sp.dma_start(SEL[:], co.dram["hankel_sel"]).then_inc(selected, 16)

        @block.vector
        def _(dve):
            dve.wait_ge(summed, 1)
            nc.vector.tensor_scalar(R[:].rearrange("p t c e -> p (t c e)"), co.PS[:, 0, 0:TT * n * 2], 1.0 / HD, EPS,
                                    ALU.mult, ALU.add).then_inc(scaled, 1)
            dve.wait_ge(rooted, 1)
            nc.vector.reciprocal(R[:], R[:]).then_inc(inverted, 1)
            dve.wait_ge(inverted, 1)
            q = R[:, :, 0:q_chunks, :]
            nc.vector.tensor_scalar(q, q, HD ** -0.5, None, ALU.mult).then_inc(inverted, 1)
            dve.wait_ge(turned, 1)
            nc.vector.tensor_copy(RT[:], co.PS[0:2 * n, 5, :]).then_inc(inverted, 1)
            for c in range(n):
                dve.wait_ge(spread, c + 1)
                g = cols["q_gain"] if c < q_chunks else cols["k_gain"]
                nc.vector.scalar_tensor_tensor(QK[:, c, :], QK[:, c, :], co.cols[:, g:g + 1], co.PS[:, 1 + c % 4, :],
                                               ALU.mult, ALU.mult).then_inc(done, 1)


@stage
def turn_values(co, groups):
    nc = co.nc
    name = co.tag("values")
    turned, stored = co.sem(f"{name}_turned"), co.sem(f"{name}_stored")
    with nc.Block() as block:
        @block.tensor
        def _(pe):
            for n, (V, tokens) in enumerate(groups):
                if n >= 2:
                    pe.wait_ge(stored, TT * (n - 1))
                for t in range(TT):
                    for c in range(4):
                        m = nc.tensor.transpose(co.PS[:, 4 * (n % 2) + t, c * P:(c + 1) * P], V[:, c, tokens(t)], co.ident)
                m.then_inc(turned, 1)

        @block.vector
        def _(dve):
            for n, (V, tokens) in enumerate(groups):
                dve.wait_ge(turned, n + 1)
                for t in range(TT):
                    nc.vector.tensor_copy(V[:, t, :], co.PS[:, 4 * (n % 2) + t, :]).then_inc(stored, 1)


@stage
def attend(co, items, score, tiles, value, width, scale, s_banks, out_bank, out_read, extra=None):
    nc = co.nc
    name = co.tag("attend")
    n = len(items)
    nb = len(s_banks)
    with ExitStack() as ctx:
        PR = co.sb(f"{name}_pr", [P, 2, width], ctx=ctx)
        PT = co.sb(f"{name}_pt", [P, 2, width], ctx=ctx)
        ST = co.sb(f"{name}_st", [P, 2, 4], ctx=ctx)
        scored, topped, negated, powered, inverted, normed, turned, copied, weighted, out_hi, out_lo = (
            co.sem(f"{name}_{s}") for s in ("scored", "topped", "negated", "powered", "inverted", "normed", "turned",
                                            "copied", "weighted", "out_hi", "out_lo"))
        block = ctx.enter_context(nc.Block())
        halves_ = [(tiles(x) + 3) // 4 for x in items]
        before = [sum(halves_[:k]) for k in range(n + 1)]

        def sview(k):
            b = s_banks[k % nb]
            return co.PS[:, b:b + (width + 511) // 512, :].rearrange("p b n -> p (b n)")

        def tview(m):
            return co.PS[:, s_banks[-1] + (width + 511) // 512 + m % 2, :]

        @block.tensor
        def _(pe):
            for k in range(n + 2):
                if k < n:
                    if k >= nb:
                        pe.wait_ge(powered, k - nb + 1)
                    score(items[k], sview(k)).then_inc(scored, 1)
                if 1 <= k <= n:
                    x = items[k - 1]
                    pe.wait_ge(normed, k)
                    for m in range(halves_[k - 1]):
                        b = before[k - 1] + m
                        if b >= 2:
                            pe.wait_ge(copied, b - 1)
                        for t in range(4 * m, min(4 * m + 4, tiles(x))):
                            i = nc.tensor.transpose(tview(b)[:, (t % 4) * P:(t % 4 + 1) * P],
                                                    PR[:, (k - 1) % 2, t * P:(t + 1) * P], co.ident)
                        i.then_inc(turned, 1)
                if k >= 2:
                    x = items[k - 2]
                    pe.wait_ge(copied, before[k - 1])
                    bank, part, cs, need = out_bank(x)
                    if need is not None:
                        pe.wait_ge(out_lo, need)
                    for t in range(tiles(x)):
                        i = nc.tensor.matmul(co.PS[part:part + HD, bank, cs], value(x, t),
                                             PT[:, (k - 2) % 2, t * P:(t + 1) * P], start=t == 0, stop=t == tiles(x) - 1)
                    i.then_inc(weighted, 1)

        @block.vector
        def _(dve):
            outs = 0
            for k in range(n + 1):
                if k < n:
                    w = tiles(items[k]) * P
                    dve.wait_ge(scored, k + 1)
                    if k >= 2:
                        dve.wait_ge(powered, k - 1)
                    nc.vector.reduce_max(ST[:, k % 2, 0:1], sview(k)[:, 0:w], axis=AX.X).then_inc(topped, 1)
                    dve.wait_ge(topped, k + 1)
                    nc.vector.tensor_scalar(ST[:, k % 2, 1:2], ST[:, k % 2, 0:1], -scale, None, ALU.mult).then_inc(negated, 1)
                if k >= 1:
                    w = tiles(items[k - 1]) * P
                    b = (k - 1) % 2
                    dve.wait_ge(powered, k)
                    nc.vector.reciprocal(ST[:, b, 3:4], ST[:, b, 2:3]).then_inc(inverted, 1)
                    dve.wait_ge(inverted, k)
                    nc.vector.tensor_scalar(PR[:, b, 0:w], PR[:, b, 0:w], ST[:, b, 3:4], None, ALU.mult).then_inc(normed, 1)
                    if k >= 3 and out_read(k - 3) is not None:
                        hi, lo, src = out_read(k - 3)
                        outs += 1
                        dve.wait_ge(out_hi, outs)
                        nc.vector.tensor_sub(lo, src, hi.bitcast(F32)).then_inc(out_lo, 1)
            for k in range(n - 2, n):
                if out_read(k) is not None:
                    hi, lo, src = out_read(k)
                    outs += 1
                    dve.wait_ge(out_hi, outs)
                    nc.vector.tensor_sub(lo, src, hi.bitcast(F32)).then_inc(out_lo, 1)

        @block.scalar
        def _(act):
            for k in range(n + 2):
                if k < n:
                    w = tiles(items[k]) * P
                    act.wait_ge(negated, k + 1)
                    if k >= 2:
                        act.wait_ge(turned, before[k - 1])
                    nc.scalar.activation(PR[:, k % 2, 0:w], sview(k)[:, 0:w], ACT.Exp, bias=ST[:, k % 2, 1:2],
                                         scale=scale, accum_out=ST[:, k % 2, 2:3]).then_inc(powered, 1)
                if 1 <= k <= n:
                    x = items[k - 1]
                    if k >= 3:
                        act.wait_ge(weighted, k - 2)
                    for m in range(halves_[k - 1]):
                        b = before[k - 1] + m
                        w0, w1 = 512 * m, min(512 * m + 512, tiles(x) * P)
                        act.wait_ge(turned, b + 1)
                        nc.scalar.activation(PT[:, (k - 1) % 2, w0:w1], tview(b)[:, 0:w1 - w0], ACT.Copy).then_inc(copied, 1)
                if k >= 2 and out_read(k - 2) is not None:
                    hi, lo, src = out_read(k - 2)
                    act.wait_ge(weighted, k - 1)
                    nc.scalar.activation(hi, src, ACT.Copy).then_inc(out_hi, 1)

        if extra:
            block.gpsimd(extra)


def plan_odd(co):
    return feed(co, "oin"), feed(co, "oout")


def odd_mixer(co, plan, cols):
    nc = co.nc
    st_in, st_out = plan
    with ExitStack() as ctx:
        QU = co.sb("QU", [P, 16, S], ctx=ctx)
        HK = co.sb("HK", [P, 8, S], ctx=ctx)
        POOLED = co.sb("POOLED", [P, 4, S], ctx=ctx)
        PB = co.sb("PB", [P, 2, S], ctx=ctx)
        PW = co.sb("PW", [P, 4, P], ctx=ctx)
        RC = co.sb("RC", [P, 4, 16], ctx=ctx)
        MR = co.sb("MR", [1, P + 64], ctx=ctx)
        copy_stage(co, st_in, to_buffer(co, QU))
        loaded = co.sem("odd_loaded")
        with nc.Block() as block:
            @block.gpsimd
            def _(pool):
                row = co.dram["hankel"]
                pool.dma_start(HK[:], bass.AP(tensor=row.tensor, offset=0, ap=[[1, P], [row.shape[1], 8], [1, S]])).then_inc(loaded, 16)
                pool.dma_start(PW[:], co.dram["pool_w"].rearrange("g i o -> i g o")).then_inc(loaded, 16)
                pool.dma_start(RC[:], co.dram["counts"].rearrange("p (g t) -> p g t", t=16)).then_inc(loaded, 16)
                pool.dma_start(MR[:], co.dram["counts_mask"]).then_inc(loaded, 16)
                pool.wait_ge(loaded, 64)
        head_norms(co, QU[:, 0:8, :], 8, 4, cols)
        turn_values(co, [(QU[:, 8:12, :], lambda t: slice(t * P, (t + 1) * P))])

        def score(x, ps):
            h, t = x
            c, r = h // 2, HD * (h % 2)
            w = (t + 1) * P
            nc.tensor.matmul(ps[:, 0:w], QU[r:r + HD, c, t * P:(t + 1) * P], QU[r:r + HD, 4 + c, 0:w], start=True, stop=False)
            nc.tensor.matmul(ps[:, 0:w], co.flip, HK[:, h, 384 - P * t:], start=False, stop=False)
            return nc.tensor.matmul(ps[:, w - 64:w], MR[:, 0:P], MR[:, P:], start=False, stop=True)

        pooling = co.sem("pooling")

        def pool_windows(pool):
            g_ = nc.gpsimd
            steps = [0]

            def step(ins):
                steps[0] += 1
                ins.then_inc(pooling, 1)
                pool.wait_ge(pooling, steps[0])
            for g in range(4):
                src = QU[:, 12 + g, :]
                for k in range(g + 1):
                    d = 1 << k
                    dst = POOLED[:, g, :] if (g - k) % 2 == 0 else PB[:, 0, :]
                    step(g_.tensor_copy(dst[:, 0:d], src[:, 0:d]))
                    step(g_.tensor_add(dst[:, d:], src[:, d:], src[:, 0:S - d]))
                    src = dst
                step(g_.tensor_mul(src[:, 0:16], src[:, 0:16], RC[:, g, :]))
                step(g_.tensor_scalar(src[:, 16:], src[:, 16:], 1.0 / (2 << g), None, ALU.mult))
                step(g_.tensor_sub(src, src, QU[:, 12 + g, :]))

        items = [(h, t) for h in range(8) for t in range(TT)]

        def out_read(k):
            if k % 8 != 7:
                return None
            c = k // 8
            return co.Hh[:, c, :], co.Hl[:, c, :], co.PS[:, 4 + c, :]
        attend(co, items, score, lambda x: x[1] + 1, lambda x, t: QU[:, 8 + t, x[0] * HD:(x[0] + 1) * HD], 512, 1.0,
               [0, 1], lambda x: (4 + x[0] // 2, HD * (x[0] % 2), slice(x[1] * P, (x[1] + 1) * P), None), out_read,
               pool_windows)
        with ExitStack() as tmp:
            T = co.sb("pool_t", [P, 4, S], ctx=tmp)
            made, scaled, rounded = co.sem("pool_made"), co.sem("pool_scaled"), co.sem("pool_rounded")
            block = tmp.enter_context(nc.Block())

            @block.tensor
            def _(pe):
                for g in range(4):
                    nc.tensor.matmul(co.PS[:, g, :], PW[:, g, :], POOLED[:, g, :], start=True, stop=True).then_inc(made, 1)

            @block.vector
            def _(dve):
                for g in range(4):
                    dve.wait_ge(made, g + 1)
                    k = cols["pool_scale"] + g
                    nc.vector.tensor_scalar(T[:, g, :], co.PS[:, g, :], co.cols[:, k:k + 1], None, ALU.mult).then_inc(scaled, 1)
                for g in range(4):
                    dve.wait_ge(rounded, g + 1)
                    nc.vector.tensor_sub(co.Hl[:, 4 + g, :], T[:, g, :], co.Hh[:, 4 + g, :].bitcast(F32)).then_inc(scaled, 1)

            @block.scalar
            def _(act):
                for g in range(4):
                    act.wait_ge(scaled, g + 1)
                    nc.scalar.activation(co.Hh[:, 4 + g, :], T[:, g, :], ACT.Copy).then_inc(rounded, 1)
    add_stage(co, st_out)



MW = 4 * S + 2 * P
TAPS = 31
ALPHA = 2 ** 0.25


@stage
def rotate(co, QKV):
    nc = co.nc
    chunks = [12 * g + c for g in range(3) for c in range(8)]
    with ExitStack() as ctx:
        ROPE = co.sb("ROPE", [P, 2, S], ctx=ctx)
        A = co.sb("rope_a", [P, 2, S], ctx=ctx)
        B = co.sb("rope_b", [P, 2, S], ctx=ctx)
        loaded, turned, cosines, sines, done = (co.sem(f"rope_{s}") for s in ("loaded", "turned", "cosines", "sines", "done"))
        block = ctx.enter_context(nc.Block())

        @block.sync
        def _(sp):
            sp.dma_start(ROPE[:], co.dram["rope"].rearrange("p (a s) -> p a s", s=S)).then_inc(loaded, 16)

        @block.tensor
        def _(pe):
            for n, c in enumerate(chunks):
                if n >= 4:
                    pe.wait_ge(sines, n - 3)
                nc.tensor.matmul(co.PS[:, n % 4, :], co.rot, QKV[:, c, :], start=True, stop=True).then_inc(turned, 1)

        @block.gpsimd
        def _(pool):
            pool.wait_ge(loaded, 16)
            for n, c in enumerate(chunks):
                if n >= 2:
                    pool.wait_ge(done, n - 1)
                nc.gpsimd.tensor_mul(A[:, n % 2], QKV[:, c, :], ROPE[:, 0]).then_inc(cosines, 1)

        @block.vector
        def _(dve):
            dve.wait_ge(loaded, 16)

            def add(n):
                dve.wait_ge(cosines, n + 1)
                dve.wait_ge(sines, n + 1)
                nc.vector.tensor_add(QKV[:, chunks[n], :], A[:, n % 2], B[:, n % 2]).then_inc(done, 1)
            for n, c in enumerate(chunks):
                dve.wait_ge(turned, n + 1)
                if n >= 2:
                    dve.wait_ge(done, n - 1)
                nc.vector.tensor_mul(B[:, n % 2], co.PS[:, n % 4, :], ROPE[:, 1]).then_inc(sines, 1)
                if n >= 1:
                    add(n - 1)
            add(len(chunks) - 1)


def plan_hybrid(co):
    st = {n: feed(co, n) for n in ("hin_qkv", "hin_b", "hin_a", "hin_gate")}
    w = co.dram["hao"]
    st["hao"] = co.plan(Stage(w.shape[0] // RAW, [
        Unit(4, lambda i, j=j: w[bass.ds(RAW * i + j, 1)].rearrange("o p n -> p (o n)"), None, 0, j) for j in range(RAW)
    ], 2, 2))
    st["ho"] = feed(co, "ho")
    return st


@stage
def gates_and_conv(co, st, GT, U, CV, cols):
    nc = co.nc
    bank_free, tapped = co.sem("gates_bank_free"), co.sem("conv_tapped")
    with nc.Block() as block:
        @block.sync
        def _(sp):
            co.load(sp, st)

        @block.tensor
        def _(pe):
            co.multiply(pe, st, bank_free)

        @block.scalar
        def _(act):
            act.sem_inc(bank_free, 4)

            def read(i, c):
                co.wait_units(act, st, i, c)
                nc.scalar.activation(one(GT, RAW * i + c), one(co.PS, c), ACT.Sigmoid).then_inc(bank_free, 1)
            co.run(act, st, co.split_hi, read)

        @block.vector
        def _(dve):
            def read(i, c):
                for tap in range(8 * c, min(8 * c + 8, TAPS)):
                    w = co.cols[:, bass.ds(cols["conv2_w"] + TAPS * i + TAPS - 1 - tap, 1)]
                    u, o = one(U, i), one(CV, i)
                    if tap == 0:
                        nc.vector.tensor_scalar(o, u, w, co.cols[:, bass.ds(cols["conv2_b"] + i, 1)],
                                                ALU.mult, ALU.add).then_inc(tapped, 1)
                    else:
                        dve.wait_ge(tapped, TAPS * i + tap)
                        nc.vector.scalar_tensor_tensor(o[:, :, tap:], u[:, :, 0:S - tap], w, o[:, :, tap:],
                                                       ALU.mult, ALU.add).then_inc(tapped, 1)
            co.run(dve, st, co.split_lo, read)


@stage
def silu_split(co, CV, C2):
    nc = co.nc
    act_done, rounded, done = co.sem("silu_done"), co.sem("silu_rounded"), co.sem("silu_split")
    with nc.Block() as block:
        @block.scalar
        def _(act):
            for c in range(4):
                nc.scalar.activation(CV[:, c, :], CV[:, c, :], ACT.Silu).then_inc(act_done, 1)
            for c in range(4):
                act.wait_ge(act_done, c + 1)
                nc.scalar.activation(C2[0][:, c, :], CV[:, c, :], ACT.Copy).then_inc(rounded, 1)

        @block.vector
        def _(dve):
            for c in range(4):
                dve.wait_ge(rounded, c + 1)
                nc.vector.tensor_sub(C2[1][:, c, :], CV[:, c, :], C2[0][:, c, :].bitcast(F32)).then_inc(done, 1)


@stage
def merge(co, st, GT):
    nc = co.nc
    with ExitStack() as ctx:
        A = co.sb("merge_a", [P, 2, 1, S], ctx=ctx)
        B = co.sb("merge_b", [P, 2, 1, S], ctx=ctx)
        banks_free, first, added, rounded, done = (
            co.sem(f"merge_{s}") for s in ("banks_free", "first", "added", "rounded", "done"))
        block = ctx.enter_context(nc.Block())

        @block.sync
        def _(sp):
            co.load(sp, st)

        @block.tensor
        def _(pe):
            co.multiply(pe, st, banks_free)

        @block.scalar
        def _(act):
            def read(i, c):
                act.wait_ge(added, 2 * i + c + 1)
                nc.scalar.activation(one(co.Hh, 2 * i + c), A[:, c], ACT.Copy).then_inc(rounded, 1)
            co.run(act, st, co.split_hi, read)

        @block.vector
        def _(dve):
            dve.sem_inc(banks_free, 2)

            def read(i, c):
                co.wait_units(dve, st, i, c)
                nc.vector.tensor_mul(A[:, c], one(co.PS, 2 * c), one(GT, 2 * i + c)).then_inc(first, 1)
                nc.vector.tensor_mul(B[:, c], one(co.PS, 2 * c + 1), one(GT, 8 + 2 * i + c)).then_inc(banks_free, 1)
                dve.wait_ge(banks_free, 2 + 2 * i + c + 1)
                nc.vector.tensor_add(A[:, c], A[:, c], B[:, c]).then_inc(added, 1)
                dve.wait_ge(rounded, 2 * i + c + 1)
                nc.vector.tensor_sub(one(co.Hl, 2 * i + c), A[:, c], one(co.Hh, 2 * i + c).bitcast(F32)).then_inc(done, 1)
            co.run(dve, st, co.split_lo, read)


def split_x(co):
    split_stage(co, [(co.X[:, c, :], co.Hh[:, c, :], co.Hl[:, c, :]) for c in range(DC)])


def hybrid_mixer(co, st, cols):
    nc = co.nc
    split_x(co)
    with ExitStack() as ctx:
        OH = co.sb("OH", [P, 4, S], F32R, ctx)
        OL = co.sb("OL", [P, 4, S], F32R, ctx)
        with ExitStack() as inner:
            QKV = co.sb("QKV", [P, 36, S], ctx=inner)
            MK = co.sb("MK", [P, MW], BF16, inner)
            IB = co.sb("IB", [P, P], BF16, inner)
            copy_stage(co, st["hin_qkv"], to_buffer(co, QKV))
            rotate(co, QKV)
            loaded, cast = co.sem("mask_loaded"), co.sem("ident_cast")
            with nc.Block() as block:
                @block.sync
                def _(sp):
                    sp.dma_start(MK[:].bitcast(mybir.dt.uint16), co.dram["mask"]).then_inc(loaded, 16)
                    sp.wait_ge(loaded, 16)

                @block.vector
                def _(dve):
                    nc.vector.tensor_copy(IB[:], co.ident).then_inc(cast, 1)
            every4 = lambda t: slice(t, None, 4)
            turn_values(co, [(QKV[:, 8:12, :], lambda t: slice(t * P, (t + 1) * P)), (QKV[:, 20:24, :], every4),
                             (QKV[:, 32:36, :], every4)])

            def score(x, ps):
                h, r = x
                c, p = h // 2, HD * (h % 2)
                q = lambda g: QKV[p:p + HD, 12 * g + c, r::4]
                k = lambda g: QKV[p:p + HD, 12 * g + 4 + c, :]
                mm = nc.tensor.matmul
                mm(ps[:, 0:S], q(0), k(0), start=True, stop=False)
                mm(ps[:, 0:S], IB[:], MK[:, r * S:(r + 1) * S], start=False, stop=True)
                mm(ps[:, S:S + P], q(1), k(1)[:, r::4], start=True, stop=False)
                mm(ps[:, S:S + P], IB[:], MK[:, 4 * S:4 * S + P], start=False, stop=True)
                mm(ps[:, S + P:S + 2 * P], q(2), k(2)[:, r::4], start=True, stop=False)
                return mm(ps[:, S + P:S + 2 * P], IB[:], MK[:, 4 * S + P:4 * S + 2 * P], start=False, stop=True)

            def value(x, t):
                h, r = x
                cs = slice(h * HD, (h + 1) * HD)
                return QKV[:, 8 + t, cs] if t < 4 else QKV[:, 20 + r if t == 4 else 32 + r, cs]

            def out_read(k):
                if k % 8 != 7:
                    return None
                c = k // 8
                back = lambda t: t[:, c, :].rearrange("p (q r) -> p r q", r=4)
                return back(OH), back(OL), co.PS[:, 6 + c % 2, :].rearrange("p (r q) -> p r q", r=4)
            attend(co, [(h, r) for h in range(8) for r in range(4)], score, lambda x: 6, value, 768, HD ** -0.5,
                   [0, 2], lambda x: (6 + x[0] // 2 % 2, HD * (x[0] % 2), slice(x[1] * P, (x[1] + 1) * P),
                                      x[0] // 2 - 1 if x[0] >= 4 and x[0] % 2 == 0 and x[1] == 0 else None), out_read)
        GT = co.sb("GT", [P, 16, S], ctx=ctx)
        CH = co.sb("CH", [P, 4, S], F32R, ctx)
        CL = co.sb("CL", [P, 4, S], F32R, ctx)
        with ExitStack() as inner:
            U = co.sb("conv_u", [P, 4, S], ctx=inner)
            CV = co.sb("conv_v", [P, 4, S], ctx=inner)
            copy_stage(co, st["hin_b"], to_buffer(co, CV, ACT.Sigmoid))
            copy_stage(co, st["hin_a"], lambda i, c: ("dve", lambda ps: nc.vector.tensor_mul(one(U, c), ps, one(CV, c))))
            gates_and_conv(co, st["hin_gate"], GT, U, CV, cols)
            norm_stage(co, 4, cols["conv2_g"], CV, LN_EPS, center=True, bias=cols["conv2_lb"], src=CV)
            silu_split(co, CV, (CH, CL))
        for j, u in enumerate(st["hao"].units):
            u.x = (OH, OL) if j % 2 == 0 else (CH, CL)
        merge(co, st["hao"], GT)
    add_stage(co, st["ho"], ALPHA)
    norm_stage(co, DC, cols["ln1_g"], co.X, LN_EPS, center=True, bias=cols["ln1_b"])

def start(co):
    nc, d = co.nc, co.dram
    loaded, set_up = co.sem("loaded"), co.sem("set_up")
    with nc.Block() as block:
        @block.sync
        def _(sp):
            sp.dma_start(co.X[:], d["xT"].rearrange("(c p) s -> p c s", p=P)).then_inc(loaded, 16)
            sp.dma_start(co.cols[:], d["cols"]).then_inc(loaded, 16)
            co.load_turn(sp, co.stages[0], 0)
            sp.dma_start(co.mats[:], d["mats"].rearrange("p (k n) -> p k n", n=P)).then_inc(loaded, 16)
            sp.wait_ge(loaded, 48)

        @block.gpsimd
        def _(pool):
            nc.gpsimd.memset(co.ones[:], 1.0).then_inc(set_up, 1)

        @block.tensor
        def _(pe):
            pe.sem_inc(co.unit_done, SPLIT)


def finish(co):
    nc, d = co.nc, co.dram
    stored = co.sem("stored")
    with nc.Block() as block:
        @block.sync
        def _(sp):
            sp.dma_start(d["out"].rearrange("(c p) s -> p c s", p=P), co.X[:]).then_inc(stored, 16)
            sp.wait_ge(stored, 16)


def program(nc, dram, cols):
    with ExitStack() as ctx:
        main(Core(nc, ctx, dram), cols)


def main(co, cols):
    first = plan_ffn(co, 0)
    even = plan_even(co)
    second = plan_ffn(co, 1)
    third = plan_ffn(co, 2)
    odd = plan_odd(co)
    fourth = plan_ffn(co, 3)
    hybrid = plan_hybrid(co)
    last = plan_ffn(co, 4)
    h = (co.Hh, co.Hl, 0)
    start(co)
    norm_stage(co, DC, cols["ffn1_norm0"], h, EPS)
    ffn(co, *first, 0.5)
    norm_stage(co, DC, cols["mix_norm0"], h, EPS)
    even_mixer(co, even, cols)
    norm_stage(co, DC, cols["ffn2_norm0"], h, EPS)
    ffn(co, *second, 0.5)
    norm_stage(co, DC, cols["ffn1_norm1"], h, EPS)
    ffn(co, *third, 0.5)
    norm_stage(co, DC, cols["mix_norm1"], h, EPS)
    odd_mixer(co, odd, cols)
    norm_stage(co, DC, cols["ffn2_norm1"], h, EPS)
    ffn(co, *fourth, 0.5)
    hybrid_mixer(co, hybrid, cols)
    split_x(co)
    ffn(co, *last, 1.0, ALPHA)
    norm_stage(co, DC, cols["ln2_g"], co.X, LN_EPS, center=True, bias=cols["ln2_b"])
    finish(co)


def blocked(w):
    k, n = w.shape
    return np.ascontiguousarray(w.reshape(k // P, P, n // P, P).transpose(2, 1, 0, 3).reshape(n // P, P, k))


def halves(w):
    b = blocked(w)
    return np.ascontiguousarray(b.reshape(b.shape[0], P, 2, HALF * P).transpose(0, 2, 1, 3).reshape(-1, P, HALF * P))


def pair(a, b):
    a, b = blocked(a), blocked(b)
    return np.ascontiguousarray(np.stack([a, b], 1).reshape(-1, *a.shape[1:]))


def constants():
    f = np.float32
    p, q = np.arange(P)[:, None], np.arange(P)[None, :]
    rot = np.zeros((P, P), f)
    for m in range(P):
        rot[m + 32 if m % 64 < 32 else m - 32, m] = -1 if m % 64 < 32 else 1
    mats = np.concatenate([p == q, q >= p, p + q == P - 1, rot, p // 64 == q // 64], 1).astype(f)
    sel8 = (np.arange(8)[:, None] == np.arange(8 * P)[None, :] // P).astype(f)
    tokens = np.concatenate([np.arange(32), 32 * np.arange(16)]).astype(f)
    small = {
        "sign": np.where(p < 64, 1, -1).astype(f), "half_pi": np.full((P, 1), np.pi / 2, f),
        "tokens": np.tile(tokens, (P, 1)), "pair": (p // 16 % 2 == np.arange(2)[None]).astype(f),
    }
    return mats, sel8, small


def lay_out(v):
    a, cols, parts = {}, {}, []

    def col(name, m):
        cols[name] = sum(x.shape[1] for x in parts)
        parts.append(np.asarray(m))

    def vec(name, x):
        col(name, np.reshape(x, (-1, P)).T)

    def rows8(name, x):
        col(name, np.concatenate([np.reshape(x, (-1, 1)), np.zeros((P - 8, 1), np.float32)]))

    ffns = [("ffn1", "", 0), ("ffn2", "", 0), ("ffn1", "", 1), ("ffn2", "", 1)]
    for n, (f, _, l) in enumerate(ffns):
        a[f"gu{n}"] = pair(v[f + "_w_gate"][l], v[f + "_w_up"][l])
        a[f"dn{n}"] = halves(v[f + "_w_down"][l])
    a["gu4"] = pair(v["w_ffn_gate_2"][0], v["w_ffn_up_2"][0])
    a["dn4"] = halves(v["w_ffn_down_2"][0])
    for l in range(2):
        for f in ("ffn1_norm", "mix_norm", "ffn2_norm"):
            vec(f"{f}{l}", v[f][l])
    w = v["even_w_in"][0]
    a["ein_zx"] = blocked(w[:, 0:1536])
    dt = np.concatenate([w[:, 1536:1544], np.zeros((D, P - 8), np.float32)], 1)
    a["ein_dt"] = np.ascontiguousarray(blocked(dt).reshape(P, RAW, 2 * P).transpose(1, 0, 2))
    a["ein_u"] = blocked(w[:, 1544:])
    a["glu"] = blocked(v["s5_w_glu"][0])
    a["eout"] = blocked(v["even_w_out"][0])
    vec("conv_w", v["ssd_conv_w"][0])
    vec("conv_b", v["ssd_conv_b"][0])
    rows8("dt_bias", v["ssd_dt_bias"][0])
    rows8("a_log", v["ssd_a_log"][0])
    vec("ssd_d", np.repeat(v["ssd_d"][0], HD))
    vec("ssd_norm", v["ssd_norm"][0])
    vec("s5_d", v["s5_d"][0])
    vec("b_glu", v["s5_b_glu"][0])
    twice = lambda x: np.concatenate([x, x], 0)
    a["s5p"] = np.concatenate([twice(v["s5_a_re"][0].T), twice(v["s5_a_im"][0].T),
                               np.tile(v["s5_log_dt"][0][None], (P, 1))], 1)
    br, bi = (v[n][0].transpose(1, 0, 2).reshape(64, -1) for n in ("s5_b_re", "s5_b_im"))
    cr, ci = (v[n][0].transpose(2, 0, 1).reshape(64, -1) for n in ("s5_c_re", "s5_c_im"))
    a["s5b"] = np.concatenate([np.concatenate([br, bi], 0), np.concatenate([bi, br], 0)], 1)
    a["s5c"] = np.concatenate([np.concatenate([cr, ci], 0), np.concatenate([ci, cr], 0)], 1)
    a["oin"] = blocked(v["odd_w_in"][0])
    a["oout"] = blocked(v["odd_w_out"][0])
    b = v["attn_rel_bias"][0]
    a["hankel"] = np.concatenate([np.repeat(b[:, 256:], 383, 1), b[:, :0:-1], b[:, :1]], 1)
    a["pool_w"] = v["pool_w"][0]
    vec("q_gain", np.tile(v["attn_q_norm"][0], 2))
    vec("k_gain", np.tile(v["attn_k_norm"][0], 2))
    vec("pool_scale", v["pool_scale"][0])
    frames = 1 / np.minimum(np.arange(1, 17)[None], np.array([2, 4, 8, 16])[:, None]).astype(np.float32)
    a["counts"] = np.tile(frames.reshape(1, -1), (P, 1))
    a["hankel_sel"] = (np.arange(16)[:, None] == np.arange(8 * P)[None, :] // HD).astype(np.float32)
    a["counts_mask"] = np.concatenate([np.where(np.arange(P) < 64, NEG, 0), np.ones(64)]).astype(np.float32)[None]
    w = v["w_in_2"][0]
    q = 9 * S
    a["hin_qkv"] = blocked(w[:, 0:q])
    a["hin_a"], a["hin_b"] = blocked(w[:, q:q + S]), blocked(w[:, q + S:q + 2 * S])
    a["hin_gate"] = blocked(w[:, q + 2 * S:])
    a["hao"] = pair(v["w_attn_out_2"][0], v["w_conv_out_2"][0])
    a["ho"] = blocked(v["w_o_2"][0])
    col("conv2_w", v["conv_w_2"][0].reshape(TAPS, 4, P).transpose(2, 1, 0).reshape(P, -1))
    for n, x in (("conv2_b", "conv_b_2"), ("conv2_g", "conv_ln_g_2"), ("conv2_lb", "conv_ln_b_2"), ("ln1_g", "ln1_g_2"),
                 ("ln1_b", "ln1_b_2"), ("ln2_g", "ln2_g_2"), ("ln2_b", "ln2_b_2")):
        vec(n, v[x][0])
    f = np.float32
    inv = (1.0 / (f(10000.0) ** (np.arange(0, HD, 2, dtype=f) / f(HD)))).astype(f)
    ang = np.arange(S, dtype=f)[None] * np.tile(inv, 4)[:, None]
    a["rope"] = np.concatenate([np.cos(ang), np.sin(ang)], 1).astype(f)
    at = np.arange(P)[:, None]
    near = [(4 * at + r - np.arange(S)[None] >= 0) & (4 * at + r - np.arange(S)[None] <= P) for r in range(4)]
    back = at - at.T
    ok = np.concatenate(near + [back >= 0, (back >= 0) & (back % 4 == 0)], 1)
    a["mask"] = (np.where(ok, 0, NEG).astype(f).view(np.uint32) >> 16).astype(np.uint16)
    mats, a["sel8"], small = constants()
    a["mats"] = mats
    for n, x in small.items():
        col(n, x)
    a["cols"] = np.concatenate(parts, 1)
    a["xT"] = v["x"][0].T
    return {n: np.ascontiguousarray(x) for n, x in a.items()}, cols


def kernel(**inputs):
    import concourse.bacc as _bacc
    from concourse.bass_utils import run_bass_kernel_spmd as _run

    v = {k: np.asarray(x) for k, x in inputs.items()}
    arrays, cols = lay_out(v)
    nc = _bacc.Bacc("TRN2", target_bir_lowering=False, num_devices=1)
    dram = {n: nc.dram_tensor("in_" + n, a.shape, mybir.dt.from_np(a.dtype), kind="ExternalInput").ap()
            for n, a in arrays.items()}
    dram["out"] = nc.dram_tensor("out_xT", (D, S), F32, kind="ExternalOutput").ap()
    program(nc, dram, cols)
    r = _run(nc, [{"in_" + n: a for n, a in arrays.items()}], core_ids=[0])
    return np.ascontiguousarray(r.results[0]["out_xT"].T).reshape(1, S, D)
```

```python
from contextlib import ExitStack

import numpy as np

import concourse.bass as bass
from concourse import mybir

F32 = mybir.dt.float32
F32R = mybir.dt.float32r
BF16 = mybir.dt.bfloat16
ALU = mybir.AluOpType
ACT = mybir.ActivationFunctionType
AX = mybir.AxisListType

P = 128
S = 512
D = 1024
DC = D // P
FF = 2816
FC = FF // P
HALF = FC // 2
EPS = 1e-6
LN_EPS = 1e-5
RAW = 4
SPLIT = 2
TT = S // P
HD = 64
NEG = -1e30
MAGIC = 1.5 * 2.0 ** 23
S5G = 32


class Unit:

    def __init__(self, kc, src, x, k0, bank, start=True, stop=True):
        self.kc, self.src, self.x, self.k0 = kc, src, x, k0
        self.bank, self.start, self.stop = bank, start, stop


class Stage:

    def __init__(self, bodies, units, chunks, banks):
        self.bodies, self.units, self.chunks, self.banks = bodies, units, chunks, banks
        self.base = None


class StageSems(ExitStack):

    def __init__(self):
        super().__init__()
        self.handles = []

    def enter_context(self, made):
        self.handles.append(super().enter_context(made))
        return self.handles[-1]


def stage(f):
    def run(co, *args, **kwargs):
        co.begin()
        f(co, *args, **kwargs)
        co.end()
    return run


class Core:

    def __init__(self, nc, ctx, dram):
        self.nc, self.ctx, self.dram = nc, ctx, dram
        self.n = 0
        self.stage_sems, self.retired, self.clearing = None, [], []
        self.X = self.sb("X", [P, DC, S])
        self.Hh = self.sb("Hh", [P, DC, S], F32R)
        self.Hl = self.sb("Hl", [P, DC, S], F32R)
        self.raw = [self.sb(f"raw{j}", [P, HALF * P]) for j in range(RAW)]
        self.wh = [self.sb(f"wh{j}", [P, HALF * P], F32R) for j in range(SPLIT)]
        self.wl = [self.sb(f"wl{j}", [P, HALF * P], F32R) for j in range(SPLIT)]
        self.RS = self.sb("RS", [P, S])
        self.SS = self.sb("SS", [P, S])
        self.ones = self.sb("ones", [P, P])
        self.cols = self.sb("cols", [P, dram["cols"].shape[1]])
        self.mats = self.sb("mats", [P, 5, P])
        self.ident, self.triu, self.flip, self.rot, self.heads = (self.mats[:, k, :] for k in range(5))
        self.PS = ctx.enter_context(nc.psum_tensor("PS", [P, 8, 512], F32))
        self.raw_in = [self.sem(f"raw_in{j}") for j in range(RAW)]
        self.hi_ready = self.sem("hi_ready")
        self.lo_ready = self.sem("lo_ready")
        self.unit_done = self.sem("unit_done")
        self.stages = []

    def sb(self, name, shape, dt=F32, ctx=None):
        return (ctx or self.ctx).enter_context(self.nc.sbuf_tensor(name, shape, dt))

    def sem(self, name):
        return (self.stage_sems or self.ctx).enter_context(self.nc.semaphore(self.tag(name)))

    def begin(self):
        for done in self.clearing:
            done.close()
        self.clearing = self.retired
        self.retired = []
        for done in self.clearing:
            for s in done.handles:
                self.nc.gpsimd.sem_clear(s)
        self.stage_sems = StageSems()

    def end(self):
        self.retired.append(self.stage_sems)
        self.stage_sems = None

    def tag(self, name):
        self.n += 1
        return f"{name}_{self.n}"

    def plan(self, stage):
        stage.base = self.stages[-1].base + RAW * self.stages[-1].bodies if self.stages else 0
        self.stages.append(stage)
        return stage

    def load_turn(self, sp, st, i):
        for j, u in enumerate(st.units):
            at = st.base + RAW * i + j
            if not (isinstance(at, int) and at < RAW):
                sp.wait_ge(self.lo_ready, at + 1 - RAW)
            sp.dma_start(self.raw[j][:, 0:u.kc * P], u.src(i)).then_inc(self.raw_in[j], 16)

    def load(self, sp, st):
        if st.bodies > 1:
            with sp.Fori(1, st.bodies) as i:
                self.load_turn(sp, st, i)
        k = self.stages.index(st)
        if k + 1 < len(self.stages):
            self.load_turn(sp, self.stages[k + 1], 0)

    def split_hi(self, act, st, i, j):
        kw = st.units[j].kc * P
        act.wait_ge(self.raw_in[j], 16 * (st.base // RAW + 1) + 16 * i)
        act.wait_ge(self.unit_done, st.base + j + 1 + RAW * i)
        self.nc.scalar.activation(self.wh[j % SPLIT][:, 0:kw], self.raw[j][:, 0:kw], ACT.Copy).then_inc(self.hi_ready, 1)

    def split_lo(self, dve, st, i, j):
        kw = st.units[j].kc * P
        dve.wait_ge(self.hi_ready, st.base + j + 1 + RAW * i)
        self.nc.vector.tensor_sub(self.wl[j % SPLIT][:, 0:kw], self.raw[j][:, 0:kw],
                                  self.wh[j % SPLIT][:, 0:kw].bitcast(F32)).then_inc(self.lo_ready, 1)

    def multiply(self, pe, st, bank_free, operand=None):
        per = RAW // st.chunks

        def turn(i):
            for j, u in enumerate(st.units):
                if j % per == 0:
                    pe.wait_ge(bank_free, st.chunks * i + j // per + 1)
                pe.wait_ge(self.lo_ready, st.base + j + 1 + RAW * i)
                if operand:
                    pe.wait_ge(operand[0], operand[1][j])
                xh, xl = u.x
                out = self.PS[:, u.bank, :]
                for k in range(u.kc):
                    wh = self.wh[j % SPLIT][:, k * P:(k + 1) * P]
                    wl = self.wl[j % SPLIT][:, k * P:(k + 1) * P]
                    first, last = u.start and k == 0, u.stop and k == u.kc - 1
                    self.nc.tensor.matmul(out, wl, xh[:, u.k0 + k, :], start=first, stop=False)
                    self.nc.tensor.matmul(out, wh, xh[:, u.k0 + k, :], start=False, stop=False)
                    done = self.nc.tensor.matmul(out, wh, xl[:, u.k0 + k, :], start=False, stop=last)
                done.then_inc(self.unit_done, 1)
        if st.bodies > 1:
            with pe.Fori(0, st.bodies) as i:
                turn(i)
        else:
            turn(0)

    def wait_units(self, eng, st, i, c, part=None):
        per = RAW // st.chunks
        j = c * per + (per - 1 if part is None else part)
        eng.wait_ge(self.unit_done, SPLIT + st.base + j + 1 + RAW * i)

    def run(self, eng, st, split, read, early=None):
        per = RAW // st.chunks

        def turn(i, first):
            for c in range(st.chunks):
                for j in range(c * per, (c + 1) * per):
                    if not (first and j < SPLIT):
                        split(eng, st, i, j)
                if c > 0:
                    read(i, c - 1)
                elif not first:
                    read(i - 1, st.chunks - 1)
                elif early:
                    early()
        turn(0, True)
        if st.bodies > 1:
            with eng.Fori(1, st.bodies) as i:
                turn(i, False)
        k = self.stages.index(st)
        if k + 1 < len(self.stages):
            for j in range(SPLIT):
                split(eng, self.stages[k + 1], 0, j)
        read(st.bodies - 1, st.chunks - 1)


def one(t, n, k=None):
    return t[:, bass.ds(n, 1), :]



@stage
def norm_stage(co, n, gain, out, eps, center=False, bias=None, src=None, block_ones=None, width=None):
    nc = co.nc
    src = co.X if src is None else src
    name = co.tag("norm")
    width = width or n * P
    with ExitStack() as ctx:
        SQ = co.sb(f"{name}_sq", [P, n, S], ctx=ctx)
        RS = co.sb(f"{name}_rs", [P, S], ctx=ctx)
        T = co.sb(f"{name}_t", [P, 2, S], ctx=ctx)
        squared = co.sem(f"{name}_squared")
        summed = co.sem(f"{name}_summed")
        rooted = co.sem(f"{name}_rooted")
        scaled = co.sem(f"{name}_scaled")
        mean_summed = co.sem(f"{name}_mean_summed")
        mean_ready = co.sem(f"{name}_mean_ready")
        centered = co.sem(f"{name}_centered")
        normed = co.sem(f"{name}_normed")
        rounded = co.sem(f"{name}_rounded")
        split = isinstance(out, tuple)
        block = ctx.enter_context(nc.Block())

        @block.tensor
        def _(pe):
            if center:
                for c in range(n):
                    m = nc.tensor.matmul(co.PS[:, 1, :], co.ones[:], src[:, c, :], start=c == 0, stop=c == n - 1)
                m.then_inc(mean_summed, 1)
            for c in range(n):
                pe.wait_ge(squared, c + 1)
                m = nc.tensor.matmul(co.PS[:, 0, :], co.ones[:], SQ[:, c, :], start=c == 0, stop=c == n - 1)
            m.then_inc(summed, 1)

        @block.scalar
        def _(act):
            for c in range(n):
                if center:
                    act.wait_ge(centered, c + 1)
                nc.scalar.activation(SQ[:, c, :], src[:, c, :], ACT.Square).then_inc(squared, 1)
            act.wait_ge(scaled, 1)
            nc.scalar.activation(RS[:], RS[:], ACT.Sqrt).then_inc(rooted, 1)
            if split:
                for c in range(n):
                    act.wait_ge(normed, c + 1)
                    nc.scalar.activation(out[0][:, out[2] + c, :], T[:, c % 2, :], ACT.Copy).then_inc(rounded, 1)

        @block.vector
        def _(dve):
            if center:
                dve.wait_ge(mean_summed, 1)
                nc.vector.tensor_scalar(T[:, 0, :], co.PS[:, 1, :], 1.0 / width, None, ALU.mult).then_inc(mean_ready, 1)
                dve.wait_ge(mean_ready, 1)
                for c in range(n):
                    nc.vector.tensor_sub(src[:, c, :], src[:, c, :], T[:, 0, :]).then_inc(centered, 1)
            dve.wait_ge(summed, 1)
            nc.vector.tensor_scalar(RS[:], co.PS[:, 0, :], 1.0 / width, eps, ALU.mult, ALU.add).then_inc(scaled, 1)
            dve.wait_ge(rooted, 1)
            nc.vector.reciprocal(RS[:], RS[:]).then_inc(scaled, 1)
            dve.wait_ge(scaled, 2)
            if center:
                dve.wait_ge(centered, n)
            for c in range(n):
                if split and c >= 2:
                    dve.wait_ge(rounded, c - 1)
                to = T[:, c % 2, :] if split or bias is not None else out[:, c, :]
                nc.vector.scalar_tensor_tensor(to, src[:, c, :], co.cols[:, gain + c:gain + c + 1], RS[:],
                                               ALU.mult, ALU.mult).then_inc(normed, 1)
                if bias is not None:
                    dve.wait_ge(normed, c + 1)
                    nc.vector.tensor_scalar(out[:, c, :], T[:, c % 2, :], co.cols[:, bias + c:bias + c + 1], None,
                                            ALU.add).then_inc(centered, 1)
                if split:
                    dve.wait_ge(rounded, c + 1)
                    nc.vector.tensor_sub(out[1][:, out[2] + c, :], T[:, c % 2, :],
                                         out[0][:, out[2] + c, :].bitcast(F32)).then_inc(centered, 1)


@stage
def split_stage(co, pairs):
    nc = co.nc
    name = co.tag("split")
    rounded, done = co.sem(f"{name}_rounded"), co.sem(f"{name}_done")
    with nc.Block() as block:
        @block.scalar
        def _(act):
            for src, hi, lo in pairs:
                nc.scalar.activation(hi, src, ACT.Copy).then_inc(rounded, 1)

        @block.vector
        def _(dve):
            for n, (src, hi, lo) in enumerate(pairs):
                dve.wait_ge(rounded, n + 1)
                nc.vector.tensor_sub(lo, src, hi.bitcast(F32)).then_inc(done, 1)



def feed(co, name, x=None):
    w = co.dram[name]
    x = x or (co.Hh, co.Hl)
    kc = w.shape[2] // P
    return co.plan(Stage(w.shape[0] // RAW, [
        Unit(kc, lambda i, j=j: w[bass.ds(RAW * i + j, 1)].rearrange("o p n -> p (o n)"), x, 0, j) for j in range(RAW)
    ], RAW, 4))


@stage
def copy_stage(co, st, reads, scaled=False):
    nc = co.nc
    name = co.tag("copy")
    bank_free = co.sem(f"{name}_bank_free")
    scale = Scale(co) if scaled else None
    with nc.Block() as block:
        @block.sync
        def _(sp):
            co.load(sp, st)

        @block.tensor
        def _(pe):
            if scaled:
                scale.pe(pe)
            co.multiply(pe, st, bank_free)

        @block.scalar
        def _(act):
            act.sem_inc(bank_free, 4)

            def read(i, c):
                if reads and reads(i, c)[0] == "act":
                    co.wait_units(act, st, i, c)
                    reads(i, c)[1](one(co.PS, c)).then_inc(bank_free, 1)
            co.run(act, st, co.split_hi, read, (lambda: scale.act(act)) if scaled else None)

        @block.vector
        def _(dve):
            def read(i, c):
                if reads and reads(i, c)[0] == "dve":
                    co.wait_units(dve, st, i, c)
                    reads(i, c)[1](one(co.PS, c)).then_inc(bank_free, 1)
            co.run(dve, st, co.split_lo, read, (lambda: scale.dve(dve)) if scaled else None)


def plan_ffn(co, k):
    gu, dn = co.dram[f"gu{k}"], co.dram[f"dn{k}"]
    x = (co.Hh, co.Hl)
    up = co.plan(Stage(FC // 2, [
        Unit(DC, lambda i, j=j: gu[bass.ds(RAW * i + j, 1)].rearrange("o p n -> p (o n)"), x, 0, j) for j in range(RAW)
    ], 2, 2))
    down = co.plan(Stage(DC // 2, [
        Unit(HALF, lambda i, j=j: dn[bass.ds(RAW * i + j, 1)].rearrange("o p n -> p (o n)"), None, HALF * (j % 2),
             4 + j // 2, j % 2 == 0, j % 2 == 1) for j in range(RAW)
    ], 2, 2))
    return up, down


class Residual:

    def __init__(self, co, ctx, st, banks, alpha, beta, gain, T=None, SQ=None, split=True):
        name = co.tag("res")
        self.co, self.st, self.banks, self.alpha, self.beta, self.gain, self.split = co, st, banks, alpha, beta, gain, split
        self.T = T or co.sb(f"{name}_t", [P, 2, 1, S], ctx=ctx)
        self.SQ = SQ or co.sb(f"{name}_sq", [P, 2, 1, S], ctx=ctx)
        self.bank_free, self.updated, self.gained, self.rounded, self.squared, self.added, self.parted = (
            co.sem(f"{name}_{s}") for s in ("bank_free", "updated", "gained", "rounded", "squared", "added", "parted"))

    def dve(self, dve, i, c):
        co, v = self.co, self.co.nc.vector
        n = self.st.chunks * i + c
        co.wait_units(dve, self.st, i, c)
        x, ps = one(co.X, n), one(co.PS, self.banks + c)
        a, b = (x, ps) if self.beta == 1.0 else (ps, x)
        v.scalar_tensor_tensor(x, a, self.alpha * self.beta, b, ALU.mult, ALU.add).then_inc(self.bank_free, 1)
        if self.split:
            dve.wait_ge(self.bank_free, self.st.banks + n + 1)
            if self.gain is None:
                t = x
            else:
                t = self.T[:, c % 2]
                v.tensor_scalar(t, x, co.cols[:, bass.ds(self.gain + n, 1)], None, ALU.mult).then_inc(self.gained, 1)
            dve.wait_ge(self.rounded, n + 1)
            v.tensor_sub(one(co.Hl, n), t, one(co.Hh, n).bitcast(F32)).then_inc(self.parted, 1)

    def act(self, act, i, c):
        co = self.co
        n = self.st.chunks * i + c
        if self.split:
            if self.gain is None:
                act.wait_ge(self.bank_free, self.st.banks + n + 1)
            else:
                act.wait_ge(self.gained, n + 1)
            t = one(co.X, n) if self.gain is None else self.T[:, c % 2]
            co.nc.scalar.activation(one(co.Hh, n), t, ACT.Copy).then_inc(self.rounded, 1)
        if self.gain is not None:
            act.wait_ge(self.added, n + 1)
            co.nc.scalar.activation(self.SQ[:, c % 2], one(co.X, n), ACT.Square).then_inc(self.squared, 1)

    def pool(self, pool):
        co = self.co
        if self.gain is None:
            return
        pool.sem_inc(self.added, 1)
        co.nc.gpsimd.memset(co.SS[:], 0.0).then_inc(self.added, 1)
        st = self.st

        def turn(i):
            for c in range(st.chunks):
                n = st.chunks * i + c
                pool.wait_ge(self.squared, n + 1)
                pool.wait_ge(self.added, n + 2)
                co.nc.gpsimd.tensor_add(co.SS[:].unsqueeze(1), co.SS[:].unsqueeze(1), self.SQ[:, c % 2]).then_inc(self.added, 1)
        with pool.Fori(0, st.bodies) as i:
            turn(i)


class Scale:

    def __init__(self, co):
        name = co.tag("scale")
        self.co = co
        self.summed, self.meaned, self.rooted, self.ready = (
            co.sem(f"{name}_{s}") for s in ("summed", "meaned", "rooted", "ready"))

    def pe(self, pe):
        co = self.co
        co.nc.tensor.matmul(co.PS[:, 7, :], co.ones[:], co.SS[:], start=True, stop=True).then_inc(self.summed, 1)

    def act(self, act):
        act.wait_ge(self.meaned, 1)
        self.co.nc.scalar.activation(self.co.RS[:], self.co.RS[:], ACT.Sqrt).then_inc(self.rooted, 1)

    def dve(self, dve):
        co = self.co
        dve.wait_ge(self.summed, 1)
        co.nc.vector.tensor_scalar(co.RS[:], co.PS[:, 7, :], 1.0 / D, EPS, ALU.mult, ALU.add).then_inc(self.meaned, 1)
        dve.wait_ge(self.rooted, 1)
        co.nc.vector.reciprocal(co.RS[:], co.RS[:]).then_inc(self.ready, 1)
        dve.wait_ge(self.ready, 1)


def rs1(co):
    return co.RS[:].unsqueeze(1)


@stage
def ffn(co, up, down, half, alpha, gain, normed=True, split=True):
    nc = co.nc
    assert half == 1.0 or alpha == 1.0
    with ExitStack() as ctx:
        name = co.tag("ffn")
        Gh = co.sb(f"{name}_gh", [P, FC, S], F32R, ctx)
        Gl = co.sb(f"{name}_gl", [P, FC, S], F32R, ctx)
        SG = co.sb(f"{name}_sg", [P, 2, 1, S], ctx=ctx)
        T = co.sb(f"{name}_t", [P, 2, 1, S], ctx=ctx)
        UR = co.sb(f"{name}_ur", [P, 2, 1, S], ctx=ctx)
        for u in down.units:
            u.x = (Gh, Gl)
        gate_read, banks_free, gated, product, rounded, g_ready = (
            co.sem(f"{name}_{s}") for s in ("gate_read", "banks_free", "gated", "product", "rounded", "g_ready"))
        scale = Scale(co) if normed else None
        res = Residual(co, ctx, down, 4, alpha, half, gain, T=T, SQ=SG, split=split)
        block = ctx.enter_context(nc.Block())

        @block.sync
        def _(sp):
            co.load(sp, up)
            co.load(sp, down)

        @block.tensor
        def _(pe):
            if normed:
                scale.pe(pe)
            co.multiply(pe, up, banks_free)
            co.multiply(pe, down, res.bank_free, (g_ready, [HALF, FC] * 2))

        @block.gpsimd
        def _(pool):
            if normed:
                pool.wait_ge(scale.summed, 1)
            res.pool(pool)

        @block.scalar
        def _(act):
            def read(i, c):
                n = 2 * i + c
                if normed:
                    act.wait_ge(gate_read, n + 1)
                    nc.scalar.activation(SG[:, c], SG[:, c], ACT.Silu).then_inc(gated, 1)
                else:
                    co.wait_units(act, up, i, c, 0)
                    nc.scalar.activation(SG[:, c], one(co.PS, 2 * c), ACT.Silu).then_inc(gated, 1)
                act.wait_ge(product, n + 1)
                nc.scalar.activation(one(Gh, n), T[:, c], ACT.Copy).then_inc(rounded, 1)
            co.run(act, up, co.split_hi, read, (lambda: scale.act(act)) if normed else None)
            co.run(act, down, co.split_hi, lambda i, c: res.act(act, i, c))

        @block.vector
        def _(dve):
            dve.sem_inc(banks_free, 2)
            dve.sem_inc(res.bank_free, 2)

            def read(i, c):
                n = 2 * i + c
                if normed:
                    co.wait_units(dve, up, i, c, 0)
                    nc.vector.tensor_mul(SG[:, c], one(co.PS, 2 * c), rs1(co)).then_inc(gate_read, 1)
                    co.wait_units(dve, up, i, c, 1)
                    nc.vector.tensor_mul(UR[:, c], one(co.PS, 2 * c + 1), rs1(co)).then_inc(banks_free, 1)
                    dve.wait_ge(gated, n + 1)
                    dve.wait_ge(banks_free, 2 + n + 1)
                    nc.vector.tensor_mul(T[:, c], UR[:, c], SG[:, c]).then_inc(product, 1)
                else:
                    co.wait_units(dve, up, i, c, 1)
                    dve.wait_ge(gated, n + 1)
                    nc.vector.tensor_mul(T[:, c], one(co.PS, 2 * c + 1), SG[:, c]).then_inc(product, 1)
                    dve.wait_ge(product, n + 1)
                    dve.sem_inc(banks_free, 1)
                dve.wait_ge(rounded, n + 1)
                nc.vector.tensor_sub(one(Gl, n), T[:, c], one(Gh, n).bitcast(F32)).then_inc(g_ready, 1)
            co.run(dve, up, co.split_lo, read, (lambda: scale.dve(dve)) if normed else None)
            co.run(dve, down, co.split_lo, lambda i, c: res.dve(dve, i, c))


@stage
def add_stage(co, st, alpha, gain, split=True):
    nc = co.nc
    with ExitStack() as ctx:
        res = Residual(co, ctx, st, 0, alpha, 1.0, gain, split=split)
        block = ctx.enter_context(nc.Block())

        @block.sync
        def _(sp):
            co.load(sp, st)

        @block.tensor
        def _(pe):
            co.multiply(pe, st, res.bank_free)

        @block.gpsimd
        def _(pool):
            res.pool(pool)

        @block.scalar
        def _(act):
            co.run(act, st, co.split_hi, lambda i, c: res.act(act, i, c))

        @block.vector
        def _(dve):
            dve.sem_inc(res.bank_free, 4)
            co.run(dve, st, co.split_lo, lambda i, c: res.dve(dve, i, c))


@stage
def enter(co, gain):
    nc, d = co.nc, co.dram
    st = co.stages[0]
    with ExitStack() as ctx:
        T = co.sb("enter_t", [P, DC, S], ctx=ctx)
        SQ = co.sb("enter_sq", [P, DC, S], ctx=ctx)
        arrived, loaded, gained, rounded, squared, added, parted = (co.sem(f"enter_{s}") for s in (
            "arrived", "loaded", "gained", "rounded", "squared", "added", "parted"))
        block = ctx.enter_context(nc.Block())

        @block.sync
        def _(sp):
            sp.dma_start(co.cols[:], d["cols"]).then_inc(loaded, 16)
            for c in range(DC):
                sp.dma_start(co.X[:, c, :], d["xT"][c * P:(c + 1) * P, :]).then_inc(arrived, 16)
                if c == 3:
                    co.load_turn(sp, st, 0)
            sp.dma_start(co.mats[:], d["mats"].rearrange("p (k n) -> p k n", n=P)).then_inc(loaded, 16)
            sp.wait_ge(loaded, 32)

        @block.gpsimd
        def _(pool):
            nc.gpsimd.memset(co.ones[:], 1.0).then_inc(added, 1)
            nc.gpsimd.memset(co.SS[:], 0.0).then_inc(added, 1)
            for c in range(DC if gain is not None else 0):
                pool.wait_ge(squared, c + 1)
                pool.wait_ge(added, c + 2)
                nc.gpsimd.tensor_add(co.SS[:], co.SS[:], SQ[:, c]).then_inc(added, 1)

        @block.tensor
        def _(pe):
            pe.sem_inc(co.unit_done, SPLIT)

        @block.scalar
        def _(act):
            act.wait_ge(arrived, 16 * DC)
            for c in range(DC):
                if gain is not None:
                    nc.scalar.activation(SQ[:, c], co.X[:, c], ACT.Square).then_inc(squared, 1)
                    act.wait_ge(gained, c + 1)
                nc.scalar.activation(co.Hh[:, c], co.X[:, c] if gain is None else T[:, c], ACT.Copy).then_inc(rounded, 1)
            for j in range(SPLIT):
                co.split_hi(act, st, 0, j)
            if gain is None:
                act.sem_inc(squared, DC)

        @block.vector
        def _(dve):
            dve.wait_ge(arrived, 16 * DC)
            dve.wait_ge(loaded, 32)
            for c in range(DC):
                if gain is not None:
                    nc.vector.tensor_scalar(T[:, c], co.X[:, c], co.cols[:, gain + c:gain + c + 1], None, ALU.mult).then_inc(gained, 1)
            for c in range(DC):
                dve.wait_ge(rounded, c + 1)
                if gain is not None:
                    dve.wait_ge(gained, c + 1)
                nc.vector.tensor_sub(co.Hl[:, c], co.X[:, c] if gain is None else T[:, c], co.Hh[:, c].bitcast(F32)).then_inc(parted, 1)
            for j in range(SPLIT):
                co.split_lo(dve, st, 0, j)



SSD_H = 8
OFF = [0, 512, 896, 1152]
TRI = 1280


@stage
def causal_conv_silu(co, EZ, XC, cols, dtm):
    nc = co.nc
    name = "ssd_conv"
    DT, AT, W = dtm
    c0 = co.cols
    tapped, activated, dt_step, a_step = (co.sem(f"{name}_{s}") for s in ("tapped", "activated", "dt_step", "a_step"))
    with nc.Block() as block:
        @block.vector
        def _(dve):
            v = nc.vector
            steps = [0]

            def step(ins):
                steps[0] += 1
                ins.then_inc(dt_step, 1)
                dve.wait_ge(dt_step, steps[0])
            xb, ab, q, z, z2, rl = (W[:, n, :] for n in range(6))
            step(v.tensor_mul(xb, co.PS[0:SSD_H, 4, :], co.RS[0:SSD_H, :]))
            step(v.tensor_scalar(xb, xb, c0[0:SSD_H, cols["dt_bias"]:cols["dt_bias"] + 1], None, ALU.add))
            step(v.scalar_tensor_tensor(ab, xb, -1.0, xb, ALU.mult, ALU.max))
            step(v.tensor_scalar(rl, xb, 0.0, None, ALU.max))
            for tap in range(4):
                for c in range(8):
                    w = c0[:, cols["conv_w"] + 8 * (3 - tap) + c:cols["conv_w"] + 8 * (3 - tap) + c + 1]
                    if tap == 0:
                        v.tensor_scalar(XC[:, c, :], EZ[:, 4 + c, :], w, c0[:, cols["conv_b"] + c:cols["conv_b"] + c + 1],
                                        ALU.mult, ALU.add).then_inc(tapped, 1)
                    else:
                        dve.wait_ge(tapped, 8 * (tap - 1) + c + 1)
                        v.scalar_tensor_tensor(XC[:, c, tap:], EZ[:, 4 + c, 0:S - tap], w, XC[:, c, tap:],
                                               ALU.mult, ALU.add).then_inc(tapped, 1)
            dve.wait_ge(a_step, 2)
            step(v.tensor_scalar(q, ab, 2.0, None, ALU.add))
            step(v.reciprocal(q, q))
            step(v.tensor_mul(z, ab, q))
            step(v.tensor_mul(z2, z, z))
            step(v.tensor_scalar(q, z2, 1.0 / 15, None, ALU.mult))
            for odd in (13, 11, 9, 7, 5, 3):
                step(v.scalar_tensor_tensor(q, q, 1.0 / odd, z2, ALU.add, ALU.mult))
            step(v.scalar_tensor_tensor(q, q, 1.0, z, ALU.add, ALU.mult))
            step(v.scalar_tensor_tensor(DT[:], q, 2.0, rl, ALU.mult, ALU.add))
            step(v.tensor_scalar(xb, DT[:], W[:, 6, 0:1], -1.0, ALU.mult, ALU.mult))
            step(v.tensor_tensor_scan(AT[:], co.ones8[:], xb, 0.0, ALU.mult, ALU.add))

        @block.scalar
        def _(act):
            nc.scalar.activation(W[:, 6, 0:1], c0[0:SSD_H, cols["a_log"]:cols["a_log"] + 1], ACT.Exp).then_inc(a_step, 1)
            act.wait_ge(dt_step, 3)
            nc.scalar.activation(W[:, 1, :], W[:, 1, :], ACT.Exp, scale=-1.0).then_inc(a_step, 1)
            for c in range(4):
                nc.scalar.activation(EZ[:, c, :], EZ[:, c, :], ACT.Silu).then_inc(activated, 1)
            for c in range(8):
                act.wait_ge(tapped, 24 + c + 1)
                nc.scalar.activation(XC[:, c, :], XC[:, c, :], ACT.Silu).then_inc(activated, 1)


@stage
def ssd_tokens(co, XC, dtm, AC, XDT, CB):
    nc = co.nc
    DT, AT, W = dtm
    name = "ssd_tok"
    cols_done, x_done, cb_done, cols_read, x_read, cb_read, masked = (
        co.sem(f"{name}_{s}") for s in ("cols_done", "x_done", "cb_done", "cols_read", "x_read", "cb_read", "masked"))
    with nc.Block() as block:
        @block.tensor
        def _(pe):
            for k, src in enumerate((AT, DT)):
                for t in range(TT):
                    m = nc.tensor.matmul(co.PS[:, 7, (k * TT + t) * 8:(k * TT + t + 1) * 8], src[:, t * P:(t + 1) * P],
                                         co.ident[0:8, 0:8], start=True, stop=True)
            m.then_inc(cols_done, 1)
            for t in range(TT):
                for c in range(4):
                    m = nc.tensor.transpose(co.PS[:, t, c * P:(c + 1) * P], XC[:, c, t * P:(t + 1) * P], co.ident)
                m.then_inc(x_done, 1)
            for g in range(2):
                for t in range(TT):
                    n = g * TT + t
                    if n >= 3:
                        pe.wait_ge(cb_read, n - 2)
                    nc.tensor.matmul(co.PS[:, 4 + n % 3, 0:S - t * P], XC[:, 4 + g, t * P:(t + 1) * P],
                                     XC[:, 6 + g, t * P:], start=True, stop=True).then_inc(cb_done, 1)

        @block.scalar
        def _(act):
            for g in range(2):
                for t in range(TT):
                    act.wait_ge(cb_done, g * TT + t + 1)
                    nc.scalar.activation(CB[:, g, OFF[t]:OFF[t] + S - t * P], co.PS[:, 4 + (g * TT + t) % 3, 0:S - t * P],
                                         ACT.Copy).then_inc(cb_read, 1)

        @block.vector
        def _(dve):
            dve.wait_ge(cols_done, 1)
            nc.vector.tensor_copy(AC[:], co.PS[:, 7, 0:64]).then_inc(cols_read, 1)
            dve.wait_ge(cols_read, 1)
            for t in range(TT):
                dve.wait_ge(x_done, t + 1)
                dt = AC[:, 32 + 8 * t:32 + 8 * t + 8].unsqueeze(2).broadcast_to([P, 8, HD])
                nc.vector.tensor_mul(XDT[:, t, :].rearrange("p (h d) -> p h d", d=HD),
                                     co.PS[:, t, :].rearrange("p (h d) -> p h d", d=HD), dt).then_inc(x_read, 1)
            for g in range(2):
                for t in range(TT):
                    dve.wait_ge(cb_read, g * TT + t + 1)
                    d = CB[:, g, OFF[t]:OFF[t] + P]
                    nc.vector.tensor_mul(d, d, co.triu).then_inc(masked, 1)


@stage
def ssd_heads(co, dtm, AC, XDT, CB, XC, EZ, Y, cols):
    nc = co.nc
    DT, AT, W = dtm
    name = "ssd_heads"
    with ExitStack() as ctx:
        SEG = co.sb(f"{name}_seg", [P, 2, TRI], ctx=ctx)
        M = co.sb(f"{name}_m", [P, 2, TRI], ctx=ctx)
        spread, seg_ready, decayed, weighted, y_done, skipped = (
            co.sem(f"{name}_{s}") for s in ("spread", "seg_ready", "decayed", "weighted", "y_done", "skipped"))
        block = ctx.enter_context(nc.Block())

        @block.tensor
        def _(pe):
            def spread_a(h):
                if h >= 2:
                    pe.wait_ge(seg_ready, h - 1)
                nc.tensor.matmul(co.PS[:, h % 2, :], co.sel8[:, h * P:(h + 1) * P], AT[:], start=True, stop=True).then_inc(spread, 1)
            spread_a(0)
            for h in range(SSD_H):
                if h + 1 < SSD_H:
                    spread_a(h + 1)
                pe.wait_ge(weighted, h + 1)
                po = HD * (h % 2)
                for t in range(TT):
                    m = nc.tensor.matmul(co.PS[po:po + HD, 2 + h // 2, t * P:], XDT[:, t, h * HD:(h + 1) * HD],
                                         M[:, h % 2, OFF[t]:OFF[t] + S - t * P], start=t == 0, stop=t == TT - 1)
                m.then_inc(y_done, 1)

        @block.scalar
        def _(act):
            for h in range(SSD_H):
                act.wait_ge(seg_ready, h + 1)
                nc.scalar.activation(SEG[:, h % 2, :], SEG[:, h % 2, :], ACT.Exp).then_inc(decayed, 1)

        @block.vector
        def _(dve):
            def weigh(h):
                dve.wait_ge(decayed, h + 1)
                if h >= 2:
                    dve.wait_ge(y_done, h - 1)
                nc.vector.tensor_mul(M[:, h % 2, :], SEG[:, h % 2, :], CB[:, h // 4, :]).then_inc(weighted, 1)
            for h in range(SSD_H):
                dve.wait_ge(spread, h + 1)
                if h >= 2:
                    dve.wait_ge(weighted, h - 1)
                for t in range(TT):
                    s = nc.vector.tensor_scalar(SEG[:, h % 2, OFF[t]:OFF[t] + S - t * P], co.PS[:, h % 2, t * P:],
                                                AC[:, 8 * t + h:8 * t + h + 1], 0.0, ALU.subtract, ALU.min)
                s.then_inc(seg_ready, 1)
                if h >= 1:
                    weigh(h - 1)
            weigh(SSD_H - 1)
            for c in range(4):
                dve.wait_ge(y_done, 2 * c + 2)
                nc.vector.scalar_tensor_tensor(Y[:, c, :], XC[:, c, :], co.cols[:, cols["ssd_d"] + c:cols["ssd_d"] + c + 1],
                                               co.PS[:, 2 + c, :], ALU.mult, ALU.add).then_inc(skipped, 1)
            for c in range(4):
                dve.wait_ge(skipped, c + 1)
                nc.vector.tensor_mul(Y[:, c, :], Y[:, c, :], EZ[:, c, :]).then_inc(skipped, 1)


NT = 48
TWO_PI = 6.283185307179586
WRAP = 6.2831845
CW1 = 6.28125
CW2 = TWO_PI - CW1


@stage
def s5_parameters(co, SP, PH, B, C, BT, CT, cols):
    nc = co.nc
    with ExitStack() as ctx:
        N = co.sb("s5_n", [P, S5G, NT], ctx=ctx)
        L = co.sb("s5_l", [P, S5G, NT], ctx=ctx)
        BB = co.sb("s5_bb", [P, 2, S5G, 16], ctx=ctx)
        CC = co.sb("s5_cc", [P, 2, S5G, 16], ctx=ctx)
        loaded, vstep, astep, turned, zeroed = (co.sem(f"s5p_{s}") for s in ("loaded", "vstep", "astep", "turned", "zeroed"))
        block = ctx.enter_context(nc.Block())
        ar, ai, dt, mag, ang, ph, sn, cs, n, t1, t2, den, fre, fim, phh, phl = (SP[:, k, :] for k in range(16))
        sg = co.cols[:, cols["sign"]:cols["sign"] + 1]

        @block.sync
        def _(sp):
            sp.dma_start(SP[:, 0:3, :], co.dram["s5p"].rearrange("p (a g) -> p a g", g=S5G)).then_inc(loaded, 16)
            sp.dma_start(B[:], co.dram["s5b"].rearrange("p (a g i) -> p a g i", g=S5G, i=16)).then_inc(loaded, 16)
            sp.dma_start(C[:], co.dram["s5c"].rearrange("p (a g i) -> p a g i", g=S5G, i=16)).then_inc(loaded, 16)

        @block.gpsimd
        def _(pool):
            nc.gpsimd.memset(CT[:], 0.0).then_inc(zeroed, 1)

        @block.scalar
        def _(act):
            act.wait_ge(loaded, 48)
            nc.scalar.activation(dt, dt, ACT.Exp).then_inc(astep, 1)
            act.wait_ge(vstep, 1)
            nc.scalar.activation(mag, t1, ACT.Exp).then_inc(astep, 1)
            act.wait_ge(vstep, 10)
            nc.scalar.activation(sn, sn, ACT.Sin, scale=WRAP).then_inc(astep, 1)
            nc.scalar.activation(cs, cs, ACT.Sin, scale=WRAP).then_inc(astep, 1)

        @block.tensor
        def _(pe):
            pe.wait_ge(vstep, 33)
            for k in range(2):
                for q in range(4):
                    m = nc.tensor.transpose(co.PS[:, k, q * P:(q + 1) * P],
                                            BB[:, k, 8 * q:8 * q + 8, :].rearrange("p g i -> p (g i)"), co.ident)
            m.then_inc(turned, 1)

        @block.vector
        def _(dve):
            v = nc.vector
            steps = [0]

            def step(ins):
                steps[0] += 1
                ins.then_inc(vstep, 1)
                dve.wait_ge(vstep, steps[0])

            def over(x, k):
                return x.unsqueeze(2).broadcast_to([P, S5G, k])
            dve.wait_ge(astep, 1)
            step(v.tensor_mul(t1, dt, ar))
            step(v.tensor_mul(ang, dt, ai))
            step(v.tensor_scalar(n, ang, 1.0 / TWO_PI, MAGIC, ALU.mult, ALU.add))
            step(v.tensor_scalar(n, n, MAGIC, None, ALU.subtract))
            step(v.scalar_tensor_tensor(ph, n, -CW1, ang, ALU.mult, ALU.add))
            step(v.scalar_tensor_tensor(ph, n, -CW2, ph, ALU.mult, ALU.add))
            step(v.tensor_scalar(ph, ph, 1.0 / TWO_PI, None, ALU.mult))
            step(v.tensor_scalar(sn, ph, 0.5, -0.5, ALU.min, ALU.max))
            step(v.scalar_tensor_tensor(cs, sn, -1.0, sn, ALU.mult, ALU.max))
            step(v.tensor_scalar(cs, cs, -1.0, 0.25, ALU.mult, ALU.add))
            dve.wait_ge(astep, 4)
            step(v.tensor_mul(sn, sn, mag))
            step(v.tensor_mul(cs, cs, mag))
            step(v.tensor_scalar(cs, cs, 1.0, None, ALU.subtract))
            step(v.tensor_mul(den, ar, ar))
            step(v.tensor_mul(t1, ai, ai))
            step(v.tensor_add(den, den, t1))
            step(v.reciprocal(den, den))
            step(v.tensor_mul(t1, cs, ar))
            step(v.tensor_mul(t2, sn, ai))
            step(v.tensor_add(t1, t1, t2))
            step(v.tensor_mul(fre, t1, den))
            step(v.tensor_mul(t1, sn, ar))
            step(v.tensor_mul(t2, cs, ai))
            step(v.tensor_sub(t1, t1, t2))
            step(v.tensor_mul(fim, t1, den))
            step(v.tensor_scalar(t1, fim, sg, -1.0, ALU.mult, ALU.mult))
            step(v.tensor_scalar(t2, fre, sg, None, ALU.mult))
            step(v.tensor_mul(BB[:, 0], B[:, 0], over(fre, 16)))
            step(v.tensor_mul(BB[:, 1], B[:, 1], over(t1, 16)))
            step(v.tensor_add(BB[:, 0], BB[:, 0], BB[:, 1]))
            step(v.tensor_mul(BB[:, 1], B[:, 1], over(t2, 16)))
            step(v.tensor_mul(CC[:, 0], B[:, 0], over(fim, 16)))
            step(v.tensor_add(BB[:, 1], BB[:, 1], CC[:, 0]))
            step(v.tensor_scalar(CC[:, 0], C[:, 0], sg, None, ALU.mult))
            step(v.tensor_scalar(CC[:, 1], C[:, 1], -1.0, None, ALU.mult))
            step(v.tensor_scalar(phh, ph, 3072.0, None, ALU.add))
            step(v.tensor_scalar(phh, phh, 3072.0, None, ALU.subtract))
            step(v.tensor_sub(phl, ph, phh))
            tv = co.cols[:, cols["tokens"]:cols["tokens"] + NT].unsqueeze(1).broadcast_to([P, S5G, NT])
            step(v.tensor_mul(PH[:], over(phh, NT), tv))
            step(v.tensor_scalar(N[:], PH[:], MAGIC, None, ALU.add))
            step(v.tensor_scalar(N[:], N[:], MAGIC, None, ALU.subtract))
            step(v.tensor_sub(PH[:], PH[:], N[:]))
            step(v.tensor_mul(L[:], over(phl, NT), tv))
            step(v.tensor_add(PH[:], PH[:], L[:]))
            dve.wait_ge(zeroed, 1)
            for k in range(2):
                for e in range(2):
                    v.tensor_copy(CT[:, k, :, e, 16 * e:16 * e + 16],
                                  CC[:, k].rearrange("p (a e) i -> p a e i", e=2)[:, :, e, :]).then_inc(zeroed, 1)
            dve.wait_ge(turned, 1)
            for k in range(2):
                for e in range(2):
                    m = co.cols[:, cols["pair"] + e:cols["pair"] + e + 1]
                    v.tensor_scalar(BT[:, k, :, e, :], co.PS[:, k, :].rearrange("p (q n) -> p q n", n=P), m, None,
                                    ALU.mult).then_inc(zeroed, 1)


@stage
def s5_groups(co, SP, PH, BT, CT, U, YB, cols):
    nc = co.nc
    with ExitStack() as ctx:
        W = co.sb("s5_w", [P, 4, S], ctx=ctx)
        R = co.sb("s5_r", [P, 4, S], ctx=ctx)
        CS = co.sb("s5_cs", [P, 4, S], ctx=ctx)
        SN = co.sb("s5_sn", [P, 4, S], ctx=ctx)
        D1 = co.sb("s5_d1", [P, 2, S], ctx=ctx)
        D2 = co.sb("s5_d2", [P, 2, S], ctx=ctx)
        G = co.sb("s5_g", [P, 2, S], ctx=ctx)
        O1 = co.sb("s5_o1", [P, 2, S], ctx=ctx)
        O2 = co.sb("s5_o2", [P, 2, S], ctx=ctx)
        (phased, whole, wrapped, sine, folded, cosine, driven, turned1, turned2, drive, states, back, out_done) = (
            co.sem(f"s5_{s}") for s in ("phased", "whole", "wrapped", "sine", "folded", "cosine", "driven",
                                        "turned1", "turned2", "drive", "states", "back", "out_done"))
        block = ctx.enter_context(nc.Block())
        y_read = co.sem("s5_y_read")
        PI2 = co.cols[:, cols["half_pi"]:cols["half_pi"] + 1]

        @block.gpsimd
        def _(pool):
            def phase(g):
                b = g % 4
                if g >= 4:
                    pool.wait_ge(cosine, g - 3)
                a = PH[:, g, 32:48].unsqueeze(2).broadcast_to([P, 16, 32])
                t = PH[:, g, 0:32].unsqueeze(1).broadcast_to([P, 16, 32])
                nc.gpsimd.tensor_add(R[:, b].rearrange("p (a t) -> p a t", t=32), a, t).then_inc(phased, 1)

            def wrap(g):
                pool.wait_ge(whole, g + 1)
                nc.gpsimd.tensor_sub(R[:, g % 4], R[:, g % 4], W[:, g % 4]).then_inc(wrapped, 1)
            for g in range(-3, S5G):
                if g + 3 < S5G:
                    phase(g + 3)
                if 0 <= g + 2 < S5G:
                    wrap(g + 2)
                if g >= 0:
                    pool.wait_ge(turned2, g + 1)
                    nc.gpsimd.tensor_add(D1[:, g % 2], D1[:, g % 2], D2[:, g % 2]).then_inc(drive, 1)

        @block.scalar
        def _(act):
            for g in range(S5G):
                b = g % 4
                act.wait_ge(wrapped, g + 1)
                if g >= 4:
                    act.wait_ge(back, g - 3)
                nc.scalar.activation(SN[:, b], R[:, b], ACT.Sin, scale=WRAP).then_inc(sine, 1)
                act.wait_ge(sine, g + 1)
                nc.scalar.activation(R[:, b], R[:, b], ACT.Abs).then_inc(folded, 1)
                act.wait_ge(folded, g + 1)
                nc.scalar.activation(CS[:, b], R[:, b], ACT.Sin, scale=-WRAP, bias=PI2).then_inc(cosine, 1)

        @block.tensor
        def _(pe):
            def drives(g):
                q, j = g // 8, g % 8
                r = 32 * (j // 2)
                if g >= 3:
                    pe.wait_ge(turned2, g - 2)
                for k in range(2):
                    m = nc.tensor.matmul(co.PS[:, 2 * (g % 3) + k, :], BT[r:r + 32, k, q, j % 2, :], U[r:r + 32, q, :],
                                         start=True, stop=True)
                m.then_inc(driven, 1)
            drives(0)
            drives(1)
            for g in range(S5G):
                if g + 2 < S5G:
                    drives(g + 2)
                q, j = g // 8, g % 8
                r = 32 * (j // 2)
                if q >= 2 and j == 0:
                    pe.wait_ge(y_read, q - 1)
                pe.wait_ge(back, g + 1)
                for k, o in enumerate((O1, O2)):
                    m = nc.tensor.matmul(co.PS[r:r + 32, 6 + q % 2, :], CT[:, k, g // 2, j % 2, :], o[:, g % 2, :],
                                         start=j % 2 == 0 and k == 0, stop=j % 2 == 1 and k == 1)
                m.then_inc(out_done, 1)

        @block.vector
        def _(dve):
            v = nc.vector

            def whole_turns(g):
                dve.wait_ge(phased, g + 1)
                if g >= 4:
                    dve.wait_ge(wrapped, g - 3)
                v.tensor_scalar(W[:, g % 4], R[:, g % 4], MAGIC, MAGIC, ALU.add, ALU.subtract).then_inc(whole, 1)

            def turn(g):
                b = g % 2
                dve.wait_ge(driven, g + 1)
                dve.wait_ge(cosine, g + 1)
                if g >= 2:
                    dve.wait_ge(states, g - 1)
                v.tensor_mul(D1[:, b], co.PS[:, 2 * (g % 3), :], CS[:, g % 4]).then_inc(turned1, 1)
                v.tensor_mul(D2[:, b], co.PS[:, 2 * (g % 3) + 1, :], SN[:, g % 4]).then_inc(turned2, 1)

            def output(q):
                dve.wait_ge(out_done, 8 * q + 8)
                k = cols["s5_d"] + q
                v.scalar_tensor_tensor(YB[:, q, :], U[:, q, :], co.cols[:, k:k + 1], co.PS[:, 6 + q % 2, :],
                                       ALU.mult, ALU.add).then_inc(y_read, 1)
            for g in range(3):
                whole_turns(g)
            turn(0)
            for g in range(S5G):
                b = g % 2
                if g + 1 < S5G:
                    turn(g + 1)
                if g + 3 < S5G:
                    whole_turns(g + 3)
                dve.wait_ge(drive, g + 1)
                mag = SP[:, 3, g:g + 1].broadcast_to([P, S])
                v.tensor_tensor_scan(G[:, b], mag, D1[:, b], 0.0, ALU.mult, ALU.add).then_inc(states, 1)
                dve.wait_ge(states, g + 1)
                if g >= 2:
                    dve.wait_ge(out_done, g - 1)
                v.tensor_mul(O1[:, b], G[:, b], CS[:, g % 4])
                v.tensor_mul(O2[:, b], G[:, b], SN[:, g % 4]).then_inc(back, 1)
                if g % 8 == 1 and g > 8:
                    output(g // 8 - 1)
            output(S5G // 8 - 1)


@stage
def s5_out(co, YB, G4):
    nc = co.nc
    with ExitStack() as ctx:
        T = co.sb("s5o_t", [P, 4, S], ctx=ctx)
        gelued, rounded, done = (co.sem(f"s5o_{s}") for s in ("gelued", "rounded", "done"))
        block = ctx.enter_context(nc.Block())

        @block.vector
        def _(dve):
            for c in range(4):
                dve.wait_ge(rounded, c + 1)
                nc.vector.tensor_sub(G4[1][:, c, :], T[:, c, :], G4[0][:, c, :].bitcast(F32)).then_inc(done, 1)

        @block.scalar
        def _(act):
            for c in range(4):
                nc.scalar.activation(T[:, c, :], YB[:, c, :], ACT.Gelu_apprx_tanh).then_inc(gelued, 1)
                act.wait_ge(gelued, c + 1)
                nc.scalar.activation(G4[0][:, c, :], T[:, c, :], ACT.Copy).then_inc(rounded, 1)


@stage
def gated_split(co, YB, SGT, M, c0):
    nc = co.nc
    name = co.tag("gsplit")
    product, rounded, done = (co.sem(f"{name}_{s}") for s in ("product", "rounded", "done"))
    with nc.Block() as block:
        @block.vector
        def _(dve):
            for c in range(4):
                nc.vector.tensor_mul(YB[:, c, :], YB[:, c, :], SGT[:, c, :]).then_inc(product, 1)
            for c in range(4):
                dve.wait_ge(rounded, c + 1)
                nc.vector.tensor_sub(M[1][:, c0 + c, :], YB[:, c, :], M[0][:, c0 + c, :].bitcast(F32)).then_inc(done, 1)

        @block.scalar
        def _(act):
            for c in range(4):
                act.wait_ge(product, c + 1)
                nc.scalar.activation(M[0][:, c0 + c, :], YB[:, c, :], ACT.Copy).then_inc(rounded, 1)


def scaled_to(co, buf):
    return lambda i, c: ("dve", lambda ps: co.nc.vector.tensor_mul(one(buf, RAW * i + c), ps, rs1(co)))


def to_buffer(co, buf, func=ACT.Copy):
    def reads(i, c):
        if c % 2 == 0 or func != ACT.Copy:
            return "act", lambda ps: co.nc.scalar.activation(one(buf, RAW * i + c), ps, func)
        return "dve", lambda ps: co.nc.vector.tensor_copy(one(buf, RAW * i + c), ps)
    return reads


def plan_even(co):
    u = feed(co, "ein_u")
    zx = feed(co, "ein_zx")
    w = co.dram["ein_dt"]
    dt = co.plan(Stage(1, [Unit(2, lambda i, j=j: w[j], (co.Hh, co.Hl), 2 * j, 4, j == 0, j == RAW - 1)
                           for j in range(RAW)], 1, 1))
    glu = feed(co, "glu")
    out = feed(co, "eout")
    return u, zx, dt, glu, out


def even_mixer(co, plan, cols, gain):
    nc = co.nc
    st_u, st_zx, st_dt, st_glu, st_out = plan
    with ExitStack() as ctx:
        U = co.sb("U", [P, 4, S], ctx=ctx)
        Y = co.sb("Y", [P, 4, S], ctx=ctx)
        copy_stage(co, st_u, scaled_to(co, U), scaled=True)
        with ExitStack() as inner:
            EZ = co.sb("EZ", [P, 12, S], ctx=inner)
            XC = co.sb("XC", [P, 8, S], ctx=inner)
            DT = co.sb("DT", [SSD_H, S], ctx=inner)
            AT = co.sb("AT", [SSD_H, S], ctx=inner)
            AC = co.sb("AC", [P, 64], ctx=inner)
            co.sel8 = co.sb("sel8", [SSD_H, SSD_H * P], ctx=inner)
            copy_stage(co, st_zx, scaled_to(co, EZ))
            with ExitStack() as tmp:
                W8 = co.sb("W8", [SSD_H, 7, S], ctx=tmp)
                co.ones8 = co.sb("ones8", [SSD_H, S], ctx=tmp)
                copy_stage(co, st_dt, None)
                fill, sel_in = co.sem("ones8_filled"), co.sem("sel8_in")
                with nc.Block() as block:
                    @block.sync
                    def _(sp):
                        sp.dma_start(co.sel8[:], co.dram["sel8"]).then_inc(sel_in, 16)
                        sp.wait_ge(sel_in, 16)

                    @block.gpsimd
                    def _(pool):
                        nc.gpsimd.memset(co.ones8[:], 1.0).then_inc(fill, 1)
                causal_conv_silu(co, EZ, XC, cols, (DT, AT, W8))
            with ExitStack() as tmp:
                XDT = co.sb("XDT", [P, TT, S], ctx=tmp)
                CB = co.sb("CB", [P, 2, TRI], ctx=tmp)
                ssd_tokens(co, XC, (DT, AT, None), AC, XDT, CB)
                ssd_heads(co, (DT, AT, None), AC, XDT, CB, XC, EZ, Y, cols)
        with ExitStack() as inner:
            YB = co.sb("YB", [P, 4, S], ctx=inner)
            with ExitStack() as tmp:
                SP = co.sb("s5_sp", [P, 16, S5G], ctx=tmp)
                PH = co.sb("s5_ph", [P, S5G, NT], ctx=tmp)
                BT = co.sb("s5_bt", [P, 2, 4, 2, P], ctx=tmp)
                CT = co.sb("s5_ct", [P, 2, S5G // 2, 2, 32], ctx=tmp)
                with ExitStack() as raw:
                    B = co.sb("s5_b", [P, 2, S5G, 16], ctx=raw)
                    C = co.sb("s5_c", [P, 2, S5G, 16], ctx=raw)
                    s5_parameters(co, SP, PH, B, C, BT, CT, cols)
                s5_groups(co, SP, PH, BT, CT, U, YB, cols)
            M = (co.sb("even_mh", [P, DC, S], F32R, inner), co.sb("even_ml", [P, DC, S], F32R, inner))
            for g in range(2):
                norm_stage(co, 2, cols["ssd_norm"] + 2 * g, (*M, 2 * g), EPS, src=Y[:, 2 * g:2 * g + 2, :])
            GH = co.sb("s5_gh", [P, 4, S], F32R, inner)
            GL = co.sb("s5_gl", [P, 4, S], F32R, inner)
            s5_out(co, YB, (GH, GL))
            for u in st_glu.units:
                u.x = (GH, GL)
            SGT = co.sb("s5_sgt", [P, 4, S], ctx=inner)
            copy_stage(co, st_glu, lambda i, c: ("act", lambda ps: nc.scalar.activation(
                SGT[:, c:c + 1, :], ps, ACT.Sigmoid, bias=co.cols[:, cols["b_glu"] + c:cols["b_glu"] + c + 1])))
            gated_split(co, YB, SGT, M, 4)
            for u in st_out.units:
                u.x = M
            add_stage(co, st_out, 1.0, gain)





@stage
def head_norms(co, QK, n, q_chunks, cols):
    nc = co.nc
    with ExitStack() as ctx:
        SQ = co.sb("hn_sq", [P, n, S], ctx=ctx)
        R = co.sb("hn_r", [P, TT, n, 2], ctx=ctx)
        RT = co.sb("hn_rt", [2 * n, S], ctx=ctx)
        SEL = co.sb("hn_sel", [2 * n, n * P], ctx=ctx)
        squared, summed, scaled, rooted, inverted, turned, selected, spread, done = (
            co.sem(f"hn_{s}") for s in ("squared", "summed", "scaled", "rooted", "inverted", "turned", "selected",
                                        "spread", "done"))
        block = ctx.enter_context(nc.Block())

        @block.scalar
        def _(act):
            for c in range(n):
                nc.scalar.activation(SQ[:, c, :], QK[:, c, :], ACT.Square).then_inc(squared, 1)
            act.wait_ge(scaled, 1)
            nc.scalar.activation(R[:], R[:], ACT.Sqrt).then_inc(rooted, 1)

        @block.tensor
        def _(pe):
            for c in range(n):
                pe.wait_ge(squared, c + 1)
                for t in range(TT):
                    m = nc.tensor.matmul(co.PS[:, 0, (t * n + c) * 2:(t * n + c) * 2 + 2], SQ[:, c, t * P:(t + 1) * P],
                                         co.heads[:, 0:P:64], start=True, stop=True)
            m.then_inc(summed, 1)
            pe.wait_ge(inverted, 2)
            for t in range(TT):
                m = nc.tensor.transpose(co.PS[0:2 * n, 5, t * P:(t + 1) * P], R[:, t, :, :].rearrange("p c e -> p (c e)"),
                                        co.ident)
            m.then_inc(turned, 1)
            pe.wait_ge(inverted, 3)
            pe.wait_ge(selected, 16)
            for c in range(n):
                if c >= 4:
                    pe.wait_ge(done, c - 3)
                nc.tensor.matmul(co.PS[:, 1 + c % 4, :], SEL[:, c * P:(c + 1) * P], RT[:], start=True, stop=True).then_inc(spread, 1)

        @block.sync
        def _(sp):
            sp.dma_start(SEL[:], co.dram["hankel_sel"]).then_inc(selected, 16)

        @block.vector
        def _(dve):
            dve.wait_ge(summed, 1)
            nc.vector.tensor_scalar(R[:].rearrange("p t c e -> p (t c e)"), co.PS[:, 0, 0:TT * n * 2], 1.0 / HD, EPS,
                                    ALU.mult, ALU.add).then_inc(scaled, 1)
            dve.wait_ge(rooted, 1)
            nc.vector.reciprocal(R[:], R[:]).then_inc(inverted, 1)
            dve.wait_ge(inverted, 1)
            q = R[:, :, 0:q_chunks, :]
            nc.vector.tensor_scalar(q, q, HD ** -0.5, None, ALU.mult).then_inc(inverted, 1)
            dve.wait_ge(turned, 1)
            nc.vector.tensor_copy(RT[:], co.PS[0:2 * n, 5, :]).then_inc(inverted, 1)
            for c in range(n):
                dve.wait_ge(spread, c + 1)
                g = cols["q_gain"] if c < q_chunks else cols["k_gain"]
                nc.vector.scalar_tensor_tensor(QK[:, c, :], QK[:, c, :], co.cols[:, g:g + 1], co.PS[:, 1 + c % 4, :],
                                               ALU.mult, ALU.mult).then_inc(done, 1)


@stage
def turn_values(co, groups):
    nc = co.nc
    name = co.tag("values")
    turned, stored = co.sem(f"{name}_turned"), co.sem(f"{name}_stored")
    with nc.Block() as block:
        @block.tensor
        def _(pe):
            for n, (V, tokens) in enumerate(groups):
                if n >= 2:
                    pe.wait_ge(stored, TT * (n - 1))
                for t in range(TT):
                    for c in range(4):
                        m = nc.tensor.transpose(co.PS[:, 4 * (n % 2) + t, c * P:(c + 1) * P], V[:, c, tokens(t)], co.ident)
                m.then_inc(turned, 1)

        @block.vector
        def _(dve):
            for n, (V, tokens) in enumerate(groups):
                dve.wait_ge(turned, n + 1)
                for t in range(TT):
                    nc.vector.tensor_copy(V[:, t, :], co.PS[:, 4 * (n % 2) + t, :]).then_inc(stored, 1)


@stage
def attend(co, items, score, tiles, value, width, scale, s_banks, out_bank, out_read, extra=None):
    nc = co.nc
    name = co.tag("attend")
    n = len(items)
    nb = len(s_banks)
    with ExitStack() as ctx:
        PR = co.sb(f"{name}_pr", [P, 3, width], ctx=ctx)
        PT = co.sb(f"{name}_pt", [P, 2, width], ctx=ctx)
        ST = co.sb(f"{name}_st", [P, 3, 4], ctx=ctx)
        scored, topped, negated, powered, inverted, normed, turned, copied, weighted, out_hi, out_lo = (
            co.sem(f"{name}_{s}") for s in ("scored", "topped", "negated", "powered", "inverted", "normed", "turned",
                                            "copied", "weighted", "out_hi", "out_lo"))
        block = ctx.enter_context(nc.Block())
        halves_ = [(tiles(x) + 3) // 4 for x in items]
        before = [sum(halves_[:k]) for k in range(n + 1)]

        def sview(k):
            b = s_banks[k % nb]
            return co.PS[:, b:b + (width + 511) // 512, :].rearrange("p b n -> p (b n)")

        def tview(m):
            return co.PS[:, s_banks[-1] + (width + 511) // 512 + m % 2, :]

        @block.tensor
        def _(pe):
            for k in range(n + 3):
                if k < n:
                    if k >= nb:
                        pe.wait_ge(powered, k - nb + 1)
                    score(items[k], sview(k)).then_inc(scored, 1)
                if 2 <= k < n + 2:
                    x = items[k - 2]
                    pe.wait_ge(normed, k - 1)
                    for m in range(halves_[k - 2]):
                        b = before[k - 2] + m
                        if b >= 2:
                            pe.wait_ge(copied, b - 1)
                        for t in range(4 * m, min(4 * m + 4, tiles(x))):
                            i = nc.tensor.transpose(tview(b)[:, (t % 4) * P:(t % 4 + 1) * P],
                                                    PR[:, (k - 2) % 3, t * P:(t + 1) * P], co.ident)
                        i.then_inc(turned, 1)
                if k >= 3:
                    x = items[k - 3]
                    pe.wait_ge(copied, before[k - 2])
                    bank, part, cs, need = out_bank(x)
                    if need is not None:
                        pe.wait_ge(out_lo, need)
                    for t in range(tiles(x)):
                        i = nc.tensor.matmul(co.PS[part:part + HD, bank, cs], value(x, t),
                                             PT[:, (k - 3) % 2, t * P:(t + 1) * P], start=t == 0, stop=t == tiles(x) - 1)
                    i.then_inc(weighted, 1)

        @block.vector
        def _(dve):
            outs = 0
            for k in range(n + 1):
                if k < n:
                    w = tiles(items[k]) * P
                    dve.wait_ge(scored, k + 1)
                    nc.vector.reduce_max(ST[:, k % 3, 0:1], sview(k)[:, 0:w], axis=AX.X).then_inc(topped, 1)
                    dve.wait_ge(topped, k + 1)
                    nc.vector.tensor_scalar(ST[:, k % 3, 1:2], ST[:, k % 3, 0:1], -scale, None, ALU.mult).then_inc(negated, 1)
                if k >= 1:
                    w = tiles(items[k - 1]) * P
                    b = (k - 1) % 3
                    dve.wait_ge(powered, k)
                    nc.vector.reciprocal(ST[:, b, 3:4], ST[:, b, 2:3]).then_inc(inverted, 1)
                    dve.wait_ge(inverted, k)
                    nc.vector.tensor_scalar(PR[:, b, 0:w], PR[:, b, 0:w], ST[:, b, 3:4], None, ALU.mult).then_inc(normed, 1)
                    if k >= 4 and out_read(k - 4) is not None:
                        hi, lo, src = out_read(k - 4)
                        outs += 1
                        dve.wait_ge(out_hi, outs)
                        nc.vector.tensor_sub(lo, src, hi.bitcast(F32)).then_inc(out_lo, 1)
            for k in range(n - 3, n):
                if out_read(k) is not None:
                    hi, lo, src = out_read(k)
                    outs += 1
                    dve.wait_ge(out_hi, outs)
                    nc.vector.tensor_sub(lo, src, hi.bitcast(F32)).then_inc(out_lo, 1)

        @block.scalar
        def _(act):
            for k in range(n + 3):
                if k < n:
                    w = tiles(items[k]) * P
                    act.wait_ge(negated, k + 1)
                    if k >= 3:
                        act.wait_ge(turned, before[k - 2])
                    nc.scalar.activation(PR[:, k % 3, 0:w], sview(k)[:, 0:w], ACT.Exp, bias=ST[:, k % 3, 1:2],
                                         scale=scale, accum_out=ST[:, k % 3, 2:3]).then_inc(powered, 1)
                if 2 <= k < n + 2:
                    x = items[k - 2]
                    if k >= 4:
                        act.wait_ge(weighted, k - 3)
                    for m in range(halves_[k - 2]):
                        b = before[k - 2] + m
                        w0, w1 = 512 * m, min(512 * m + 512, tiles(x) * P)
                        act.wait_ge(turned, b + 1)
                        nc.scalar.activation(PT[:, (k - 2) % 2, w0:w1], tview(b)[:, 0:w1 - w0], ACT.Copy).then_inc(copied, 1)
                if k >= 3 and out_read(k - 3) is not None:
                    hi, lo, src = out_read(k - 3)
                    act.wait_ge(weighted, k - 2)
                    nc.scalar.activation(hi, src, ACT.Copy).then_inc(out_hi, 1)

        if extra:
            block.gpsimd(extra)


def plan_odd(co):
    return feed(co, "oin"), feed(co, "oout")


def odd_mixer(co, plan, cols, gain):
    nc = co.nc
    st_in, st_out = plan
    with ExitStack() as ctx:
        QU = co.sb("QU", [P, 16, S], ctx=ctx)
        HK = co.sb("HK", [P, 8, S], ctx=ctx)
        POOLED = co.sb("POOLED", [P, 4, S], ctx=ctx)
        PB = co.sb("PB", [P, 2, S], ctx=ctx)
        PW = co.sb("PW", [P, 4, P], ctx=ctx)
        RC = co.sb("RC", [P, 4, 16], ctx=ctx)
        MR = co.sb("MR", [1, P + 64], ctx=ctx)
        copy_stage(co, st_in, scaled_to(co, QU), scaled=True)
        loaded = co.sem("odd_loaded")
        with nc.Block() as block:
            @block.gpsimd
            def _(pool):
                row = co.dram["hankel"]
                pool.dma_start(HK[:], bass.AP(tensor=row.tensor, offset=0, ap=[[1, P], [row.shape[1], 8], [1, S]])).then_inc(loaded, 16)
                pool.dma_start(PW[:], co.dram["pool_w"].rearrange("g i o -> i g o")).then_inc(loaded, 16)
                pool.dma_start(RC[:], co.dram["counts"].rearrange("p (g t) -> p g t", t=16)).then_inc(loaded, 16)
                pool.dma_start(MR[:], co.dram["counts_mask"]).then_inc(loaded, 16)
                pool.wait_ge(loaded, 64)
        head_norms(co, QU[:, 0:8, :], 8, 4, cols)
        M = (co.sb("odd_mh", [P, DC, S], F32R, ctx), co.sb("odd_ml", [P, DC, S], F32R, ctx))
        turn_values(co, [(QU[:, 8:12, :], lambda t: slice(t * P, (t + 1) * P))])

        def score(x, ps):
            h, t = x
            c, r = h // 2, HD * (h % 2)
            w = (t + 1) * P
            nc.tensor.matmul(ps[:, 0:w], QU[r:r + HD, c, t * P:(t + 1) * P], QU[r:r + HD, 4 + c, 0:w], start=True, stop=False)
            nc.tensor.matmul(ps[:, 0:w], co.flip, HK[:, h, 384 - P * t:], start=False, stop=False)
            return nc.tensor.matmul(ps[:, w - 64:w], MR[:, 0:P], MR[:, P:], start=False, stop=True)

        pooling = co.sem("pooling")

        def pool_windows(pool):
            g_ = nc.gpsimd
            steps = [0]

            def step(ins):
                steps[0] += 1
                ins.then_inc(pooling, 1)
                pool.wait_ge(pooling, steps[0])
            for g in range(4):
                src = QU[:, 12 + g, :]
                for k in range(g + 1):
                    d = 1 << k
                    dst = POOLED[:, g, :] if (g - k) % 2 == 0 else PB[:, 0, :]
                    step(g_.tensor_copy(dst[:, 0:d], src[:, 0:d]))
                    step(g_.tensor_add(dst[:, d:], src[:, d:], src[:, 0:S - d]))
                    src = dst
                step(g_.tensor_mul(src[:, 0:16], src[:, 0:16], RC[:, g, :]))
                step(g_.tensor_scalar(src[:, 16:], src[:, 16:], 1.0 / (2 << g), None, ALU.mult))
                step(g_.tensor_sub(src, src, QU[:, 12 + g, :]))

        items = [(h, t) for h in range(8) for t in range(TT)]

        def out_read(k):
            if k % 8 != 7:
                return None
            c = k // 8
            return M[0][:, c, :], M[1][:, c, :], co.PS[:, 4 + c, :]
        attend(co, items, score, lambda x: x[1] + 1, lambda x, t: QU[:, 8 + t, x[0] * HD:(x[0] + 1) * HD], 512, 1.0,
               [0, 1], lambda x: (4 + x[0] // 2, HD * (x[0] % 2), slice(x[1] * P, (x[1] + 1) * P), None), out_read,
               pool_windows)
        with ExitStack() as tmp:
            T = co.sb("pool_t", [P, 4, S], ctx=tmp)
            made, scaled, rounded = co.sem("pool_made"), co.sem("pool_scaled"), co.sem("pool_rounded")
            block = tmp.enter_context(nc.Block())

            @block.tensor
            def _(pe):
                for g in range(4):
                    nc.tensor.matmul(co.PS[:, g, :], PW[:, g, :], POOLED[:, g, :], start=True, stop=True).then_inc(made, 1)

            @block.vector
            def _(dve):
                for g in range(4):
                    dve.wait_ge(made, g + 1)
                    k = cols["pool_scale"] + g
                    nc.vector.tensor_scalar(T[:, g, :], co.PS[:, g, :], co.cols[:, k:k + 1], None, ALU.mult).then_inc(scaled, 1)
                for g in range(4):
                    dve.wait_ge(rounded, g + 1)
                    nc.vector.tensor_sub(M[1][:, 4 + g, :], T[:, g, :], M[0][:, 4 + g, :].bitcast(F32)).then_inc(scaled, 1)

            @block.scalar
            def _(act):
                for g in range(4):
                    act.wait_ge(scaled, g + 1)
                    nc.scalar.activation(M[0][:, 4 + g, :], T[:, g, :], ACT.Copy).then_inc(rounded, 1)
        for u in st_out.units:
            u.x = M
        add_stage(co, st_out, 1.0, gain)



WINDOW = S + 4
MW = WINDOW + 2 * P
TAPS = 31
ALPHA = 2 ** 0.25


@stage
def rotate(co, QKV):
    nc = co.nc
    chunks = [12 * g + c for g in range(3) for c in range(8)]
    with ExitStack() as ctx:
        ROPE = co.sb("ROPE", [P, 2, S], ctx=ctx)
        A = co.sb("rope_a", [P, 2, S], ctx=ctx)
        B = co.sb("rope_b", [P, 2, S], ctx=ctx)
        loaded, turned, cosines, sines, done = (co.sem(f"rope_{s}") for s in ("loaded", "turned", "cosines", "sines", "done"))
        block = ctx.enter_context(nc.Block())

        @block.sync
        def _(sp):
            sp.dma_start(ROPE[:], co.dram["rope"].rearrange("p (a s) -> p a s", s=S)).then_inc(loaded, 16)

        @block.tensor
        def _(pe):
            for n, c in enumerate(chunks):
                if n >= 4:
                    pe.wait_ge(sines, n - 3)
                nc.tensor.matmul(co.PS[:, n % 4, :], co.rot, QKV[:, c, :], start=True, stop=True).then_inc(turned, 1)

        @block.gpsimd
        def _(pool):
            pool.wait_ge(loaded, 16)
            for n, c in enumerate(chunks):
                if n >= 2:
                    pool.wait_ge(done, n - 1)
                nc.gpsimd.tensor_mul(A[:, n % 2], QKV[:, c, :], ROPE[:, 0]).then_inc(cosines, 1)

        @block.vector
        def _(dve):
            dve.wait_ge(loaded, 16)

            def add(n):
                dve.wait_ge(cosines, n + 1)
                dve.wait_ge(sines, n + 1)
                nc.vector.tensor_add(QKV[:, chunks[n], :], A[:, n % 2], B[:, n % 2]).then_inc(done, 1)
            for n, c in enumerate(chunks):
                dve.wait_ge(turned, n + 1)
                if n >= 2:
                    dve.wait_ge(done, n - 1)
                nc.vector.tensor_mul(B[:, n % 2], co.PS[:, n % 4, :], ROPE[:, 1]).then_inc(sines, 1)
                if n >= 1:
                    add(n - 1)
            add(len(chunks) - 1)


def plan_hybrid(co):
    st = {n: feed(co, n) for n in ("hin_qkv", "hin_b", "hin_a", "hin_gate")}
    w = co.dram["hao"]
    st["hao"] = co.plan(Stage(w.shape[0] // RAW, [
        Unit(4, lambda i, j=j: w[bass.ds(RAW * i + j, 1)].rearrange("o p n -> p (o n)"), None, 0, j) for j in range(RAW)
    ], 2, 2))
    st["ho"] = feed(co, "ho")
    return st


@stage
def gates_and_conv(co, st, GT, U, CV, cols):
    nc = co.nc
    bank_free, tapped = co.sem("gates_bank_free"), co.sem("conv_tapped")
    with nc.Block() as block:
        @block.sync
        def _(sp):
            co.load(sp, st)

        @block.tensor
        def _(pe):
            co.multiply(pe, st, bank_free)

        @block.scalar
        def _(act):
            act.sem_inc(bank_free, 4)

            def read(i, c):
                co.wait_units(act, st, i, c)
                nc.scalar.activation(one(GT, RAW * i + c), one(co.PS, c), ACT.Sigmoid).then_inc(bank_free, 1)
            co.run(act, st, co.split_hi, read)

        @block.vector
        def _(dve):
            def read(i, c):
                last = isinstance(i, int) and i == st.bodies - 1 and c == RAW - 1
                for e in range(1 if last else 2):
                    tap = 8 * i + 2 * c + e
                    for n in range(4):
                        dve.wait_ge(tapped, 4 * tap + n + 1)
                        nc.vector.scalar_tensor_tensor(CV[:, n, :], U[:, n, bass.ds(tap, S)],
                                                       co.cols[:, bass.ds(cols["conv2_w"] + TAPS * n + tap, 1)],
                                                       CV[:, n, :], ALU.mult, ALU.add).then_inc(tapped, 1)
            for n in range(4):
                k = cols["conv2_b"] + n
                nc.vector.tensor_scalar(CV[:, n, :], U[:, n, 0:S], 0.0, co.cols[:, k:k + 1],
                                        ALU.mult, ALU.add).then_inc(tapped, 1)
            co.run(dve, st, co.split_lo, read)


@stage
def silu_split(co, CV, C2):
    nc = co.nc
    act_done, rounded, done = co.sem("silu_done"), co.sem("silu_rounded"), co.sem("silu_split")
    with nc.Block() as block:
        @block.scalar
        def _(act):
            for c in range(4):
                nc.scalar.activation(CV[:, c, :], CV[:, c, :], ACT.Silu).then_inc(act_done, 1)
            for c in range(4):
                act.wait_ge(act_done, c + 1)
                nc.scalar.activation(C2[0][:, c, :], CV[:, c, :], ACT.Copy).then_inc(rounded, 1)

        @block.vector
        def _(dve):
            for c in range(4):
                dve.wait_ge(rounded, c + 1)
                nc.vector.tensor_sub(C2[1][:, c, :], CV[:, c, :], C2[0][:, c, :].bitcast(F32)).then_inc(done, 1)


@stage
def merge(co, st, GT, M):
    nc = co.nc
    with ExitStack() as ctx:
        A = co.sb("merge_a", [P, 2, 1, S], ctx=ctx)
        B = co.sb("merge_b", [P, 2, 1, S], ctx=ctx)
        banks_free, first, added, rounded, done = (
            co.sem(f"merge_{s}") for s in ("banks_free", "first", "added", "rounded", "done"))
        block = ctx.enter_context(nc.Block())

        @block.sync
        def _(sp):
            co.load(sp, st)

        @block.tensor
        def _(pe):
            co.multiply(pe, st, banks_free)

        @block.scalar
        def _(act):
            def read(i, c):
                act.wait_ge(added, 2 * i + c + 1)
                nc.scalar.activation(one(M[0], 2 * i + c), A[:, c], ACT.Copy).then_inc(rounded, 1)
            co.run(act, st, co.split_hi, read)

        @block.vector
        def _(dve):
            dve.sem_inc(banks_free, 2)

            def read(i, c):
                co.wait_units(dve, st, i, c)
                nc.vector.tensor_mul(A[:, c], one(co.PS, 2 * c), one(GT, 2 * i + c)).then_inc(first, 1)
                nc.vector.tensor_mul(B[:, c], one(co.PS, 2 * c + 1), one(GT, 8 + 2 * i + c)).then_inc(banks_free, 1)
                dve.wait_ge(banks_free, 2 + 2 * i + c + 1)
                nc.vector.tensor_add(A[:, c], A[:, c], B[:, c]).then_inc(added, 1)
                dve.wait_ge(rounded, 2 * i + c + 1)
                nc.vector.tensor_sub(one(M[1], 2 * i + c), A[:, c], one(M[0], 2 * i + c).bitcast(F32)).then_inc(done, 1)
            co.run(dve, st, co.split_lo, read)


def split_x(co):
    split_stage(co, [(co.X[:, c, :], co.Hh[:, c, :], co.Hl[:, c, :]) for c in range(DC)])


def hybrid_mixer(co, st, cols):
    nc = co.nc
    with ExitStack() as ctx:
        OH = co.sb("OH", [P, 4, S], F32R, ctx)
        OL = co.sb("OL", [P, 4, S], F32R, ctx)
        with ExitStack() as inner:
            QKV = co.sb("QKV", [P, 36, S], ctx=inner)
            MK = co.sb("MK", [P, MW], BF16, inner)
            IB = co.sb("IB", [P, P], BF16, inner)
            copy_stage(co, st["hin_qkv"], to_buffer(co, QKV))
            rotate(co, QKV)
            loaded, cast = co.sem("mask_loaded"), co.sem("ident_cast")
            with nc.Block() as block:
                @block.sync
                def _(sp):
                    sp.dma_start(MK[:].bitcast(mybir.dt.uint16), co.dram["mask"]).then_inc(loaded, 16)
                    sp.wait_ge(loaded, 16)

                @block.vector
                def _(dve):
                    nc.vector.tensor_copy(IB[:], co.ident).then_inc(cast, 1)
            every4 = lambda t: slice(t, None, 4)
            turn_values(co, [(QKV[:, 8:12, :], lambda t: slice(t * P, (t + 1) * P)), (QKV[:, 20:24, :], every4),
                             (QKV[:, 32:36, :], every4)])

            def score(x, ps):
                h, r = x
                c, p = h // 2, HD * (h % 2)
                q = lambda g: QKV[p:p + HD, 12 * g + c, r::4]
                k = lambda g: QKV[p:p + HD, 12 * g + 4 + c, :]
                mm = nc.tensor.matmul
                mm(ps[:, 0:S], q(0), k(0), start=True, stop=False)
                mm(ps[:, 0:S], IB[:], MK[:, 3 - r:3 - r + S], start=False, stop=True)
                mm(ps[:, S:S + P], q(1), k(1)[:, r::4], start=True, stop=False)
                mm(ps[:, S:S + P], IB[:], MK[:, WINDOW:WINDOW + P], start=False, stop=True)
                mm(ps[:, S + P:S + 2 * P], q(2), k(2)[:, r::4], start=True, stop=False)
                return mm(ps[:, S + P:S + 2 * P], IB[:], MK[:, WINDOW + P:WINDOW + 2 * P], start=False, stop=True)

            def value(x, t):
                h, r = x
                cs = slice(h * HD, (h + 1) * HD)
                return QKV[:, 8 + t, cs] if t < 4 else QKV[:, 20 + r if t == 4 else 32 + r, cs]

            def out_read(k):
                if k % 8 != 7:
                    return None
                c = k // 8
                back = lambda t: t[:, c, :].rearrange("p (q r) -> p r q", r=4)
                return back(OH), back(OL), co.PS[:, 6 + c % 2, :].rearrange("p (r q) -> p r q", r=4)
            attend(co, [(h, r) for h in range(8) for r in range(4)], score, lambda x: 6, value, 768, HD ** -0.5,
                   [0, 2], lambda x: (6 + x[0] // 2 % 2, HD * (x[0] % 2), slice(x[1] * P, (x[1] + 1) * P),
                                      x[0] // 2 - 1 if x[0] >= 4 and x[0] % 2 == 0 and x[1] == 0 else None), out_read)
        GT = co.sb("GT", [P, 16, S], ctx=ctx)
        CH = co.sb("CH", [P, 4, S], F32R, ctx)
        CL = co.sb("CL", [P, 4, S], F32R, ctx)
        with ExitStack() as inner:
            U = co.sb("conv_u", [P, 4, S + TAPS - 1], ctx=inner)
            CV = co.sb("conv_v", [P, 4, S], ctx=inner)
            zeroed = co.sem("conv_zeroed")
            nc.gpsimd.memset(U[:, :, 0:TAPS - 1], 0.0).then_inc(zeroed, 1)
            copy_stage(co, st["hin_b"], to_buffer(co, CV, ACT.Sigmoid))
            copy_stage(co, st["hin_a"], lambda i, c: ("dve", lambda ps: nc.vector.tensor_mul(U[:, c:c + 1, TAPS - 1:], ps, one(CV, c))))
            gates_and_conv(co, st["hin_gate"], GT, U, CV, cols)
            norm_stage(co, 4, cols["conv2_g"], CV, LN_EPS, center=True, bias=cols["conv2_lb"], src=CV)
            silu_split(co, CV, (CH, CL))
        for j, u in enumerate(st["hao"].units):
            u.x = (OH, OL) if j % 2 == 0 else (CH, CL)
        M = (co.sb("hybrid_mh", [P, DC, S], F32R, ctx), co.sb("hybrid_ml", [P, DC, S], F32R, ctx))
        merge(co, st["hao"], GT, M)
        for u in st["ho"].units:
            u.x = M
        add_stage(co, st["ho"], ALPHA, None, split=False)
    norm_stage(co, DC, cols["ln1_g"], co.X, LN_EPS, center=True, bias=cols["ln1_b"])

def finish(co):
    nc, d = co.nc, co.dram
    stored = co.sem("stored")
    with nc.Block() as block:
        @block.sync
        def _(sp):
            sp.dma_start(d["out"].rearrange("(c p) s -> p c s", p=P), co.X[:]).then_inc(stored, 16)
            sp.wait_ge(stored, 16)


def program(nc, dram, cols):
    with ExitStack() as ctx:
        main(Core(nc, ctx, dram), cols)


def main(co, cols):
    first = plan_ffn(co, 0)
    even = plan_even(co)
    second = plan_ffn(co, 1)
    third = plan_ffn(co, 2)
    odd = plan_odd(co)
    fourth = plan_ffn(co, 3)
    hybrid = plan_hybrid(co)
    last = plan_ffn(co, 4)
    enter(co, cols["ffn1_norm0"])
    ffn(co, *first, 0.5, 1.0, cols["mix_norm0"])
    even_mixer(co, even, cols, cols["ffn2_norm0"])
    ffn(co, *second, 0.5, 1.0, cols["ffn1_norm1"])
    ffn(co, *third, 0.5, 1.0, cols["mix_norm1"])
    odd_mixer(co, odd, cols, cols["ffn2_norm1"])
    ffn(co, *fourth, 0.5, 1.0, None)
    hybrid_mixer(co, hybrid, cols)
    split_x(co)
    ffn(co, *last, 1.0, ALPHA, None, normed=False, split=False)
    norm_stage(co, DC, cols["ln2_g"], co.X, LN_EPS, center=True, bias=cols["ln2_b"])
    finish(co)


def blocked(w):
    k, n = w.shape
    return np.ascontiguousarray(w.reshape(k // P, P, n // P, P).transpose(2, 1, 0, 3).reshape(n // P, P, k))


def halves(w):
    b = blocked(w)
    return np.ascontiguousarray(b.reshape(b.shape[0], P, 2, HALF * P).transpose(0, 2, 1, 3).reshape(-1, P, HALF * P))


def pair(a, b):
    a, b = blocked(a), blocked(b)
    return np.ascontiguousarray(np.stack([a, b], 1).reshape(-1, *a.shape[1:]))


def constants():
    f = np.float32
    p, q = np.arange(P)[:, None], np.arange(P)[None, :]
    rot = np.zeros((P, P), f)
    for m in range(P):
        rot[m + 32 if m % 64 < 32 else m - 32, m] = -1 if m % 64 < 32 else 1
    mats = np.concatenate([p == q, q >= p, p + q == P - 1, rot, p // 64 == q // 64], 1).astype(f)
    sel8 = (np.arange(8)[:, None] == np.arange(8 * P)[None, :] // P).astype(f)
    tokens = np.concatenate([np.arange(32), 32 * np.arange(16)]).astype(f)
    small = {
        "sign": np.where(p < 64, 1, -1).astype(f), "half_pi": np.full((P, 1), np.pi / 2, f),
        "tokens": np.tile(tokens, (P, 1)), "pair": (p // 16 % 2 == np.arange(2)[None]).astype(f),
    }
    return mats, sel8, small


def lay_out(v):
    a, cols, parts = {}, {}, []

    def col(name, m):
        cols[name] = sum(x.shape[1] for x in parts)
        parts.append(np.asarray(m))

    def vec(name, x):
        col(name, np.reshape(x, (-1, P)).T)

    def rows8(name, x):
        col(name, np.concatenate([np.reshape(x, (-1, 1)), np.zeros((P - 8, 1), np.float32)]))

    ffns = [("ffn1", "", 0), ("ffn2", "", 0), ("ffn1", "", 1), ("ffn2", "", 1)]
    for n, (f, _, l) in enumerate(ffns):
        a[f"gu{n}"] = pair(v[f + "_w_gate"][l], v[f + "_w_up"][l])
        a[f"dn{n}"] = halves(v[f + "_w_down"][l])
    a["gu4"] = pair(v["w_ffn_gate_2"][0], v["w_ffn_up_2"][0])
    a["dn4"] = halves(v["w_ffn_down_2"][0])
    for l in range(2):
        for f in ("ffn1_norm", "mix_norm", "ffn2_norm"):
            vec(f"{f}{l}", v[f][l])
    w = v["even_w_in"][0]
    a["ein_zx"] = blocked(w[:, 0:1536])
    dt = np.concatenate([w[:, 1536:1544], np.zeros((D, P - 8), np.float32)], 1)
    a["ein_dt"] = np.ascontiguousarray(blocked(dt).reshape(P, RAW, 2 * P).transpose(1, 0, 2))
    a["ein_u"] = blocked(w[:, 1544:])
    a["glu"] = blocked(v["s5_w_glu"][0])
    a["eout"] = blocked(v["even_w_out"][0])
    vec("conv_w", v["ssd_conv_w"][0])
    vec("conv_b", v["ssd_conv_b"][0])
    rows8("dt_bias", v["ssd_dt_bias"][0])
    rows8("a_log", v["ssd_a_log"][0])
    vec("ssd_d", np.repeat(v["ssd_d"][0], HD))
    vec("ssd_norm", v["ssd_norm"][0])
    vec("s5_d", v["s5_d"][0])
    vec("b_glu", v["s5_b_glu"][0])
    twice = lambda x: np.concatenate([x, x], 0)
    a["s5p"] = np.concatenate([twice(v["s5_a_re"][0].T), twice(v["s5_a_im"][0].T),
                               np.tile(v["s5_log_dt"][0][None], (P, 1))], 1)
    br, bi = (v[n][0].transpose(1, 0, 2).reshape(64, -1) for n in ("s5_b_re", "s5_b_im"))
    cr, ci = (v[n][0].transpose(2, 0, 1).reshape(64, -1) for n in ("s5_c_re", "s5_c_im"))
    a["s5b"] = np.concatenate([np.concatenate([br, bi], 0), np.concatenate([bi, br], 0)], 1)
    a["s5c"] = np.concatenate([np.concatenate([cr, ci], 0), np.concatenate([ci, cr], 0)], 1)
    a["oin"] = blocked(v["odd_w_in"][0])
    a["oout"] = blocked(v["odd_w_out"][0])
    b = v["attn_rel_bias"][0]
    a["hankel"] = np.concatenate([np.repeat(b[:, 256:], 383, 1), b[:, :0:-1], b[:, :1]], 1)
    a["pool_w"] = v["pool_w"][0]
    vec("q_gain", np.tile(v["attn_q_norm"][0], 2))
    vec("k_gain", np.tile(v["attn_k_norm"][0], 2))
    vec("pool_scale", v["pool_scale"][0])
    frames = 1 / np.minimum(np.arange(1, 17)[None], np.array([2, 4, 8, 16])[:, None]).astype(np.float32)
    a["counts"] = np.tile(frames.reshape(1, -1), (P, 1))
    a["hankel_sel"] = (np.arange(16)[:, None] == np.arange(8 * P)[None, :] // HD).astype(np.float32)
    a["counts_mask"] = np.concatenate([np.where(np.arange(P) < 64, NEG, 0), np.ones(64)]).astype(np.float32)[None]
    w = v["w_in_2"][0]
    q = 9 * S
    a["hin_qkv"] = blocked(w[:, 0:q])
    a["hin_a"], a["hin_b"] = blocked(w[:, q:q + S]), blocked(w[:, q + S:q + 2 * S])
    a["hin_gate"] = blocked(w[:, q + 2 * S:])
    a["hao"] = pair(v["w_attn_out_2"][0], v["w_conv_out_2"][0])
    a["ho"] = blocked(v["w_o_2"][0])
    col("conv2_w", v["conv_w_2"][0].reshape(TAPS, 4, P).transpose(2, 1, 0).reshape(P, -1))
    for n, x in (("conv2_b", "conv_b_2"), ("conv2_g", "conv_ln_g_2"), ("conv2_lb", "conv_ln_b_2"), ("ln1_g", "ln1_g_2"),
                 ("ln1_b", "ln1_b_2"), ("ln2_g", "ln2_g_2"), ("ln2_b", "ln2_b_2")):
        vec(n, v[x][0])
    f = np.float32
    inv = (1.0 / (f(10000.0) ** (np.arange(0, HD, 2, dtype=f) / f(HD)))).astype(f)
    ang = np.arange(S, dtype=f)[None] * np.tile(inv, 4)[:, None]
    a["rope"] = np.concatenate([np.cos(ang), np.sin(ang)], 1).astype(f)
    at = np.arange(P)[:, None]
    ago = 4 * at + 3 - np.arange(WINDOW)[None]
    near = (ago >= 0) & (ago <= P)
    back = at - at.T
    ok = np.concatenate([near, back >= 0, (back >= 0) & (back % 4 == 0)], 1)
    a["mask"] = (np.where(ok, 0, NEG).astype(f).view(np.uint32) >> 16).astype(np.uint16)
    mats, a["sel8"], small = constants()
    a["mats"] = mats
    for n, x in small.items():
        col(n, x)
    a["cols"] = np.concatenate(parts, 1)
    a["xT"] = v["x"][0].T
    return {n: np.ascontiguousarray(x) for n, x in a.items()}, cols


def kernel(**inputs):
    import concourse.bacc as _bacc
    from concourse.bass_utils import run_bass_kernel_spmd as _run

    v = {k: np.asarray(x) for k, x in inputs.items()}
    arrays, cols = lay_out(v)
    nc = _bacc.Bacc("TRN2", target_bir_lowering=False, num_devices=1)
    dram = {n: nc.dram_tensor("in_" + n, a.shape, mybir.dt.from_np(a.dtype), kind="ExternalInput").ap()
            for n, a in arrays.items()}
    dram["out"] = nc.dram_tensor("out_xT", (D, S), F32, kind="ExternalOutput").ap()
    program(nc, dram, cols)
    r = _run(nc, [{"in_" + n: a for n, a in arrays.items()}], core_ids=[0])
    return np.ascontiguousarray(r.results[0]["out_xT"].T).reshape(1, S, D)
```

```python
from contextlib import ExitStack

import numpy as np

import concourse.bass as bass
from concourse import mybir

F32 = mybir.dt.float32
F32R = mybir.dt.float32r
BF16 = mybir.dt.bfloat16
ALU = mybir.AluOpType
ACT = mybir.ActivationFunctionType
AX = mybir.AxisListType

P = 128
S = 512
D = 1024
DC = D // P
FF = 2816
FC = FF // P
HALF = FC // 2
EPS = 1e-6
LN_EPS = 1e-5
RAW = 4
SPLIT = 2
TT = S // P
HD = 64
NEG = -1e30
MAGIC = 1.5 * 2.0 ** 23
S5G = 32


class Unit:

    def __init__(self, kc, src, x, k0, bank, start=True, stop=True):
        self.kc, self.src, self.x, self.k0 = kc, src, x, k0
        self.bank, self.start, self.stop = bank, start, stop


class Stage:

    def __init__(self, bodies, units, chunks, banks):
        self.bodies, self.units, self.chunks, self.banks = bodies, units, chunks, banks
        self.base = None


class StageSems(ExitStack):

    def __init__(self):
        super().__init__()
        self.handles = []

    def enter_context(self, made):
        self.handles.append(super().enter_context(made))
        return self.handles[-1]


def stage(f):
    def run(co, *args, **kwargs):
        co.begin()
        f(co, *args, **kwargs)
        co.end()
    return run


class Core:

    def __init__(self, nc, ctx, dram):
        self.nc, self.ctx, self.dram = nc, ctx, dram
        self.n = 0
        self.stage_sems, self.retired, self.clearing = None, [], []
        self.X = self.sb("X", [P, DC, S])
        self.Hh = self.sb("Hh", [P, DC, S], F32R)
        self.Hl = self.sb("Hl", [P, DC, S], F32R)
        self.raw = [self.sb(f"raw{j}", [P, HALF * P]) for j in range(RAW)]
        self.wh = [self.sb(f"wh{j}", [P, HALF * P], F32R) for j in range(SPLIT)]
        self.wl = [self.sb(f"wl{j}", [P, HALF * P], F32R) for j in range(SPLIT)]
        self.RS = self.sb("RS", [P, S])
        self.SS = self.sb("SS", [P, S])
        self.ones = self.sb("ones", [P, P])
        self.cols = self.sb("cols", [P, dram["cols"].shape[1]])
        self.mats = self.sb("mats", [P, 4, P])
        self.ident, self.triu, self.flip, self.heads = (self.mats[:, k, :] for k in range(4))
        self.PS = ctx.enter_context(nc.psum_tensor("PS", [P, 8, 512], F32))
        self.raw_in = [self.sem(f"raw_in{j}") for j in range(RAW)]
        self.hi_ready = self.sem("hi_ready")
        self.lo_ready = self.sem("lo_ready")
        self.unit_done = self.sem("unit_done")
        self.stages = []

    def sb(self, name, shape, dt=F32, ctx=None):
        return (ctx or self.ctx).enter_context(self.nc.sbuf_tensor(name, shape, dt))

    def sem(self, name):
        return (self.stage_sems or self.ctx).enter_context(self.nc.semaphore(self.tag(name)))

    def begin(self):
        for done in self.clearing:
            done.close()
        self.clearing = self.retired
        self.retired = []
        for done in self.clearing:
            for s in done.handles:
                self.nc.gpsimd.sem_clear(s)
        self.stage_sems = StageSems()

    def end(self):
        self.retired.append(self.stage_sems)
        self.stage_sems = None

    def tag(self, name):
        self.n += 1
        return f"{name}_{self.n}"

    def plan(self, stage):
        stage.base = self.stages[-1].base + RAW * self.stages[-1].bodies if self.stages else 0
        self.stages.append(stage)
        return stage

    def load_turn(self, sp, st, i):
        for j, u in enumerate(st.units):
            at = st.base + RAW * i + j
            if not (isinstance(at, int) and at < RAW):
                sp.wait_ge(self.lo_ready, at + 1 - RAW)
            sp.dma_start(self.raw[j][:, 0:u.kc * P], u.src(i)).then_inc(self.raw_in[j], 16)

    def load(self, sp, st):
        if st.bodies > 1:
            with sp.Fori(1, st.bodies) as i:
                self.load_turn(sp, st, i)
        k = self.stages.index(st)
        if k + 1 < len(self.stages):
            self.load_turn(sp, self.stages[k + 1], 0)

    def split_hi(self, act, st, i, j):
        kw = st.units[j].kc * P
        act.wait_ge(self.raw_in[j], 16 * (st.base // RAW + 1) + 16 * i)
        act.wait_ge(self.unit_done, st.base + j + 1 + RAW * i)
        self.nc.scalar.activation(self.wh[j % SPLIT][:, 0:kw], self.raw[j][:, 0:kw], ACT.Copy).then_inc(self.hi_ready, 1)

    def split_lo(self, dve, st, i, j):
        kw = st.units[j].kc * P
        dve.wait_ge(self.hi_ready, st.base + j + 1 + RAW * i)
        self.nc.vector.tensor_sub(self.wl[j % SPLIT][:, 0:kw], self.raw[j][:, 0:kw],
                                  self.wh[j % SPLIT][:, 0:kw].bitcast(F32)).then_inc(self.lo_ready, 1)

    def multiply(self, pe, st, bank_free, operand=None, after=0):
        per = RAW // st.chunks

        def turn(i):
            for j, u in enumerate(st.units):
                if j % per == 0:
                    pe.wait_ge(bank_free, after + st.chunks * i + j // per + 1)
                pe.wait_ge(self.lo_ready, st.base + j + 1 + RAW * i)
                if operand:
                    pe.wait_ge(operand[0], operand[1][j])
                xh, xl = u.x
                out = self.PS[:, u.bank, :]
                for k in range(u.kc):
                    wh = self.wh[j % SPLIT][:, k * P:(k + 1) * P]
                    wl = self.wl[j % SPLIT][:, k * P:(k + 1) * P]
                    first, last = u.start and k == 0, u.stop and k == u.kc - 1
                    self.nc.tensor.matmul(out, wl, xh[:, u.k0 + k, :], start=first, stop=False)
                    self.nc.tensor.matmul(out, wh, xh[:, u.k0 + k, :], start=False, stop=False)
                    done = self.nc.tensor.matmul(out, wh, xl[:, u.k0 + k, :], start=False, stop=last)
                done.then_inc(self.unit_done, 1)
        if st.bodies > 1:
            with pe.Fori(0, st.bodies) as i:
                turn(i)
        else:
            turn(0)

    def wait_units(self, eng, st, i, c, part=None):
        per = RAW // st.chunks
        j = c * per + (per - 1 if part is None else part)
        eng.wait_ge(self.unit_done, SPLIT + st.base + j + 1 + RAW * i)

    def run(self, eng, st, split, read, early=None):
        per = RAW // st.chunks

        def turn(i, first):
            for c in range(st.chunks):
                for j in range(c * per, (c + 1) * per):
                    if not (first and j < SPLIT):
                        split(eng, st, i, j)
                if c > 0:
                    read(i, c - 1)
                elif not first:
                    read(i - 1, st.chunks - 1)
                elif early:
                    early()
        turn(0, True)
        if st.bodies > 1:
            with eng.Fori(1, st.bodies) as i:
                turn(i, False)
        k = self.stages.index(st)
        if k + 1 < len(self.stages):
            for j in range(SPLIT):
                split(eng, self.stages[k + 1], 0, j)
        read(st.bodies - 1, st.chunks - 1)


def one(t, n, k=None):
    return t[:, bass.ds(n, 1), :]



@stage
def layer_norm(co, src, n, gain, bias, totals=False, silu=False, parts=None, store=None):
    nc = co.nc
    name = co.tag("ln")
    width = n * P
    with ExitStack() as ctx:
        SQ = co.sb(f"{name}_sq", [P, n, S], ctx=ctx)
        MR = co.sb(f"{name}_mr", [P, 2, S], ctx=ctx)
        mean, root = MR[:, 0, :], MR[:, 1, :]
        summed, meaned, centered, squared, scaled, rooted, normed, biased, rounded, parted, stored = (
            co.sem(f"{name}_{s}") for s in ("summed", "meaned", "centered", "squared", "scaled", "rooted", "normed",
                                            "biased", "rounded", "parted", "stored"))
        block = ctx.enter_context(nc.Block())

        @block.tensor
        def _(pe):
            if totals:
                m = nc.tensor.matmul(co.PS[:, 1, :], co.ones[:], co.SS[:], start=True, stop=True)
            else:
                for c in range(n):
                    m = nc.tensor.matmul(co.PS[:, 1, :], co.ones[:], src[:, c, :], start=c == 0, stop=c == n - 1)
            m.then_inc(summed, 1)
            for c in range(n):
                pe.wait_ge(squared, c + 1)
                m = nc.tensor.matmul(co.PS[:, 0, :], co.ones[:], SQ[:, c, :], start=c == 0, stop=c == n - 1)
            m.then_inc(summed, 1)

        @block.scalar
        def _(act):
            for c in range(n):
                act.wait_ge(centered, c + 1)
                nc.scalar.activation(SQ[:, c, :], src[:, c, :], ACT.Square).then_inc(squared, 1)
            act.wait_ge(scaled, 1)
            nc.scalar.activation(root, root, ACT.Sqrt).then_inc(rooted, 1)
            for c in range(n + 1):
                if c < n:
                    act.wait_ge(normed, c + 1)
                    nc.scalar.activation(src[:, c, :], src[:, c, :], ACT.Silu if silu else ACT.Identity,
                                         bias=co.cols[:, bias + c:bias + c + 1]).then_inc(biased, 1)
                if parts and c > 0:
                    act.wait_ge(biased, c)
                    nc.scalar.activation(parts[0][:, c - 1, :], src[:, c - 1, :], ACT.Copy).then_inc(rounded, 1)

        @block.vector
        def _(dve):
            def part(c):
                dve.wait_ge(rounded, c + 1)
                nc.vector.tensor_sub(parts[1][:, c, :], src[:, c, :], parts[0][:, c, :].bitcast(F32)).then_inc(parted, 1)
            dve.wait_ge(summed, 1)
            nc.vector.tensor_scalar(mean, co.PS[:, 1, :], 1.0 / width, None, ALU.mult).then_inc(meaned, 1)
            dve.wait_ge(meaned, 1)
            for c in range(n):
                nc.vector.tensor_sub(src[:, c, :], src[:, c, :], mean).then_inc(centered, 1)
            dve.wait_ge(summed, 2)
            nc.vector.tensor_scalar(root, co.PS[:, 0, :], 1.0 / width, LN_EPS, ALU.mult, ALU.add).then_inc(scaled, 1)
            dve.wait_ge(rooted, 1)
            nc.vector.reciprocal(root, root).then_inc(scaled, 1)
            dve.wait_ge(scaled, 2)
            dve.wait_ge(centered, n)
            for c in range(n):
                nc.vector.scalar_tensor_tensor(src[:, c, :], src[:, c, :], co.cols[:, gain + c:gain + c + 1], root,
                                               ALU.mult, ALU.mult).then_inc(normed, 1)
                if parts and c >= 2:
                    part(c - 2)
            if parts:
                part(n - 2)
                part(n - 1)

        if store is not None:
            @block.sync
            def _(sp):
                for c in range(n):
                    sp.wait_ge(biased, c + 1)
                    sp.dma_start(store[c * P:(c + 1) * P, :], src[:, c, :]).then_inc(stored, 16)
                sp.wait_ge(stored, 16 * n)



def feed(co, name, x=None):
    w = co.dram[name]
    x = x or (co.Hh, co.Hl)
    kc = w.shape[2] // P
    return co.plan(Stage(w.shape[0] // RAW, [
        Unit(kc, lambda i, j=j: w[bass.ds(RAW * i + j, 1)].rearrange("o p n -> p (o n)"), x, 0, j) for j in range(RAW)
    ], RAW, 4))


@stage
def copy_stage(co, st, reads, scaled=False, loads=()):
    nc = co.nc
    name = co.tag("copy")
    bank_free = co.sem(f"{name}_bank_free")
    arrived = co.sem(f"{name}_arrived")
    scale = Scale(co) if scaled else None
    with nc.Block() as block:
        @block.sync
        def _(sp):
            for to, src in loads:
                sp.dma_start(to, src).then_inc(arrived, 16)
            co.load(sp, st)
            if loads:
                sp.wait_ge(arrived, 16 * len(loads))

        @block.tensor
        def _(pe):
            if scaled:
                scale.pe(pe)
            co.multiply(pe, st, bank_free)

        @block.scalar
        def _(act):
            act.sem_inc(bank_free, 4)

            def read(i, c):
                if reads and reads(i, c)[0] == "act":
                    co.wait_units(act, st, i, c)
                    reads(i, c)[1](one(co.PS, c)).then_inc(bank_free, 1)
            co.run(act, st, co.split_hi, read, (lambda: scale.act(act)) if scaled else None)

        @block.vector
        def _(dve):
            def read(i, c):
                if reads and reads(i, c)[0] == "dve":
                    co.wait_units(dve, st, i, c)
                    reads(i, c)[1](one(co.PS, c)).then_inc(bank_free, 1)
            co.run(dve, st, co.split_lo, read, (lambda: scale.dve(dve)) if scaled else None)


def plan_ffn(co, k):
    gu, dn = co.dram[f"gu{k}"], co.dram[f"dn{k}"]
    x = (co.Hh, co.Hl)
    up = co.plan(Stage(FC // 2, [
        Unit(DC, lambda i, j=j: gu[bass.ds(RAW * i + j, 1)].rearrange("o p n -> p (o n)"), x, 0, j) for j in range(RAW)
    ], 2, 2))
    down = co.plan(Stage(DC // 2, [
        Unit(HALF, lambda i, j=j: dn[bass.ds(RAW * i + j, 1)].rearrange("o p n -> p (o n)"), None, HALF * (j % 2),
             4 + j // 2, j % 2 == 0, j % 2 == 1) for j in range(RAW)
    ], 2, 2))
    return up, down


class Residual:

    def __init__(self, co, ctx, st, banks, alpha, beta, gain, T=None, SQ=None, split=True,
                 totals=False):
        name = co.tag("res")
        self.totals = totals
        self.co, self.st, self.banks, self.alpha, self.beta, self.gain, self.split = co, st, banks, alpha, beta, gain, split
        self.T = T or co.sb(f"{name}_t", [P, 2, 1, S], ctx=ctx)
        self.SQ = SQ or co.sb(f"{name}_sq", [P, 2, 1, S], ctx=ctx)
        self.bank_free, self.updated, self.gained, self.rounded, self.squared, self.added, self.parted = (
            co.sem(f"{name}_{s}") for s in ("bank_free", "updated", "gained", "rounded", "squared", "added", "parted"))

    def dve(self, dve, i, c):
        co, v = self.co, self.co.nc.vector
        n = self.st.chunks * i + c
        co.wait_units(dve, self.st, i, c)
        x, ps = one(co.X, n), one(co.PS, self.banks + c)
        a, b = (x, ps) if self.beta == 1.0 else (ps, x)
        v.scalar_tensor_tensor(x, a, self.alpha * self.beta, b, ALU.mult, ALU.add).then_inc(self.bank_free, 1)
        if self.split:
            dve.wait_ge(self.bank_free, self.st.banks + n + 1)
            if self.gain is None:
                t = x
            else:
                t = self.T[:, c % 2]
                v.tensor_scalar(t, x, co.cols[:, bass.ds(self.gain + n, 1)], None, ALU.mult).then_inc(self.gained, 1)
            dve.wait_ge(self.rounded, n + 1)
            v.tensor_sub(one(co.Hl, n), t, one(co.Hh, n).bitcast(F32)).then_inc(self.parted, 1)

    def act(self, act, i, c):
        co = self.co
        n = self.st.chunks * i + c
        if self.split:
            if self.gain is None:
                act.wait_ge(self.bank_free, self.st.banks + n + 1)
            else:
                act.wait_ge(self.gained, n + 1)
            t = one(co.X, n) if self.gain is None else self.T[:, c % 2]
            co.nc.scalar.activation(one(co.Hh, n), t, ACT.Copy).then_inc(self.rounded, 1)
        if self.gain is not None:
            act.wait_ge(self.added, n + 1)
            co.nc.scalar.activation(self.SQ[:, c % 2], one(co.X, n), ACT.Square).then_inc(self.squared, 1)

    def pool(self, pool):
        co = self.co
        if self.totals:
            co.nc.gpsimd.memset(co.SS[:], 0.0).then_inc(self.added, 1)
            with pool.Fori(0, self.st.bodies) as i:
                for c in range(self.st.chunks):
                    n = self.st.chunks * i + c
                    pool.wait_ge(self.bank_free, self.st.banks + n + 1)
                    pool.wait_ge(self.added, n + 1)
                    co.nc.gpsimd.tensor_add(co.SS[:].unsqueeze(1), co.SS[:].unsqueeze(1), one(co.X, n)).then_inc(self.added, 1)
        if self.gain is None:
            return
        pool.sem_inc(self.added, 1)
        co.nc.gpsimd.memset(co.SS[:], 0.0).then_inc(self.added, 1)
        st = self.st

        def turn(i):
            for c in range(st.chunks):
                n = st.chunks * i + c
                pool.wait_ge(self.squared, n + 1)
                pool.wait_ge(self.added, n + 2)
                co.nc.gpsimd.tensor_add(co.SS[:].unsqueeze(1), co.SS[:].unsqueeze(1), self.SQ[:, c % 2]).then_inc(self.added, 1)
        with pool.Fori(0, st.bodies) as i:
            turn(i)


class Scale:

    def __init__(self, co):
        name = co.tag("scale")
        self.co = co
        self.summed, self.meaned, self.rooted, self.ready = (
            co.sem(f"{name}_{s}") for s in ("summed", "meaned", "rooted", "ready"))

    def pe(self, pe):
        co = self.co
        co.nc.tensor.matmul(co.PS[:, 7, :], co.ones[:], co.SS[:], start=True, stop=True).then_inc(self.summed, 1)

    def act(self, act):
        act.wait_ge(self.meaned, 1)
        self.co.nc.scalar.activation(self.co.RS[:], self.co.RS[:], ACT.Sqrt).then_inc(self.rooted, 1)

    def dve(self, dve):
        co = self.co
        dve.wait_ge(self.summed, 1)
        co.nc.vector.tensor_scalar(co.RS[:], co.PS[:, 7, :], 1.0 / D, EPS, ALU.mult, ALU.add).then_inc(self.meaned, 1)
        dve.wait_ge(self.rooted, 1)
        co.nc.vector.reciprocal(co.RS[:], co.RS[:]).then_inc(self.ready, 1)
        dve.wait_ge(self.ready, 1)


def rs1(co):
    return co.RS[:].unsqueeze(1)


@stage
def ffn(co, up, down, half, alpha, gain, normed=True, split=True, totals=False):
    nc = co.nc
    assert half == 1.0 or alpha == 1.0
    with ExitStack() as ctx:
        name = co.tag("ffn")
        Gh = co.sb(f"{name}_gh", [P, FC, S], F32R, ctx)
        Gl = co.sb(f"{name}_gl", [P, FC, S], F32R, ctx)
        SG = co.sb(f"{name}_sg", [P, 2, 1, S], ctx=ctx)
        T = co.sb(f"{name}_t", [P, 2, 1, S], ctx=ctx)
        UR = co.sb(f"{name}_ur", [P, 2, 1, S], ctx=ctx)
        for u in down.units:
            u.x = (Gh, Gl)
        gate_read, banks_free, gated, product, rounded, g_ready = (
            co.sem(f"{name}_{s}") for s in ("gate_read", "banks_free", "gated", "product", "rounded", "g_ready"))
        scale = Scale(co) if normed else None
        res = Residual(co, ctx, down, 4, alpha, half, gain, T=T, SQ=SG, split=split, totals=totals)
        block = ctx.enter_context(nc.Block())

        @block.sync
        def _(sp):
            co.load(sp, up)
            co.load(sp, down)

        @block.tensor
        def _(pe):
            if normed:
                scale.pe(pe)
            co.multiply(pe, up, banks_free)
            co.multiply(pe, down, res.bank_free, (g_ready, [HALF, FC] * 2))

        @block.gpsimd
        def _(pool):
            if normed:
                pool.wait_ge(scale.summed, 1)
            res.pool(pool)

        @block.scalar
        def _(act):
            def read(i, c):
                n = 2 * i + c
                if normed:
                    act.wait_ge(gate_read, n + 1)
                    nc.scalar.activation(SG[:, c], SG[:, c], ACT.Silu).then_inc(gated, 1)
                else:
                    co.wait_units(act, up, i, c, 0)
                    nc.scalar.activation(SG[:, c], one(co.PS, 2 * c), ACT.Silu).then_inc(gated, 1)
                act.wait_ge(*((product, n + 1) if normed else (banks_free, 2 + n + 1)))
                nc.scalar.activation(one(Gh, n), T[:, c], ACT.Copy).then_inc(rounded, 1)
            co.run(act, up, co.split_hi, read, (lambda: scale.act(act)) if normed else None)
            co.run(act, down, co.split_hi, lambda i, c: res.act(act, i, c))

        @block.vector
        def _(dve):
            dve.sem_inc(banks_free, 2)
            dve.sem_inc(res.bank_free, 2)

            def read(i, c):
                n = 2 * i + c
                if normed:
                    co.wait_units(dve, up, i, c, 0)
                    nc.vector.tensor_mul(SG[:, c], one(co.PS, 2 * c), rs1(co)).then_inc(gate_read, 1)
                    co.wait_units(dve, up, i, c, 1)
                    nc.vector.tensor_mul(UR[:, c], one(co.PS, 2 * c + 1), rs1(co)).then_inc(banks_free, 1)
                    dve.wait_ge(gated, n + 1)
                    dve.wait_ge(banks_free, 2 + n + 1)
                    nc.vector.tensor_mul(T[:, c], UR[:, c], SG[:, c]).then_inc(product, 1)
                else:
                    co.wait_units(dve, up, i, c, 1)
                    dve.wait_ge(gated, n + 1)
                    nc.vector.tensor_mul(T[:, c], one(co.PS, 2 * c + 1), SG[:, c]).then_inc(banks_free, 1)
                dve.wait_ge(rounded, n + 1)
                nc.vector.tensor_sub(one(Gl, n), T[:, c], one(Gh, n).bitcast(F32)).then_inc(g_ready, 1)
            co.run(dve, up, co.split_lo, read, (lambda: scale.dve(dve)) if normed else None)
            co.run(dve, down, co.split_lo, lambda i, c: res.dve(dve, i, c))


@stage
def add_stage(co, st, alpha, gain, split=True, totals=False):
    nc = co.nc
    with ExitStack() as ctx:
        res = Residual(co, ctx, st, 0, alpha, 1.0, gain, split=split, totals=totals)
        block = ctx.enter_context(nc.Block())

        @block.sync
        def _(sp):
            co.load(sp, st)

        @block.tensor
        def _(pe):
            co.multiply(pe, st, res.bank_free)

        @block.gpsimd
        def _(pool):
            res.pool(pool)

        @block.scalar
        def _(act):
            co.run(act, st, co.split_hi, lambda i, c: res.act(act, i, c))

        @block.vector
        def _(dve):
            dve.sem_inc(res.bank_free, 4)
            co.run(dve, st, co.split_lo, lambda i, c: res.dve(dve, i, c))


@stage
def enter(co, gain):
    nc, d = co.nc, co.dram
    st = co.stages[0]
    with ExitStack() as ctx:
        T = co.sb("enter_t", [P, DC, S], ctx=ctx)
        SQ = co.sb("enter_sq", [P, DC, S], ctx=ctx)
        loaded, gained, rounded, squared, added, parted = (co.sem(f"enter_{s}") for s in (
            "loaded", "gained", "rounded", "squared", "added", "parted"))
        arrived = [co.sem(f"enter_arrived{c}") for c in range(DC)]
        block = ctx.enter_context(nc.Block())

        @block.sync
        def _(sp):
            sp.dma_start(co.cols[:], d["cols"]).then_inc(loaded, 16)
            for c in range(DC):
                sp.dma_start(co.X[:, c, :], d["xT"][c * P:(c + 1) * P, :]).then_inc(arrived[c], 16)
                if c == 3:
                    co.load_turn(sp, st, 0)
            sp.wait_ge(loaded, 16)
            sp.dma_start(co.mats[:], d["mats"].rearrange("p (k n) -> p k n", n=P)).then_inc(loaded, 16)
            sp.wait_ge(loaded, 32)

        @block.gpsimd
        def _(pool):
            nc.gpsimd.memset(co.ones[:], 1.0).then_inc(added, 1)
            nc.gpsimd.memset(co.SS[:], 0.0).then_inc(added, 1)
            for c in range(DC):
                pool.wait_ge(squared, c + 1)
                pool.wait_ge(added, c + 2)
                nc.gpsimd.tensor_add(co.SS[:], co.SS[:], SQ[:, c]).then_inc(added, 1)

        @block.tensor
        def _(pe):
            pe.sem_inc(co.unit_done, SPLIT)

        @block.scalar
        def _(act):
            for c in range(DC):
                act.wait_ge(arrived[c], 16)
                nc.scalar.activation(SQ[:, c], co.X[:, c], ACT.Square).then_inc(squared, 1)
                act.wait_ge(gained, c + 1)
                nc.scalar.activation(co.Hh[:, c], T[:, c], ACT.Copy).then_inc(rounded, 1)
                if c in (DC - 3, DC - 2):
                    co.split_hi(act, st, 0, c - (DC - 3))

        @block.vector
        def _(dve):
            dve.wait_ge(loaded, 16)
            for c in range(DC):
                dve.wait_ge(arrived[c], 16)
                nc.vector.tensor_scalar(T[:, c], co.X[:, c], co.cols[:, gain + c:gain + c + 1], None, ALU.mult).then_inc(gained, 1)
                if c > 0:
                    dve.wait_ge(gained, c)
                    dve.wait_ge(rounded, c)
                    nc.vector.tensor_sub(co.Hl[:, c - 1], T[:, c - 1], co.Hh[:, c - 1].bitcast(F32)).then_inc(parted, 1)
            for j in range(SPLIT):
                co.split_lo(dve, st, 0, j)
            dve.wait_ge(gained, DC)
            dve.wait_ge(rounded, DC)
            nc.vector.tensor_sub(co.Hl[:, DC - 1], T[:, DC - 1], co.Hh[:, DC - 1].bitcast(F32)).then_inc(parted, 1)



SSD_H = 8
OFF = [0, 512, 896, 1152]
TRI = 1280


class StepSizes:

    def __init__(self, co, DT, AT, W, cols):
        self.co, self.DT, self.AT, self.W, self.cols = co, DT, AT, W, cols
        self.ready, self.exped, self.pooled, self.filled = (
            co.sem(f"dt_{s}") for s in ("ready", "exped", "pooled", "filled"))
        self.steps = 0
        self.rows = [W[:, n, :] for n in range(6)]

    def step(self, dve, ins):
        self.steps += 1
        ins.then_inc(self.ready, 1)
        dve.wait_ge(self.ready, self.steps)

    def take(self, dve):
        v, c0 = self.co.nc.vector, self.co.cols
        x, e, q, z, z2, rl = self.rows
        k = self.cols["dt_bias"]
        self.step(dve, v.tensor_mul(x, self.co.PS[0:SSD_H, 4, :], self.co.RS[0:SSD_H, :]))
        self.step(dve, v.tensor_scalar(x, x, c0[0:SSD_H, k:k + 1], None, ALU.add))
        self.step(dve, v.scalar_tensor_tensor(e, x, -1.0, x, ALU.mult, ALU.max))
        self.step(dve, v.tensor_scalar(rl, x, 0.0, None, ALU.max))

    def exponentials(self, act):
        a, k = self.co.nc.scalar, self.cols["a_log"]
        a.activation(self.W[:, 6, 0:1], self.co.cols[0:SSD_H, k:k + 1], ACT.Exp).then_inc(self.exped, 1)
        act.wait_ge(self.ready, 3)
        a.activation(self.rows[1], self.rows[1], ACT.Exp, scale=-1.0).then_inc(self.exped, 1)

    def quotient(self, dve):
        v = self.co.nc.vector
        x, e, q, z, z2, rl = self.rows
        dve.wait_ge(self.exped, 2)
        self.step(dve, v.tensor_scalar(q, e, 2.0, None, ALU.add))
        self.step(dve, v.reciprocal(q, q))
        self.step(dve, v.tensor_mul(z, e, q))
        self.step(dve, v.tensor_mul(z2, z, z))

    def series(self, pool):
        g = self.co.nc.gpsimd
        x, e, q, z, z2, rl = self.rows
        g.memset(self.co.ones8[:], 1.0).then_inc(self.filled, 1)
        pool.wait_ge(self.ready, 8)
        n = [0]

        def step(ins):
            n[0] += 1
            ins.then_inc(self.pooled, 1)
            pool.wait_ge(self.pooled, n[0])
        step(g.tensor_scalar(q, z2, 1.0 / 15, None, ALU.mult))
        for odd, by in ((13, z2), (11, z2), (9, z2), (7, z2), (5, z2), (3, z2), (1, z)):
            step(g.tensor_scalar(q, q, 1.0 / odd, None, ALU.add))
            step(g.tensor_mul(q, q, by))

    def finish(self, dve):
        v = self.co.nc.vector
        x, e, q, z, z2, rl = self.rows
        dve.wait_ge(self.pooled, 15)
        self.step(dve, v.scalar_tensor_tensor(self.DT[:], q, 2.0, rl, ALU.mult, ALU.add))
        self.step(dve, v.tensor_scalar(x, self.DT[:], self.W[:, 6, 0:1], -1.0, ALU.mult, ALU.mult))
        dve.wait_ge(self.filled, 1)
        self.step(dve, v.tensor_tensor_scan(self.AT[:], self.co.ones8[:], x, 0.0, ALU.mult, ALU.add))


@stage
def even_input(co, stages, U, Z, XB, XC, sizes, params, cols, loads):
    nc = co.nc
    st_dt, st_u, st_z, st_x, st_bc = stages
    (bank_free, dt_bank_free, arrived, z_taken, taken, tapped0, tapped, activated) = (
        co.sem(f"ein_{s}") for s in ("bank_free", "dt_bank_free", "arrived", "z_taken", "taken", "tapped0", "tapped",
                                     "activated"))
    scale = Scale(co)
    sizes = StepSizes(co, *sizes, cols)
    params = S5Parameters(co, *params, cols)
    c0, w0, b0 = co.cols, cols["conv_w"], cols["conv_b"]
    with nc.Block() as block:
        @block.sync
        def _(sp):
            for to, src in loads:
                sp.dma_start(to, src).then_inc(arrived, 16)
            for st in stages:
                co.load(sp, st)

        @block.tensor
        def _(pe):
            scale.pe(pe)
            co.multiply(pe, st_dt, dt_bank_free)
            for n, st in enumerate(stages[1:]):
                co.multiply(pe, st, bank_free, after=4 * n)

        @block.gpsimd
        def _(pool):
            params.phases(pool)
            sizes.series(pool)

        @block.scalar
        def _(act):
            def silu(n):
                act.wait_ge(tapped, 3 * n + 3)
                nc.scalar.activation(XC[:, n, :], XC[:, n, :], ACT.Silu).then_inc(activated, 1)

            def read_z(i, c):
                act.wait_ge(z_taken, c + 1)
                nc.scalar.activation(Z[:, c, :], Z[:, c, :], ACT.Silu).then_inc(activated, 1)

            def read_conv(n):
                act.wait_ge(taken, n + 1)
                nc.scalar.activation(XC[:, n, :], XB[:, n, :], ACT.Identity, bias=c0[:, b0 + n:b0 + n + 1],
                                     scale=c0[:, w0 + 24 + n:w0 + 25 + n]).then_inc(tapped0, 1)
                if n >= 2:
                    silu(n - 2)

            def early_dt():
                scale.act(act)
                act.wait_ge(arrived, 16 * len(loads))
                params.step_exp(act)

            def early_u():
                sizes.exponentials(act)
                params.decay_and_turn(act)
            co.run(act, st_dt, co.split_hi, lambda i, c: None, early_dt)
            co.run(act, st_u, co.split_hi, lambda i, c: None, early_u)
            co.run(act, st_z, co.split_hi, read_z)
            co.run(act, st_x, co.split_hi, lambda i, c: read_conv(c))
            co.run(act, st_bc, co.split_hi, lambda i, c: read_conv(4 + c))
            silu(6)
            silu(7)

        @block.vector
        def _(dve):
            v = nc.vector
            dve.sem_inc(dt_bank_free, 1)
            dve.sem_inc(bank_free, 4)

            def read_dt(i, c):
                co.wait_units(dve, st_dt, i, c)
                sizes.take(dve)

            def read_u(i, c):
                co.wait_units(dve, st_u, i, c)
                v.tensor_mul(U[:, c, :], co.PS[:, c, :], co.RS[:]).then_inc(bank_free, 1)

            def read_z(i, c):
                co.wait_units(dve, st_z, i, c)
                v.tensor_mul(Z[:, c, :], co.PS[:, c, :], co.RS[:]).then_inc(z_taken, 1)
                dve.wait_ge(z_taken, c + 1)
                dve.sem_inc(bank_free, 1)

            def taps(n):
                dve.wait_ge(tapped0, n + 1)
                for tap in range(1, 4):
                    k = w0 + 8 * (3 - tap) + n
                    if tap > 1:
                        dve.wait_ge(tapped, 3 * n + tap - 1)
                    v.scalar_tensor_tensor(XC[:, n, tap:], XB[:, n, 0:S - tap], c0[:, k:k + 1], XC[:, n, tap:],
                                           ALU.mult, ALU.add).then_inc(tapped, 1)

            def read_conv(st, c, n):
                co.wait_units(dve, st, 0, c)
                v.tensor_mul(XB[:, n, :], co.PS[:, c, :], co.RS[:]).then_inc(taken, 1)
                dve.wait_ge(taken, n + 1)
                dve.sem_inc(bank_free, 1)
                if n >= 1:
                    taps(n - 1)
            co.run(dve, st_dt, co.split_lo, read_dt, lambda: scale.dve(dve))
            co.run(dve, st_u, co.split_lo, read_u, lambda: params.angles(dve))
            co.run(dve, st_z, co.split_lo, read_z, lambda: sizes.quotient(dve))
            co.run(dve, st_x, co.split_lo, lambda i, c: read_conv(st_x, c, c), lambda: params.matrices(dve))
            co.run(dve, st_bc, co.split_lo, lambda i, c: read_conv(st_bc, c, 4 + c), lambda: sizes.finish(dve))
            taps(7)


@stage
def ssd_tokens(co, XC, DT, AT, AC, XDT, CB):
    nc = co.nc
    name = "ssd_tok"
    cols_done, x_done, cb_done, cols_read, x_read, cb_read, masked = (
        co.sem(f"{name}_{s}") for s in ("cols_done", "x_done", "cb_done", "cols_read", "x_read", "cb_read", "masked"))
    with nc.Block() as block:
        @block.tensor
        def _(pe):
            for k, src in enumerate((AT, DT)):
                for t in range(TT):
                    m = nc.tensor.matmul(co.PS[:, 7, (k * TT + t) * 8:(k * TT + t + 1) * 8], src[:, t * P:(t + 1) * P],
                                         co.ident[0:8, 0:8], start=True, stop=True)
            m.then_inc(cols_done, 1)
            for t in range(TT):
                for c in range(4):
                    m = nc.tensor.transpose(co.PS[:, t, c * P:(c + 1) * P], XC[:, c, t * P:(t + 1) * P], co.ident)
                m.then_inc(x_done, 1)
            for g in range(2):
                for t in range(TT):
                    n = g * TT + t
                    if n >= 3:
                        pe.wait_ge(cb_read, n - 2)
                    nc.tensor.matmul(co.PS[:, 4 + n % 3, 0:S - t * P], XC[:, 4 + g, t * P:(t + 1) * P],
                                     XC[:, 6 + g, t * P:], start=True, stop=True).then_inc(cb_done, 1)

        @block.scalar
        def _(act):
            for g in range(2):
                for t in range(TT):
                    act.wait_ge(cb_done, g * TT + t + 1)
                    nc.scalar.activation(CB[:, g, OFF[t]:OFF[t] + S - t * P], co.PS[:, 4 + (g * TT + t) % 3, 0:S - t * P],
                                         ACT.Copy).then_inc(cb_read, 1)

        @block.vector
        def _(dve):
            dve.wait_ge(cols_done, 1)
            nc.vector.tensor_copy(AC[:], co.PS[:, 7, 0:64]).then_inc(cols_read, 1)
            dve.wait_ge(cols_read, 1)
            for t in range(TT):
                dve.wait_ge(x_done, t + 1)
                dt = AC[:, 32 + 8 * t:32 + 8 * t + 8].unsqueeze(2).broadcast_to([P, 8, HD])
                nc.vector.tensor_mul(XDT[:, t, :].rearrange("p (h d) -> p h d", d=HD),
                                     co.PS[:, t, :].rearrange("p (h d) -> p h d", d=HD), dt).then_inc(x_read, 1)
            for g in range(2):
                for t in range(TT):
                    dve.wait_ge(cb_read, g * TT + t + 1)
                    d = CB[:, g, OFF[t]:OFF[t] + P]
                    nc.vector.tensor_mul(d, d, co.triu).then_inc(masked, 1)


@stage
def ssd_heads(co, AT, AC, XDT, CB, XC, Z, Y, cols):
    nc = co.nc
    name = "ssd_heads"
    BANK = (0, 1, 6)
    with ExitStack() as ctx:
        SEG = co.sb(f"{name}_seg", [P, 3, TRI], ctx=ctx)
        spread, seg_ready, decayed, weighted, y_done, skipped = (
            co.sem(f"{name}_{s}") for s in ("spread", "seg_ready", "decayed", "weighted", "y_done", "skipped"))
        block = ctx.enter_context(nc.Block())

        @block.tensor
        def _(pe):
            def spread_a(h):
                if h >= 3:
                    pe.wait_ge(seg_ready, h - 2)
                nc.tensor.matmul(co.PS[:, BANK[h % 3], :], co.sel8[:, h * P:(h + 1) * P], AT[:], start=True, stop=True).then_inc(spread, 1)
            spread_a(0)
            spread_a(1)
            for h in range(SSD_H):
                if h + 2 < SSD_H:
                    spread_a(h + 2)
                pe.wait_ge(weighted, h + 1)
                po = HD * (h % 2)
                for t in range(TT):
                    m = nc.tensor.matmul(co.PS[po:po + HD, 2 + h // 2, t * P:], XDT[:, t, h * HD:(h + 1) * HD],
                                         SEG[:, h % 3, OFF[t]:OFF[t] + S - t * P], start=t == 0, stop=t == TT - 1)
                m.then_inc(y_done, 1)

        @block.scalar
        def _(act):
            for h in range(SSD_H):
                act.wait_ge(seg_ready, h + 1)
                nc.scalar.activation(SEG[:, h % 3, :], SEG[:, h % 3, :], ACT.Exp).then_inc(decayed, 1)

        @block.vector
        def _(dve):
            def weigh(h):
                dve.wait_ge(decayed, h + 1)
                nc.vector.tensor_mul(SEG[:, h % 3, :], SEG[:, h % 3, :], CB[:, h // 4, :]).then_inc(weighted, 1)
            for h in range(SSD_H):
                dve.wait_ge(spread, h + 1)
                if h >= 3:
                    dve.wait_ge(y_done, h - 2)
                for t in range(TT):
                    s = nc.vector.tensor_scalar(SEG[:, h % 3, OFF[t]:OFF[t] + S - t * P], co.PS[:, BANK[h % 3], t * P:],
                                                AC[:, 8 * t + h:8 * t + h + 1], 0.0, ALU.subtract, ALU.min)
                s.then_inc(seg_ready, 1)
                if h >= 1:
                    weigh(h - 1)
            weigh(SSD_H - 1)
            for c in range(4):
                dve.wait_ge(y_done, 2 * c + 2)
                nc.vector.scalar_tensor_tensor(Y[:, c, :], XC[:, c, :], co.cols[:, cols["ssd_d"] + c:cols["ssd_d"] + c + 1],
                                               co.PS[:, 2 + c, :], ALU.mult, ALU.add).then_inc(skipped, 1)
            for c in range(4):
                dve.wait_ge(skipped, c + 1)
                nc.vector.tensor_mul(Y[:, c, :], Y[:, c, :], Z[:, c, :]).then_inc(skipped, 1)


NT = 48
TWO_PI = 6.283185307179586
WRAP = 6.2831845
CW1 = 6.28125
CW2 = TWO_PI - CW1


class S5Parameters:

    def __init__(self, co, SP, PH, B, C, N, L, cols):
        self.co, self.SP, self.PH, self.B, self.C, self.N, self.L, self.cols = co, SP, PH, B, C, N, L, cols
        self.ready, self.acted, self.phased = (co.sem(f"s5p_{s}") for s in ("ready", "acted", "phased"))
        self.steps = 0
        self.rows = [SP[:, k, :] for k in range(16)]

    def step(self, dve, ins):
        self.steps += 1
        ins.then_inc(self.ready, 1)
        dve.wait_ge(self.ready, self.steps)

    def over(self, x, k):
        return x.unsqueeze(2).broadcast_to([P, S5G, k])

    def step_exp(self, act):
        dt = self.rows[2]
        self.co.nc.scalar.activation(dt, dt, ACT.Exp).then_inc(self.acted, 1)

    def decay_and_turn(self, act):
        a = self.co.nc.scalar
        ar, ai, dt, mag, ang, ph, sn, cs, n, t1, t2, den, fre, fim, phh, phl = self.rows
        act.wait_ge(self.ready, 1)
        a.activation(mag, t1, ACT.Exp).then_inc(self.acted, 1)
        act.wait_ge(self.ready, 10)
        a.activation(sn, sn, ACT.Sin, scale=WRAP).then_inc(self.acted, 1)
        a.activation(cs, cs, ACT.Sin, scale=WRAP).then_inc(self.acted, 1)

    def angles(self, dve):
        v = self.co.nc.vector
        step = lambda ins: self.step(dve, ins)
        ar, ai, dt, mag, ang, ph, sn, cs, n, t1, t2, den, fre, fim, phh, phl = self.rows
        dve.wait_ge(self.acted, 1)
        step(v.tensor_mul(t1, dt, ar))
        step(v.tensor_mul(ang, dt, ai))
        step(v.tensor_scalar(n, ang, 1.0 / TWO_PI, MAGIC, ALU.mult, ALU.add))
        step(v.tensor_scalar(n, n, MAGIC, None, ALU.subtract))
        step(v.scalar_tensor_tensor(ph, n, -CW1, ang, ALU.mult, ALU.add))
        step(v.scalar_tensor_tensor(ph, n, -CW2, ph, ALU.mult, ALU.add))
        step(v.tensor_scalar(ph, ph, 1.0 / TWO_PI, None, ALU.mult))
        step(v.tensor_scalar(sn, ph, 0.5, -0.5, ALU.min, ALU.max))
        step(v.scalar_tensor_tensor(cs, sn, -1.0, sn, ALU.mult, ALU.max))
        step(v.tensor_scalar(cs, cs, -1.0, 0.25, ALU.mult, ALU.add))
        step(v.tensor_scalar(phh, ph, 3072.0, None, ALU.add))
        step(v.tensor_scalar(phh, phh, 3072.0, None, ALU.subtract))
        step(v.tensor_sub(phl, ph, phh))

    def phases(self, pool):
        g = self.co.nc.gpsimd
        phh, phl = self.rows[14:16]
        k = self.cols["tokens"]
        tokens = self.co.cols[:, k:k + NT].unsqueeze(1).broadcast_to([P, S5G, NT])
        pool.wait_ge(self.ready, 13)
        PH, N, L = self.PH, self.N, self.L
        for n, make in enumerate((lambda: g.tensor_mul(PH[:], self.over(phh, NT), tokens),
                                  lambda: g.tensor_scalar(N[:], PH[:], MAGIC, None, ALU.add),
                                  lambda: g.tensor_scalar(N[:], N[:], MAGIC, None, ALU.subtract),
                                  lambda: g.tensor_sub(PH[:], PH[:], N[:]),
                                  lambda: g.tensor_mul(L[:], self.over(phl, NT), tokens),
                                  lambda: g.tensor_add(PH[:], PH[:], L[:]))):
            make().then_inc(self.phased, 1)
            pool.wait_ge(self.phased, n + 1)

    def matrices(self, dve):
        v = self.co.nc.vector
        step = lambda ins: self.step(dve, ins)
        over, B, C = self.over, self.B, self.C
        ar, ai, dt, mag, ang, ph, sn, cs, n, t1, t2, den, fre, fim, phh, phl = self.rows
        k = self.cols["sign"]
        sg = self.co.cols[:, k:k + 1]
        dve.wait_ge(self.acted, 4)
        step(v.tensor_mul(sn, sn, mag))
        step(v.tensor_mul(cs, cs, mag))
        step(v.tensor_scalar(cs, cs, 1.0, None, ALU.subtract))
        step(v.tensor_mul(den, ar, ar))
        step(v.tensor_mul(t1, ai, ai))
        step(v.tensor_add(den, den, t1))
        step(v.reciprocal(den, den))
        step(v.tensor_mul(t1, cs, ar))
        step(v.tensor_mul(t2, sn, ai))
        step(v.tensor_add(t1, t1, t2))
        step(v.tensor_mul(fre, t1, den))
        step(v.tensor_mul(t1, sn, ar))
        step(v.tensor_mul(t2, cs, ai))
        step(v.tensor_sub(t1, t1, t2))
        step(v.tensor_mul(fim, t1, den))
        step(v.tensor_scalar(t1, fim, sg, -1.0, ALU.mult, ALU.mult))
        step(v.tensor_scalar(t2, fre, sg, None, ALU.mult))
        dve.wait_ge(self.phased, 6)
        X, Y = self.N[:, :, 0:16], self.L[:, :, 0:16]
        step(v.tensor_mul(X, B[:, 0], over(fim, 16)))
        step(v.tensor_mul(Y, B[:, 1], over(t2, 16)))
        step(v.tensor_mul(B[:, 0], B[:, 0], over(fre, 16)))
        step(v.tensor_mul(B[:, 1], B[:, 1], over(t1, 16)))
        step(v.tensor_add(B[:, 0], B[:, 0], B[:, 1]))
        step(v.tensor_add(B[:, 1], X, Y))
        step(v.tensor_scalar(C[:, 0], C[:, 0], sg, None, ALU.mult))
        step(v.tensor_scalar(C[:, 1], C[:, 1], -1.0, None, ALU.mult))


@stage
def s5_matrices(co, BB, CC, BT, CT, cols):
    nc = co.nc
    turned, zeroed, placed = (co.sem(f"s5m_{s}") for s in ("turned", "zeroed", "placed"))
    with nc.Block() as block:
        @block.gpsimd
        def _(pool):
            nc.gpsimd.memset(CT[:], 0.0).then_inc(zeroed, 1)

        @block.tensor
        def _(pe):
            for k in range(2):
                for q in range(4):
                    m = nc.tensor.transpose(co.PS[:, k, q * P:(q + 1) * P],
                                            BB[:, k, 8 * q:8 * q + 8, :].rearrange("p g i -> p (g i)"), co.ident)
            m.then_inc(turned, 1)

        @block.vector
        def _(dve):
            v = nc.vector
            dve.wait_ge(turned, 1)
            for k in range(2):
                for e in range(2):
                    m = co.cols[:, cols["pair"] + e:cols["pair"] + e + 1]
                    v.tensor_scalar(BT[:, k, :, e, :], co.PS[:, k, :].rearrange("p (q n) -> p q n", n=P), m, None,
                                    ALU.mult).then_inc(placed, 1)
            dve.wait_ge(zeroed, 1)
            for k in range(2):
                for e in range(2):
                    v.tensor_copy(CT[:, k, :, e, 16 * e:16 * e + 16],
                                  CC[:, k].rearrange("p (a e) i -> p a e i", e=2)[:, :, e, :]).then_inc(placed, 1)


@stage
def s5_groups(co, SP, PH, BT, CT, U, YB, cols):
    nc = co.nc
    with ExitStack() as ctx:
        W = co.sb("s5_w", [P, 4, S], ctx=ctx)
        R = co.sb("s5_r", [P, 4, S], ctx=ctx)
        CS = co.sb("s5_cs", [P, 4, S], ctx=ctx)
        SN = co.sb("s5_sn", [P, 4, S], ctx=ctx)
        D1 = co.sb("s5_d1", [P, 3, S], ctx=ctx)
        D2 = co.sb("s5_d2", [P, 3, S], ctx=ctx)
        G = co.sb("s5_g", [P, 2, S], ctx=ctx)
        (phased, whole, wrapped, sine, folded, cosine, driven, turned1, turned2, drive, states, back, out_done) = (
            co.sem(f"s5_{s}") for s in ("phased", "whole", "wrapped", "sine", "folded", "cosine", "driven",
                                        "turned1", "turned2", "drive", "states", "back", "out_done"))
        block = ctx.enter_context(nc.Block())
        y_read = co.sem("s5_y_read")
        PI2 = co.cols[:, cols["half_pi"]:cols["half_pi"] + 1]

        @block.gpsimd
        def _(pool):
            def phase(g):
                b = g % 4
                if g >= 4:
                    pool.wait_ge(cosine, g - 3)
                a = PH[:, g, 32:48].unsqueeze(2).broadcast_to([P, 16, 32])
                t = PH[:, g, 0:32].unsqueeze(1).broadcast_to([P, 16, 32])
                nc.gpsimd.tensor_add(R[:, b].rearrange("p (a t) -> p a t", t=32), a, t).then_inc(phased, 1)

            def wrap(g):
                pool.wait_ge(whole, g + 1)
                nc.gpsimd.tensor_sub(R[:, g % 4], R[:, g % 4], W[:, g % 4]).then_inc(wrapped, 1)
            def add(g):
                pool.wait_ge(turned2, g + 1)
                nc.gpsimd.tensor_add(D1[:, g % 3], D1[:, g % 3], D2[:, g % 3]).then_inc(drive, 1)
            for g in range(4):
                phase(g)
            for g in range(3):
                wrap(g)
            add(0)
            for g in range(S5G):
                if g + 1 < S5G:
                    add(g + 1)
                if g + 3 < S5G:
                    wrap(g + 3)
                if g + 4 < S5G:
                    phase(g + 4)

        @block.scalar
        def _(act):
            for g in range(S5G):
                b = g % 4
                act.wait_ge(wrapped, g + 1)
                if g >= 4:
                    act.wait_ge(out_done, g - 3)
                nc.scalar.activation(SN[:, b], R[:, b], ACT.Sin, scale=WRAP).then_inc(sine, 1)
                act.wait_ge(sine, g + 1)
                nc.scalar.activation(R[:, b], R[:, b], ACT.Abs).then_inc(folded, 1)
                act.wait_ge(folded, g + 1)
                nc.scalar.activation(CS[:, b], R[:, b], ACT.Sin, scale=-WRAP, bias=PI2).then_inc(cosine, 1)

        @block.tensor
        def _(pe):
            def drives(g):
                q, j = g // 8, g % 8
                r = 32 * (j // 2)
                if g >= 3:
                    pe.wait_ge(turned2, g - 2)
                for k in range(2):
                    m = nc.tensor.matmul(co.PS[:, 2 * (g % 3) + k, :], BT[r:r + 32, k, q, j % 2, :], U[r:r + 32, q, :],
                                         start=True, stop=True)
                m.then_inc(driven, 1)
            for g in range(3):
                drives(g)
            for g in range(S5G):
                if g + 3 < S5G:
                    drives(g + 3)
                q, j = g // 8, g % 8
                r = 32 * (j // 2)
                if q >= 2 and j == 0:
                    pe.wait_ge(y_read, q - 1)
                pe.wait_ge(back, g + 1)
                for k, o in enumerate((CS, SN)):
                    m = nc.tensor.matmul(co.PS[r:r + 32, 6 + q % 2, :], CT[:, k, g // 2, j % 2, :], o[:, g % 4, :],
                                         start=j % 2 == 0 and k == 0, stop=j % 2 == 1 and k == 1)
                m.then_inc(out_done, 1)

        @block.vector
        def _(dve):
            v = nc.vector

            def whole_turns(g):
                dve.wait_ge(phased, g + 1)
                if g >= 4:
                    dve.wait_ge(wrapped, g - 3)
                v.tensor_scalar(W[:, g % 4], R[:, g % 4], MAGIC, MAGIC, ALU.add, ALU.subtract).then_inc(whole, 1)

            def turn(g):
                b = g % 3
                dve.wait_ge(driven, g + 1)
                dve.wait_ge(cosine, g + 1)
                if g >= 3:
                    dve.wait_ge(states, g - 2)
                v.tensor_mul(D1[:, b], co.PS[:, 2 * (g % 3), :], CS[:, g % 4]).then_inc(turned1, 1)
                v.tensor_mul(D2[:, b], co.PS[:, 2 * (g % 3) + 1, :], SN[:, g % 4]).then_inc(turned2, 1)

            def output(q):
                dve.wait_ge(out_done, 8 * q + 8)
                k = cols["s5_d"] + q
                v.scalar_tensor_tensor(YB[:, q, :], U[:, q, :], co.cols[:, k:k + 1], co.PS[:, 6 + q % 2, :],
                                       ALU.mult, ALU.add).then_inc(y_read, 1)
            for g in range(4):
                whole_turns(g)
            turn(0)
            turn(1)
            for g in range(S5G):
                b = g % 2
                dve.wait_ge(drive, g + 1)
                mag = SP[:, 3, g:g + 1].broadcast_to([P, S])
                v.tensor_tensor_scan(G[:, b], mag, D1[:, g % 3], 0.0, ALU.mult, ALU.add).then_inc(states, 1)
                if g + 2 < S5G:
                    turn(g + 2)
                if g + 4 < S5G:
                    whole_turns(g + 4)
                dve.wait_ge(states, g + 1)
                v.tensor_mul(CS[:, g % 4], G[:, b], CS[:, g % 4])
                v.tensor_mul(SN[:, g % 4], G[:, b], SN[:, g % 4]).then_inc(back, 1)
                if g % 8 == 1 and g > 8:
                    output(g // 8 - 1)
            output(S5G // 8 - 1)


@stage
def finish_halves(co, st, Y, YB, T, M, cols):
    nc = co.nc
    gain = cols["ssd_norm"]
    with ExitStack() as ctx:
        SQ = co.sb("fin_sq", [P, 4, S], ctx=ctx)
        R = co.sb("fin_r", [P, 2, S], ctx=ctx)
        G = (co.sb("fin_gh", [P, 4, S], F32R, ctx), co.sb("fin_gl", [P, 4, S], F32R, ctx))
        for u in st.units:
            u.x = G
        (squared, summed, scaled, rooted, inverted, gelued, g_rounded, g_parted, normed, rounded, parted, bank_free,
         gates, gated, y_rounded) = (
            co.sem(f"fin_{s}") for s in ("squared", "summed", "scaled", "rooted", "inverted", "gelued", "g_rounded",
                                         "g_parted", "normed", "rounded", "parted", "bank_free", "gates", "gated",
                                         "y_rounded"))
        block = ctx.enter_context(nc.Block())

        @block.sync
        def _(sp):
            co.load(sp, st)

        @block.tensor
        def _(pe):
            for c in range(4):
                pe.wait_ge(squared, c + 1)
                m = nc.tensor.matmul(co.PS[:, 4 + c // 2, :], co.ones[:], SQ[:, c, :], start=c % 2 == 0, stop=c % 2 == 1)
            m.then_inc(summed, 1)
            co.multiply(pe, st, bank_free, (g_parted, [4] * RAW))

        @block.scalar
        def _(act):
            act.sem_inc(bank_free, 4)
            for c in range(4):
                nc.scalar.activation(SQ[:, c, :], Y[:, c, :], ACT.Square).then_inc(squared, 1)
            for c in range(4):
                nc.scalar.activation(T[:, c, :], YB[:, c, :], ACT.Gelu_apprx_tanh).then_inc(gelued, 1)
            for c in range(4):
                act.wait_ge(gelued, c + 1)
                nc.scalar.activation(G[0][:, c, :], T[:, c, :], ACT.Copy).then_inc(g_rounded, 1)
            act.wait_ge(scaled, 1)
            nc.scalar.activation(R[:], R[:], ACT.Sqrt).then_inc(rooted, 1)

            def norm_hi():
                for c in range(4):
                    act.wait_ge(normed, c + 1)
                    nc.scalar.activation(M[0][:, c, :], Y[:, c, :], ACT.Copy).then_inc(rounded, 1)

            def read(i, c):
                co.wait_units(act, st, i, c)
                k = cols["b_glu"] + c
                nc.scalar.activation(T[:, c, :], co.PS[:, c, :], ACT.Sigmoid, bias=co.cols[:, k:k + 1]).then_inc(gates, 1)
            co.run(act, st, co.split_hi, read, norm_hi)
            for c in range(4):
                act.wait_ge(gated, c + 1)
                nc.scalar.activation(M[0][:, 4 + c, :], YB[:, c, :], ACT.Copy).then_inc(y_rounded, 1)

        @block.vector
        def _(dve):
            dve.wait_ge(summed, 1)
            nc.vector.tensor_scalar(R[:], co.PS[:, 4:6, :], 1.0 / 256, EPS, ALU.mult, ALU.add).then_inc(scaled, 1)
            for c in range(4):
                dve.wait_ge(g_rounded, c + 1)
                nc.vector.tensor_sub(G[1][:, c, :], T[:, c, :], G[0][:, c, :].bitcast(F32)).then_inc(g_parted, 1)

            def norm():
                dve.wait_ge(rooted, 1)
                for g in range(2):
                    nc.vector.reciprocal(R[:, g, :], R[:, g, :]).then_inc(inverted, 1)
                    dve.wait_ge(inverted, g + 1)
                    for c in (2 * g, 2 * g + 1):
                        k = gain + c
                        nc.vector.scalar_tensor_tensor(Y[:, c, :], Y[:, c, :], co.cols[:, k:k + 1], R[:, g, :],
                                                       ALU.mult, ALU.mult).then_inc(normed, 1)
                for c in range(4):
                    dve.wait_ge(rounded, c + 1)
                    nc.vector.tensor_sub(M[1][:, c, :], Y[:, c, :], M[0][:, c, :].bitcast(F32)).then_inc(parted, 1)

            def read(i, c):
                dve.wait_ge(gates, c + 1)
                nc.vector.tensor_mul(YB[:, c, :], YB[:, c, :], T[:, c, :]).then_inc(gated, 1)
            co.run(dve, st, co.split_lo, read, norm)
            for c in range(4):
                dve.wait_ge(y_rounded, c + 1)
                nc.vector.tensor_sub(M[1][:, 4 + c, :], YB[:, c, :], M[0][:, 4 + c, :].bitcast(F32)).then_inc(parted, 1)


def scaled_to(co, buf):
    return lambda i, c: ("dve", lambda ps: co.nc.vector.tensor_mul(one(buf, RAW * i + c), ps, rs1(co)))


def to_buffer(co, buf, func=ACT.Copy):
    def reads(i, c):
        if c % 2 == 0 or func != ACT.Copy:
            return "act", lambda ps: co.nc.scalar.activation(one(buf, RAW * i + c), ps, func)
        return "dve", lambda ps: co.nc.vector.tensor_copy(one(buf, RAW * i + c), ps)
    return reads


def plan_even(co):
    w = co.dram["ein_dt"]
    dt = co.plan(Stage(1, [Unit(2, lambda i, j=j: w[j], (co.Hh, co.Hl), 2 * j, 4, j == 0, j == RAW - 1)
                           for j in range(RAW)], 1, 1))
    return [dt] + [feed(co, n) for n in ("ein_u", "ein_z", "ein_x", "ein_bc")], feed(co, "glu"), feed(co, "eout")


def even_mixer(co, plan, cols, gain):
    nc = co.nc
    st_in, st_glu, st_out = plan
    d = co.dram
    with ExitStack() as ctx:
        U = co.sb("U", [P, 4, S], ctx=ctx)
        Y = co.sb("Y", [P, 4, S], ctx=ctx)
        SP = co.sb("s5_sp", [P, 16, S5G], ctx=ctx)
        B = co.sb("s5_b", [P, 2, S5G, 16], ctx=ctx)
        C = co.sb("s5_c", [P, 2, S5G, 16], ctx=ctx)
        PH = co.sb("s5_ph", [P, S5G, NT], ctx=ctx)
        with ExitStack() as inner:
            Z = co.sb("ssd_z", [P, 4, S], ctx=inner)
            XC = co.sb("XC", [P, 8, S], ctx=inner)
            DT = co.sb("DT", [SSD_H, S], ctx=inner)
            AT = co.sb("AT", [SSD_H, S], ctx=inner)
            AC = co.sb("AC", [P, 64], ctx=inner)
            co.sel8 = co.sb("sel8", [SSD_H, SSD_H * P], ctx=inner)
            with ExitStack() as tmp:
                XB = co.sb("XB", [P, 8, S], ctx=tmp)
                W8 = co.sb("W8", [SSD_H, 7, S], ctx=tmp)
                co.ones8 = co.sb("ones8", [SSD_H, S], ctx=tmp)
                N = Y[:, 0:3, :].rearrange("p a s -> p (a s)").rearrange("p (g t) -> p g t", t=NT)
                L = co.sb("s5_l", [P, S5G, NT], ctx=tmp)
                even_input(co, st_in, U, Z, XB, XC, (DT, AT, W8), (SP, PH, B, C, N, L), cols, [
                    (SP[:, 0:3, :], d["s5p"].rearrange("p (a g) -> p a g", g=S5G)),
                    (B[:], d["s5b"].rearrange("p (a g i) -> p a g i", g=S5G, i=16)),
                    (C[:], d["s5c"].rearrange("p (a g i) -> p a g i", g=S5G, i=16)), (co.sel8[:], d["sel8"])])
            with ExitStack() as tmp:
                XDT = co.sb("XDT", [P, TT, S], ctx=tmp)
                CB = co.sb("CB", [P, 2, TRI], ctx=tmp)
                ssd_tokens(co, XC, DT, AT, AC, XDT, CB)
                ssd_heads(co, AT, AC, XDT, CB, XC, Z, Y, cols)
        with ExitStack() as inner:
            YB = co.sb("YB", [P, 4, S], ctx=inner)
            with ExitStack() as tmp:
                BT = co.sb("s5_bt", [P, 2, 4, 2, P], ctx=tmp)
                CT = co.sb("s5_ct", [P, 2, S5G // 2, 2, 32], ctx=tmp)
                s5_matrices(co, B, C, BT, CT, cols)
                s5_groups(co, SP, PH, BT, CT, U, YB, cols)
            M = (co.sb("even_mh", [P, DC, S], F32R, inner), co.sb("even_ml", [P, DC, S], F32R, inner))
            finish_halves(co, st_glu, Y, YB, U, M, cols)
            for u in st_out.units:
                u.x = M
            add_stage(co, st_out, 1.0, gain)





@stage
def head_norms(co, QK, V, SEL, n, q_chunks, cols):
    nc = co.nc
    with ExitStack() as ctx:
        SQ = co.sb("hn_sq", [P, n, S], ctx=ctx)
        R = co.sb("hn_r", [P, TT, n, 2], ctx=ctx)
        RT = co.sb("hn_rt", [2 * n, S], ctx=ctx)
        squared, summed, scaled, rooted, inverted, turned, spread, done, v_turned, v_stored = (
            co.sem(f"hn_{s}") for s in ("squared", "summed", "scaled", "rooted", "inverted", "turned", "spread", "done",
                                        "v_turned", "v_stored"))
        block = ctx.enter_context(nc.Block())

        @block.scalar
        def _(act):
            for c in range(n):
                nc.scalar.activation(SQ[:, c, :], QK[:, c, :], ACT.Square).then_inc(squared, 1)
            act.wait_ge(scaled, 1)
            nc.scalar.activation(R[:], R[:], ACT.Sqrt).then_inc(rooted, 1)

        @block.tensor
        def _(pe):
            for t in range(TT):
                for c in range(4):
                    m = nc.tensor.transpose(co.PS[:, 1 + t, c * P:(c + 1) * P], V[:, c, t * P:(t + 1) * P], co.ident)
            m.then_inc(v_turned, 1)
            for c in range(n):
                pe.wait_ge(squared, c + 1)
                for t in range(TT):
                    m = nc.tensor.matmul(co.PS[:, 0, (t * n + c) * 2:(t * n + c) * 2 + 2], SQ[:, c, t * P:(t + 1) * P],
                                         co.heads[:, 0:P:64], start=True, stop=True)
            m.then_inc(summed, 1)
            pe.wait_ge(inverted, 2)
            for t in range(TT):
                m = nc.tensor.transpose(co.PS[0:2 * n, 5, t * P:(t + 1) * P], R[:, t, :, :].rearrange("p c e -> p (c e)"),
                                        co.ident)
            m.then_inc(turned, 1)
            pe.wait_ge(inverted, 3)
            for c in range(n):
                if c < 4:
                    pe.wait_ge(v_stored, c + 1)
                else:
                    pe.wait_ge(done, c - 3)
                nc.tensor.matmul(co.PS[:, 1 + c % 4, :], SEL[:, c * P:(c + 1) * P], RT[:], start=True, stop=True).then_inc(spread, 1)

        @block.vector
        def _(dve):
            dve.wait_ge(v_turned, 1)
            for t in range(TT):
                nc.vector.tensor_copy(V[:, t, :], co.PS[:, 1 + t, :]).then_inc(v_stored, 1)
            dve.wait_ge(summed, 1)
            nc.vector.tensor_scalar(R[:].rearrange("p t c e -> p (t c e)"), co.PS[:, 0, 0:TT * n * 2], 1.0 / HD, EPS,
                                    ALU.mult, ALU.add).then_inc(scaled, 1)
            dve.wait_ge(rooted, 1)
            nc.vector.reciprocal(R[:], R[:]).then_inc(inverted, 1)
            dve.wait_ge(inverted, 1)
            q = R[:, :, 0:q_chunks, :]
            nc.vector.tensor_scalar(q, q, HD ** -0.5, None, ALU.mult).then_inc(inverted, 1)
            dve.wait_ge(turned, 1)
            nc.vector.tensor_copy(RT[:], co.PS[0:2 * n, 5, :]).then_inc(inverted, 1)
            for c in range(n):
                dve.wait_ge(spread, c + 1)
                g = cols["q_gain"] if c < q_chunks else cols["k_gain"]
                nc.vector.scalar_tensor_tensor(QK[:, c, :], QK[:, c, :], co.cols[:, g:g + 1], co.PS[:, 1 + c % 4, :],
                                               ALU.mult, ALU.mult).then_inc(done, 1)


@stage
def turn_values(co, groups):
    nc = co.nc
    name = co.tag("values")
    turned, stored = co.sem(f"{name}_turned"), co.sem(f"{name}_stored")
    with nc.Block() as block:
        @block.tensor
        def _(pe):
            for n, (V, tokens) in enumerate(groups):
                if n >= 2:
                    pe.wait_ge(stored, TT * (n - 1))
                for t in range(TT):
                    for c in range(4):
                        m = nc.tensor.transpose(co.PS[:, 4 * (n % 2) + t, c * P:(c + 1) * P], V[:, c, tokens(t)], co.ident)
                m.then_inc(turned, 1)

        @block.vector
        def _(dve):
            for n, (V, tokens) in enumerate(groups):
                dve.wait_ge(turned, n + 1)
                for t in range(TT):
                    nc.vector.tensor_copy(V[:, t, :], co.PS[:, 4 * (n % 2) + t, :]).then_inc(stored, 1)


@stage
def attend(co, items, score, tiles, value, width, scale, s_banks, out_bank, out_read, extra=None):
    nc = co.nc
    name = co.tag("attend")
    n = len(items)
    nb = len(s_banks)
    with ExitStack() as ctx:
        PR = co.sb(f"{name}_pr", [P, 3, width], ctx=ctx)
        PT = co.sb(f"{name}_pt", [P, 2, width], ctx=ctx)
        ST = co.sb(f"{name}_st", [P, 3, 4], ctx=ctx)
        scored, topped, negated, powered, inverted, normed, turned, copied, weighted, out_hi, out_lo = (
            co.sem(f"{name}_{s}") for s in ("scored", "topped", "negated", "powered", "inverted", "normed", "turned",
                                            "copied", "weighted", "out_hi", "out_lo"))
        block = ctx.enter_context(nc.Block())
        key_banks = [(tiles(x) + 3) // 4 for x in items]
        before = [sum(key_banks[:k]) for k in range(n + 1)]

        def sview(k):
            b = s_banks[k % nb]
            return co.PS[:, b:b + (width + 511) // 512, :].rearrange("p b n -> p (b n)")

        def tview(m):
            return co.PS[:, s_banks[-1] + (width + 511) // 512 + m % 2, :]

        @block.tensor
        def _(pe):
            for k in range(n + 3):
                if k < n:
                    if k >= nb:
                        pe.wait_ge(powered, k - nb + 1)
                    score(items[k], sview(k)).then_inc(scored, 1)
                if 2 <= k < n + 2:
                    x = items[k - 2]
                    pe.wait_ge(normed, k - 1)
                    for m in range(key_banks[k - 2]):
                        b = before[k - 2] + m
                        if b >= 2:
                            pe.wait_ge(copied, b - 1)
                        for t in range(4 * m, min(4 * m + 4, tiles(x))):
                            i = nc.tensor.transpose(tview(b)[:, (t % 4) * P:(t % 4 + 1) * P],
                                                    PR[:, (k - 2) % 3, t * P:(t + 1) * P], co.ident)
                        i.then_inc(turned, 1)
                if k >= 3:
                    x = items[k - 3]
                    pe.wait_ge(copied, before[k - 2])
                    bank, part, cs, need = out_bank(x)
                    if need is not None:
                        pe.wait_ge(out_lo, need)
                    for t in range(tiles(x)):
                        i = nc.tensor.matmul(co.PS[part:part + HD, bank, cs], value(x, t),
                                             PT[:, (k - 3) % 2, t * P:(t + 1) * P], start=t == 0, stop=t == tiles(x) - 1)
                    i.then_inc(weighted, 1)

        @block.vector
        def _(dve):
            outs = 0
            for k in range(n + 1):
                if k < n:
                    w = tiles(items[k]) * P
                    dve.wait_ge(scored, k + 1)
                    nc.vector.reduce_max(ST[:, k % 3, 0:1], sview(k)[:, 0:w], axis=AX.X).then_inc(topped, 1)
                    dve.wait_ge(topped, k + 1)
                    nc.vector.tensor_scalar(ST[:, k % 3, 1:2], ST[:, k % 3, 0:1], -scale, None, ALU.mult).then_inc(negated, 1)
                if k >= 1:
                    w = tiles(items[k - 1]) * P
                    b = (k - 1) % 3
                    dve.wait_ge(powered, k)
                    nc.vector.reciprocal(ST[:, b, 3:4], ST[:, b, 2:3]).then_inc(inverted, 1)
                    dve.wait_ge(inverted, k)
                    nc.vector.tensor_scalar(PR[:, b, 0:w], PR[:, b, 0:w], ST[:, b, 3:4], None, ALU.mult).then_inc(normed, 1)
                    if k >= 4 and out_read(k - 4) is not None:
                        hi, lo, src = out_read(k - 4)
                        outs += 1
                        dve.wait_ge(out_hi, outs)
                        nc.vector.tensor_sub(lo, src, hi.bitcast(F32)).then_inc(out_lo, 1)
            for k in range(n - 3, n):
                if out_read(k) is not None:
                    hi, lo, src = out_read(k)
                    outs += 1
                    dve.wait_ge(out_hi, outs)
                    nc.vector.tensor_sub(lo, src, hi.bitcast(F32)).then_inc(out_lo, 1)

        @block.scalar
        def _(act):
            for k in range(n + 3):
                if k < n:
                    w = tiles(items[k]) * P
                    act.wait_ge(negated, k + 1)
                    if k >= 3:
                        act.wait_ge(turned, before[k - 2])
                    nc.scalar.activation(PR[:, k % 3, 0:w], sview(k)[:, 0:w], ACT.Exp, bias=ST[:, k % 3, 1:2],
                                         scale=scale, accum_out=ST[:, k % 3, 2:3]).then_inc(powered, 1)
                if 2 <= k < n + 2:
                    x = items[k - 2]
                    if k >= 4:
                        act.wait_ge(weighted, k - 3)
                    for m in range(key_banks[k - 2]):
                        b = before[k - 2] + m
                        w0, w1 = 512 * m, min(512 * m + 512, tiles(x) * P)
                        act.wait_ge(turned, b + 1)
                        nc.scalar.activation(PT[:, (k - 2) % 2, w0:w1], tview(b)[:, 0:w1 - w0], ACT.Copy).then_inc(copied, 1)
                if k >= 3 and out_read(k - 3) is not None:
                    hi, lo, src = out_read(k - 3)
                    act.wait_ge(weighted, k - 2)
                    nc.scalar.activation(hi, src, ACT.Copy).then_inc(out_hi, 1)

        if extra:
            block.gpsimd(extra)


def plan_odd(co):
    return feed(co, "oin"), feed(co, "oout")


def odd_mixer(co, plan, cols, gain):
    nc = co.nc
    st_in, st_out = plan
    with ExitStack() as ctx:
        QU = co.sb("QU", [P, 16, S], ctx=ctx)
        HK = co.sb("HK", [P, 8, S], ctx=ctx)
        POOLED = co.sb("POOLED", [P, 4, S], ctx=ctx)
        PB = co.sb("PB", [P, 2, S], ctx=ctx)
        PW = co.sb("PW", [P, 4, P], ctx=ctx)
        RC = co.sb("RC", [P, 4, 16], ctx=ctx)
        MR = co.sb("MR", [1, P + 64], ctx=ctx)
        SEL = POOLED[0:16, 0:2, :].rearrange("p a s -> p (a s)")
        d = co.dram
        row = d["hankel"]
        copy_stage(co, st_in, scaled_to(co, QU), scaled=True, loads=[
            (HK[:], bass.AP(tensor=row.tensor, offset=0, ap=[[1, P], [row.shape[1], 8], [1, S]])),
            (PW[:], d["pool_w"].rearrange("g i o -> i g o")), (RC[:], d["counts"].rearrange("p (g t) -> p g t", t=16)),
            (MR[:], d["chunk_mask"]), (SEL, d["head_sel"])])
        head_norms(co, QU[:, 0:8, :], QU[:, 8:12, :], SEL, 8, 4, cols)
        M = (co.sb("odd_mh", [P, DC, S], F32R, ctx), co.sb("odd_ml", [P, DC, S], F32R, ctx))

        def score(x, ps):
            h, t = x
            c, r = h // 2, HD * (h % 2)
            w = (t + 1) * P
            nc.tensor.matmul(ps[:, 0:w], QU[r:r + HD, c, t * P:(t + 1) * P], QU[r:r + HD, 4 + c, 0:w], start=True, stop=False)
            nc.tensor.matmul(ps[:, 0:w], co.flip, HK[:, h, 384 - P * t:], start=False, stop=False)
            return nc.tensor.matmul(ps[:, w - 64:w], MR[:, 0:P], MR[:, P:], start=False, stop=True)

        pooling = co.sem("pooling")

        def pool_windows(pool):
            g_ = nc.gpsimd
            steps = [0]

            def step(ins):
                steps[0] += 1
                ins.then_inc(pooling, 1)
                pool.wait_ge(pooling, steps[0])
            for g in range(4):
                src = QU[:, 12 + g, :]
                for k in range(g + 1):
                    d = 1 << k
                    dst = POOLED[:, g, :] if (g - k) % 2 == 0 else PB[:, 0, :]
                    step(g_.tensor_copy(dst[:, 0:d], src[:, 0:d]))
                    step(g_.tensor_add(dst[:, d:], src[:, d:], src[:, 0:S - d]))
                    src = dst
                step(g_.tensor_mul(src[:, 0:16], src[:, 0:16], RC[:, g, :]))
                step(g_.tensor_scalar(src[:, 16:], src[:, 16:], 1.0 / (2 << g), None, ALU.mult))
                step(g_.tensor_sub(src, src, QU[:, 12 + g, :]))

        items = [(h, t) for h in range(8) for t in range(TT)]

        def out_read(k):
            if k % 8 != 7:
                return None
            c = k // 8
            return M[0][:, c, :], M[1][:, c, :], co.PS[:, 4 + c, :]
        attend(co, items, score, lambda x: x[1] + 1, lambda x, t: QU[:, 8 + t, x[0] * HD:(x[0] + 1) * HD], 512, 1.0,
               [0, 1], lambda x: (4 + x[0] // 2, HD * (x[0] % 2), slice(x[1] * P, (x[1] + 1) * P), None), out_read,
               pool_windows)
        with ExitStack() as tmp:
            T = co.sb("pool_t", [P, 4, S], ctx=tmp)
            made, scaled, rounded = co.sem("pool_made"), co.sem("pool_scaled"), co.sem("pool_rounded")
            block = tmp.enter_context(nc.Block())

            @block.tensor
            def _(pe):
                for g in range(4):
                    nc.tensor.matmul(co.PS[:, g, :], PW[:, g, :], POOLED[:, g, :], start=True, stop=True).then_inc(made, 1)

            @block.vector
            def _(dve):
                for g in range(4):
                    dve.wait_ge(made, g + 1)
                    k = cols["pool_scale"] + g
                    nc.vector.tensor_scalar(T[:, g, :], co.PS[:, g, :], co.cols[:, k:k + 1], None, ALU.mult).then_inc(scaled, 1)
                for g in range(4):
                    dve.wait_ge(rounded, g + 1)
                    nc.vector.tensor_sub(M[1][:, 4 + g, :], T[:, g, :], M[0][:, 4 + g, :].bitcast(F32)).then_inc(scaled, 1)

            @block.scalar
            def _(act):
                for g in range(4):
                    act.wait_ge(scaled, g + 1)
                    nc.scalar.activation(M[0][:, 4 + g, :], T[:, g, :], ACT.Copy).then_inc(rounded, 1)
        for u in st_out.units:
            u.x = M
        add_stage(co, st_out, 1.0, gain)



WINDOW = S + 4
MW = WINDOW + 2 * P
TAPS = 31
ALPHA = 2 ** 0.25


@stage
def rotated_input(co, st_qk, st_v, QKV, IB, loads):
    nc = co.nc
    with ExitStack() as ctx:
        ROPE = co.sb("ROPE", [P, 2, S], ctx=ctx)
        A = co.sb("rope_a", [P, 2, 1, S], ctx=ctx)
        B = co.sb("rope_b", [P, RAW, 1, S], ctx=ctx)
        bank_free, arrived, taken, cosines, sines, done, cast = (
            co.sem(f"rope_{s}") for s in ("bank_free", "arrived", "taken", "cosines", "sines", "done", "cast"))
        swapped = [co.sem(f"rope_swapped{c}") for c in range(RAW)]
        cos, sin = (ROPE[:, k:k + 1, :] for k in range(2))
        block = ctx.enter_context(nc.Block())

        @block.sync
        def _(sp):
            sp.dma_start(ROPE[:], co.dram["rope"].rearrange("p (a s) -> p a s", s=S)).then_inc(arrived, 16)
            for to, src in loads:
                sp.dma_start(to, src).then_inc(arrived, 16)
            co.load(sp, st_qk)
            co.load(sp, st_v)

        @block.tensor
        def _(pe):
            co.multiply(pe, st_qk, bank_free)
            co.multiply(pe, st_v, bank_free, after=RAW * st_qk.bodies)

        @block.gpsimd
        def _(pool):
            pool.sem_inc(done, 2)
            pool.wait_ge(arrived, 16 * (1 + len(loads)))
            with pool.Fori(0, st_qk.bodies) as i:
                for c in range(RAW):
                    n = RAW * i + c
                    pool.wait_ge(taken, n + 1)
                    pool.wait_ge(done, n + 1)
                    nc.gpsimd.tensor_mul(A[:, c % 2], one(QKV, n), cos).then_inc(cosines, 1)

        @block.scalar
        def _(act):
            act.sem_inc(bank_free, RAW)

            def read_qk(i, c):
                n = RAW * i + c
                co.wait_units(act, st_qk, i, c)
                nc.scalar.activation(one(QKV, n), one(co.PS, c), ACT.Copy).then_inc(taken, 1)
                act.wait_ge(taken, n + 1)
                act.sem_inc(bank_free, 1)
                if not (isinstance(i, int) and i == 0):
                    act.wait_ge(done, n - 1)
                for q in range(4):
                    p, o = 32 * q, 32 * (q ^ 1)
                    act.dma_start(B[p:p + 32, c], QKV[o:o + 32, bass.ds(n, 1), :]).then_inc(swapped[c], 16)
            co.run(act, st_qk, co.split_hi, read_qk)

            def read_v(i, c):
                co.wait_units(act, st_v, i, c)
                nc.scalar.activation(one(QKV, 24 + RAW * i + c), one(co.PS, c), ACT.Copy).then_inc(bank_free, 1)
            co.run(act, st_v, co.split_hi, read_v)

        @block.vector
        def _(dve):
            nc.vector.tensor_copy(IB[:], co.ident).then_inc(cast, 1)
            dve.wait_ge(arrived, 16 * (1 + len(loads)))

            def rotate(i, c):
                n = RAW * i + c
                dve.wait_ge(swapped[c], 64 * i + 64)
                nc.vector.tensor_mul(B[:, c], B[:, c], sin).then_inc(sines, 1)
                dve.wait_ge(sines, n + 1)
                dve.wait_ge(cosines, n + 1)
                nc.vector.tensor_add(one(QKV, n), A[:, c % 2], B[:, c]).then_inc(done, 1)

            def read_qk(i, c):
                if c > 0:
                    rotate(i, c - 1)
                elif not (isinstance(i, int) and i == 0):
                    rotate(i - 1, RAW - 1)
            co.run(dve, st_qk, co.split_lo, read_qk)
            rotate(st_qk.bodies - 1, RAW - 1)
            co.run(dve, st_v, co.split_lo, lambda i, c: None)


def plan_hybrid(co):
    st = {n: feed(co, n) for n in ("hin_qk", "hin_v", "hin_b", "hin_a", "hin_gate")}
    w = co.dram["hao"]
    st["hao"] = co.plan(Stage(w.shape[0] // RAW, [
        Unit(4, lambda i, j=j: w[bass.ds(RAW * i + j, 1)].rearrange("o p n -> p (o n)"), None, 0, j) for j in range(RAW)
    ], 2, 2))
    st["ho"] = feed(co, "ho")
    return st


@stage
def gates_and_conv(co, st, GT, U, CV, cols):
    nc = co.nc
    bank_free, tapped, pool_tapped, pool_product = (
        co.sem(s) for s in ("gates_bank_free", "conv_tapped", "conv_pool_tapped", "conv_pool_product"))
    with ExitStack() as ctx:
        TP = co.sb("conv_tp", [P, 2, S], ctx=ctx)
        block = ctx.enter_context(nc.Block())

        @block.sync
        def _(sp):
            co.load(sp, st)

        @block.tensor
        def _(pe):
            co.multiply(pe, st, bank_free)

        @block.scalar
        def _(act):
            act.sem_inc(bank_free, 4)

            def read(i, c):
                co.wait_units(act, st, i, c)
                nc.scalar.activation(one(GT, RAW * i + c), one(co.PS, c), ACT.Sigmoid).then_inc(bank_free, 1)
            co.run(act, st, co.split_hi, read)

        @block.vector
        def _(dve):
            v = nc.vector

            def read(i, c):
                last = isinstance(i, int) and i == st.bodies - 1 and c == RAW - 1
                for e in range(1 if last else 2):
                    tap = 8 * i + 2 * c + e
                    for n in range(3):
                        dve.wait_ge(tapped, 3 * tap + n + 1)
                        v.scalar_tensor_tensor(CV[:, n, :], U[:, n, bass.ds(tap, S)],
                                               co.cols[:, bass.ds(cols["conv2_w"] + TAPS * n + tap, 1)],
                                               CV[:, n, :], ALU.mult, ALU.add).then_inc(tapped, 1)
            for n in range(3):
                k = cols["conv2_b"] + n
                v.tensor_scalar(CV[:, n, :], U[:, n, 0:S], 0.0, co.cols[:, k:k + 1],
                                        ALU.mult, ALU.add).then_inc(tapped, 1)
            co.run(dve, st, co.split_lo, read)

        @block.gpsimd
        def _(pool):
            k = cols["conv2_b"] + 3
            nc.gpsimd.tensor_scalar(CV[:, 3, :], U[:, 3, 0:S], 0.0, co.cols[:, k:k + 1], ALU.mult, ALU.add).then_inc(pool_tapped, 1)
            def product(tap, slot):
                nc.gpsimd.tensor_mul(TP[:, slot, :], U[:, 3, bass.ds(tap, S)],
                                     co.cols[:, bass.ds(w + tap, 1)].broadcast_to([P, S])).then_inc(pool_product, 1)

            def add(tap, slot):
                pool.wait_ge(pool_product, tap + 1)
                pool.wait_ge(pool_tapped, tap + 1)
                nc.gpsimd.tensor_add(CV[:, 3, :], CV[:, 3, :], TP[:, slot, :]).then_inc(pool_tapped, 1)
            w = cols["conv2_w"] + TAPS * 3
            product(0, 0)
            with pool.Fori(0, TAPS // 2) as i:
                for e in range(2):
                    pool.wait_ge(pool_tapped, 2 * i + e + 1)
                    product(2 * i + e + 1, 1 - e)
                    add(2 * i + e, e)
            add(TAPS - 1, 0)


@stage
def merge(co, st, GT, M):
    nc = co.nc
    with ExitStack() as ctx:
        A = co.sb("merge_a", [P, 2, 1, S], ctx=ctx)
        B = co.sb("merge_b", [P, 2, 1, S], ctx=ctx)
        banks_free, first, added, rounded, done = (
            co.sem(f"merge_{s}") for s in ("banks_free", "first", "added", "rounded", "done"))
        block = ctx.enter_context(nc.Block())

        @block.sync
        def _(sp):
            co.load(sp, st)

        @block.tensor
        def _(pe):
            co.multiply(pe, st, banks_free)

        @block.scalar
        def _(act):
            def read(i, c):
                act.wait_ge(added, 2 * i + c + 1)
                nc.scalar.activation(one(M[0], 2 * i + c), A[:, c], ACT.Copy).then_inc(rounded, 1)
            co.run(act, st, co.split_hi, read)

        @block.vector
        def _(dve):
            dve.sem_inc(banks_free, 2)

            def read(i, c):
                co.wait_units(dve, st, i, c)
                nc.vector.tensor_mul(A[:, c], one(co.PS, 2 * c), one(GT, 2 * i + c)).then_inc(first, 1)
                nc.vector.tensor_mul(B[:, c], one(co.PS, 2 * c + 1), one(GT, 8 + 2 * i + c)).then_inc(banks_free, 1)
                dve.wait_ge(banks_free, 2 + 2 * i + c + 1)
                nc.vector.tensor_add(A[:, c], A[:, c], B[:, c]).then_inc(added, 1)
                dve.wait_ge(rounded, 2 * i + c + 1)
                nc.vector.tensor_sub(one(M[1], 2 * i + c), A[:, c], one(M[0], 2 * i + c).bitcast(F32)).then_inc(done, 1)
            co.run(dve, st, co.split_lo, read)


def hybrid_mixer(co, st, cols):
    nc = co.nc
    with ExitStack() as ctx:
        OH = co.sb("OH", [P, 4, S], F32R, ctx)
        OL = co.sb("OL", [P, 4, S], F32R, ctx)
        with ExitStack() as inner:
            QKV = co.sb("QKV", [P, 36, S], ctx=inner)
            MK = co.sb("MK", [P, MW], BF16, inner)
            IB = co.sb("IB", [P, P], BF16, inner)
            rotated_input(co, st["hin_qk"], st["hin_v"], QKV, IB, [(MK[:].bitcast(mybir.dt.uint16), co.dram["mask"])])
            every4 = lambda t: slice(t, None, 4)
            turn_values(co, [(QKV[:, 24:28, :], lambda t: slice(t * P, (t + 1) * P)), (QKV[:, 28:32, :], every4),
                             (QKV[:, 32:36, :], every4)])

            def score(x, ps):
                h, r = x
                c, p = h // 2, HD * (h % 2)
                q = lambda g: QKV[p:p + HD, 8 * g + c, r::4]
                k = lambda g: QKV[p:p + HD, 8 * g + 4 + c, :]
                mm = nc.tensor.matmul
                mm(ps[:, 0:S], q(0), k(0), start=True, stop=False)
                mm(ps[:, 0:S], IB[:], MK[:, 3 - r:3 - r + S], start=False, stop=True)
                mm(ps[:, S:S + P], q(1), k(1)[:, r::4], start=True, stop=False)
                mm(ps[:, S:S + P], IB[:], MK[:, WINDOW:WINDOW + P], start=False, stop=True)
                mm(ps[:, S + P:S + 2 * P], q(2), k(2)[:, r::4], start=True, stop=False)
                return mm(ps[:, S + P:S + 2 * P], IB[:], MK[:, WINDOW + P:WINDOW + 2 * P], start=False, stop=True)

            def value(x, t):
                h, r = x
                cs = slice(h * HD, (h + 1) * HD)
                return QKV[:, 24 + t, cs] if t < 4 else QKV[:, 28 + r if t == 4 else 32 + r, cs]

            def out_read(k):
                if k % 8 != 7:
                    return None
                c = k // 8
                back = lambda t: t[:, c, :].rearrange("p (q r) -> p r q", r=4)
                return back(OH), back(OL), co.PS[:, 6 + c % 2, :].rearrange("p (r q) -> p r q", r=4)
            attend(co, [(h, r) for h in range(8) for r in range(4)], score, lambda x: 6, value, 768, HD ** -0.5,
                   [0, 2], lambda x: (6 + x[0] // 2 % 2, HD * (x[0] % 2), slice(x[1] * P, (x[1] + 1) * P),
                                      x[0] // 2 - 1 if x[0] >= 4 and x[0] % 2 == 0 and x[1] == 0 else None), out_read)
        GT = co.sb("GT", [P, 16, S], ctx=ctx)
        CH = co.sb("CH", [P, 4, S], F32R, ctx)
        CL = co.sb("CL", [P, 4, S], F32R, ctx)
        with ExitStack() as inner:
            U = co.sb("conv_u", [P, 4, S + TAPS - 1], ctx=inner)
            CV = co.sb("conv_v", [P, 4, S], ctx=inner)
            zeroed = co.sem("conv_zeroed")
            nc.gpsimd.memset(U[:, :, 0:TAPS - 1], 0.0).then_inc(zeroed, 1)
            copy_stage(co, st["hin_b"], to_buffer(co, CV, ACT.Sigmoid))
            copy_stage(co, st["hin_a"], lambda i, c: ("dve", lambda ps: nc.vector.tensor_mul(U[:, c:c + 1, TAPS - 1:], ps, one(CV, c))))
            gates_and_conv(co, st["hin_gate"], GT, U, CV, cols)
            layer_norm(co, CV, 4, cols["conv2_g"], cols["conv2_lb"], silu=True, parts=(CH, CL))
        for j, u in enumerate(st["hao"].units):
            u.x = (OH, OL) if j % 2 == 0 else (CH, CL)
        M = (co.sb("hybrid_mh", [P, DC, S], F32R, ctx), co.sb("hybrid_ml", [P, DC, S], F32R, ctx))
        merge(co, st["hao"], GT, M)
        for u in st["ho"].units:
            u.x = M
        add_stage(co, st["ho"], ALPHA, None, split=False, totals=True)
    layer_norm(co, co.X, DC, cols["ln1_g"], cols["ln1_b"], totals=True, parts=(co.Hh, co.Hl))

def program(nc, dram, cols):
    with ExitStack() as ctx:
        main(Core(nc, ctx, dram), cols)


def main(co, cols):
    first = plan_ffn(co, 0)
    even = plan_even(co)
    second = plan_ffn(co, 1)
    third = plan_ffn(co, 2)
    odd = plan_odd(co)
    fourth = plan_ffn(co, 3)
    hybrid = plan_hybrid(co)
    last = plan_ffn(co, 4)
    enter(co, cols["ffn1_norm0"])
    ffn(co, *first, 0.5, 1.0, cols["mix_norm0"])
    even_mixer(co, even, cols, cols["ffn2_norm0"])
    ffn(co, *second, 0.5, 1.0, cols["ffn1_norm1"])
    ffn(co, *third, 0.5, 1.0, cols["mix_norm1"])
    odd_mixer(co, odd, cols, cols["ffn2_norm1"])
    ffn(co, *fourth, 0.5, 1.0, None)
    hybrid_mixer(co, hybrid, cols)
    ffn(co, *last, 1.0, ALPHA, None, normed=False, split=False, totals=True)
    layer_norm(co, co.X, DC, cols["ln2_g"], cols["ln2_b"], totals=True, store=co.dram["out"])


def blocked(w):
    k, n = w.shape
    return np.ascontiguousarray(w.reshape(k // P, P, n // P, P).transpose(2, 1, 0, 3).reshape(n // P, P, k))


def halves(w):
    b = blocked(w)
    return np.ascontiguousarray(b.reshape(b.shape[0], P, 2, HALF * P).transpose(0, 2, 1, 3).reshape(-1, P, HALF * P))


def pair(a, b):
    a, b = blocked(a), blocked(b)
    return np.ascontiguousarray(np.stack([a, b], 1).reshape(-1, *a.shape[1:]))


def constants():
    f = np.float32
    p, q = np.arange(P)[:, None], np.arange(P)[None, :]
    mats = np.concatenate([p == q, q >= p, p + q == P - 1, p // 64 == q // 64], 1).astype(f)
    sel8 = (np.arange(8)[:, None] == np.arange(8 * P)[None, :] // P).astype(f)
    tokens = np.concatenate([np.arange(32), 32 * np.arange(16)]).astype(f)
    small = {
        "sign": np.where(p < 64, 1, -1).astype(f), "half_pi": np.full((P, 1), np.pi / 2, f),
        "tokens": np.tile(tokens, (P, 1)), "pair": (p // 16 % 2 == np.arange(2)[None]).astype(f),
    }
    return mats, sel8, small


def lay_out(v):
    a, cols, parts = {}, {}, []

    def col(name, m):
        cols[name] = sum(x.shape[1] for x in parts)
        parts.append(np.asarray(m))

    def vec(name, x):
        col(name, np.reshape(x, (-1, P)).T)

    def rows8(name, x):
        col(name, np.concatenate([np.reshape(x, (-1, 1)), np.zeros((P - 8, 1), np.float32)]))

    ffns = [("ffn1", "", 0), ("ffn2", "", 0), ("ffn1", "", 1), ("ffn2", "", 1)]
    for n, (f, _, l) in enumerate(ffns):
        a[f"gu{n}"] = pair(v[f + "_w_gate"][l], v[f + "_w_up"][l])
        a[f"dn{n}"] = halves(v[f + "_w_down"][l])
    a["gu4"] = pair(v["w_ffn_gate_2"][0], v["w_ffn_up_2"][0])
    a["dn4"] = halves(v["w_ffn_down_2"][0])
    for l in range(2):
        for f in ("ffn1_norm", "mix_norm", "ffn2_norm"):
            vec(f"{f}{l}", v[f][l])
    w = v["even_w_in"][0]
    for n, name in enumerate(("ein_z", "ein_x", "ein_bc")):
        a[name] = blocked(w[:, S * n:S * n + S])
    dt = np.concatenate([w[:, 1536:1544], np.zeros((D, P - 8), np.float32)], 1)
    a["ein_dt"] = np.ascontiguousarray(blocked(dt).reshape(P, RAW, 2 * P).transpose(1, 0, 2))
    a["ein_u"] = blocked(w[:, 1544:])
    a["glu"] = blocked(v["s5_w_glu"][0])
    a["eout"] = blocked(v["even_w_out"][0])
    vec("conv_w", v["ssd_conv_w"][0])
    vec("conv_b", v["ssd_conv_b"][0])
    rows8("dt_bias", v["ssd_dt_bias"][0])
    rows8("a_log", v["ssd_a_log"][0])
    vec("ssd_d", np.repeat(v["ssd_d"][0], HD))
    vec("ssd_norm", v["ssd_norm"][0])
    vec("s5_d", v["s5_d"][0])
    vec("b_glu", v["s5_b_glu"][0])
    twice = lambda x: np.concatenate([x, x], 0)
    a["s5p"] = np.concatenate([twice(v["s5_a_re"][0].T), twice(v["s5_a_im"][0].T),
                               np.tile(v["s5_log_dt"][0][None], (P, 1))], 1)
    br, bi = (v[n][0].transpose(1, 0, 2).reshape(64, -1) for n in ("s5_b_re", "s5_b_im"))
    cr, ci = (v[n][0].transpose(2, 0, 1).reshape(64, -1) for n in ("s5_c_re", "s5_c_im"))
    a["s5b"] = np.concatenate([np.concatenate([br, bi], 0), np.concatenate([bi, br], 0)], 1)
    a["s5c"] = np.concatenate([np.concatenate([cr, ci], 0), np.concatenate([ci, cr], 0)], 1)
    a["oin"] = blocked(v["odd_w_in"][0])
    a["oout"] = blocked(v["odd_w_out"][0])
    b = v["attn_rel_bias"][0]
    a["hankel"] = np.concatenate([np.repeat(b[:, 256:], 383, 1), b[:, :0:-1], b[:, :1]], 1)
    a["pool_w"] = v["pool_w"][0]
    vec("q_gain", np.tile(v["attn_q_norm"][0], 2))
    vec("k_gain", np.tile(v["attn_k_norm"][0], 2))
    vec("pool_scale", v["pool_scale"][0])
    frames = 1 / np.minimum(np.arange(1, 17)[None], np.array([2, 4, 8, 16])[:, None]).astype(np.float32)
    a["counts"] = np.tile(frames.reshape(1, -1), (P, 1))
    a["head_sel"] = (np.arange(16)[:, None] == np.arange(8 * P)[None, :] // HD).astype(np.float32)
    a["chunk_mask"] = np.concatenate([np.where(np.arange(P) < 64, NEG, 0), np.ones(64)]).astype(np.float32)[None]
    w = v["w_in_2"][0]
    q = 9 * S
    a["hin_qk"] = blocked(np.concatenate([w[:, S * n:S * n + S] for n in (0, 1, 3, 4, 6, 7)], 1))
    a["hin_v"] = blocked(np.concatenate([w[:, S * n:S * n + S] for n in (2, 5, 8)], 1))
    a["hin_a"], a["hin_b"] = blocked(w[:, q:q + S]), blocked(w[:, q + S:q + 2 * S])
    a["hin_gate"] = blocked(w[:, q + 2 * S:])
    a["hao"] = pair(v["w_attn_out_2"][0], v["w_conv_out_2"][0])
    a["ho"] = blocked(v["w_o_2"][0])
    col("conv2_w", v["conv_w_2"][0].reshape(TAPS, 4, P).transpose(2, 1, 0).reshape(P, -1))
    for n, x in (("conv2_b", "conv_b_2"), ("conv2_g", "conv_ln_g_2"), ("conv2_lb", "conv_ln_b_2"), ("ln1_g", "ln1_g_2"),
                 ("ln1_b", "ln1_b_2"), ("ln2_g", "ln2_g_2"), ("ln2_b", "ln2_b_2")):
        vec(n, v[x][0])
    f = np.float32
    inv = (1.0 / (f(10000.0) ** (np.arange(0, HD, 2, dtype=f) / f(HD)))).astype(f)
    ang = np.arange(S, dtype=f)[None] * np.tile(inv, 4)[:, None]
    sign = np.where(np.arange(P) % HD < HD // 2, -1, 1)[:, None]
    a["rope"] = np.concatenate([np.cos(ang), sign * np.sin(ang)], 1).astype(f)
    at = np.arange(P)[:, None]
    ago = 4 * at + 3 - np.arange(WINDOW)[None]
    near = (ago >= 0) & (ago <= P)
    back = at - at.T
    ok = np.concatenate([near, back >= 0, (back >= 0) & (back % 4 == 0)], 1)
    a["mask"] = (np.where(ok, 0, NEG).astype(f).view(np.uint32) >> 16).astype(np.uint16)
    mats, a["sel8"], small = constants()
    a["mats"] = mats
    for n, x in small.items():
        col(n, x)
    a["cols"] = np.concatenate(parts, 1)
    a["xT"] = v["x"][0].T
    return {n: np.ascontiguousarray(x) for n, x in a.items()}, cols


def kernel(**inputs):
    import concourse.bacc as _bacc
    from concourse.bass_utils import run_bass_kernel_spmd as _run

    v = {k: np.asarray(x) for k, x in inputs.items()}
    arrays, cols = lay_out(v)
    nc = _bacc.Bacc("TRN2", target_bir_lowering=False, num_devices=1)
    dram = {n: nc.dram_tensor("in_" + n, a.shape, mybir.dt.from_np(a.dtype), kind="ExternalInput").ap()
            for n, a in arrays.items()}
    dram["out"] = nc.dram_tensor("out_xT", (D, S), F32, kind="ExternalOutput").ap()
    program(nc, dram, cols)
    r = _run(nc, [{"in_" + n: a for n, a in arrays.items()}], core_ids=[0])
    return np.ascontiguousarray(r.results[0]["out_xT"].T).reshape(1, S, D)
```
